# Optimizing a Trainium2 kernel written in Bass

```python
import jax, jax.numpy as jnp
from jax import lax
import numpy as np

D_MODEL = 1024
BATCH = 1
SEQ = 256
DEPTH = 2

CHUNK = 64
PLE_DIM = 256
EPS = 1e-6
N_EVEN = (DEPTH + 1) // 2
N_ODD = DEPTH // 2

MIX_WIDTH = D_MODEL
A_HEADS = 8
A_HEAD_DIM = MIX_WIDTH // 2 // A_HEADS
A_WIDTH = A_HEADS * A_HEAD_DIM
GMLP_BLOCK = 128
B_WIDTH = MIX_WIDTH - A_WIDTH
CONV_W = 3
AB_IN = 2 * A_WIDTH + 3 * B_WIDTH

C_HEAD_DIM = 128
C_HEADS = D_MODEL // C_HEAD_DIM
C_WIDTH = C_HEADS * C_HEAD_DIM

D_FF = ((8 * D_MODEL // 3 + 127) // 128) * 128
N_EXPERTS = 8
TOP_K = 2
E_FF = 7 * D_MODEL // 2

kernel_name = "hybrid_gmlp_shortconv_hgrn2_moe_trunk"

def rms_norm(x, g):
    xf = x.astype(jnp.float32)
    y = xf * lax.rsqrt(jnp.mean(xf * xf, axis=-1, keepdims=True) + EPS)
    return (y * g.astype(jnp.float32)).astype(x.dtype)

def layer_norm(x, g, b):
    xf = x.astype(jnp.float32)
    mu = jnp.mean(xf, axis=-1, keepdims=True)
    xc = xf - mu
    y = xc * lax.rsqrt(jnp.mean(xc * xc, axis=-1, keepdims=True) + EPS)
    return (y * g.astype(jnp.float32) + b.astype(jnp.float32)).astype(x.dtype)

def swiglu(h, w_gu, w_down):
    gate, up = jnp.split(h @ w_gu, 2, axis=-1)
    return (jax.nn.silu(gate) * up) @ w_down

def gmlp_spatial_gate(u, v, ln_g, ln_b, w_s, b_s):
    bsz, s, _ = u.shape
    nb = s // GMLP_BLOCK
    v = v.reshape(bsz, s, A_HEADS, A_HEAD_DIM)
    v = layer_norm(v, ln_g.reshape(A_HEADS, A_HEAD_DIM), ln_b.reshape(A_HEADS, A_HEAD_DIM))
    v = v.reshape(bsz, nb, GMLP_BLOCK, A_HEADS, A_HEAD_DIM)
    chunk_id = jnp.arange(GMLP_BLOCK) // CHUNK
    mask = chunk_id[None, :] <= chunk_id[:, None]
    w = jnp.where(mask[None], w_s, 0)
    f = jnp.einsum('hij,bnjhd->bnihd', w, v) + b_s.T[:, :, None]
    return u * f.reshape(bsz, s, A_WIDTH)

def causal_depthwise_conv(x, w):
    return lax.conv_general_dilated(
        x, w[:, None, :], window_strides=(1,), padding=[(CONV_W - 1, 0)],
        dimension_numbers=('NWC', 'WIO', 'NWC'), feature_group_count=x.shape[-1])

def mixer_ab(h, w_in, a_ln_g, a_ln_b, a_ws, a_bs, b_conv, w_out):
    z = h @ w_in
    u, v, xb, cg, bg = jnp.split(
        z, [A_WIDTH, 2 * A_WIDTH, 2 * A_WIDTH + B_WIDTH, 2 * A_WIDTH + 2 * B_WIDTH], axis=-1)
    ya = gmlp_spatial_gate(jax.nn.gelu(u), jax.nn.gelu(v), a_ln_g, a_ln_b, a_ws, a_bs)
    yb = bg * causal_depthwise_conv(cg * xb, b_conv)
    return jnp.concatenate([ya, yb], axis=-1) @ w_out

def hgrn2(h, w_in, lb, o_norm_g, w_out):
    bsz, s, _ = h.shape
    n = s // CHUNK
    q, f, i, g = jnp.split(h @ w_in, 4, axis=-1)
    forget = lb + (1.0 - lb) * jax.nn.sigmoid(f.astype(jnp.float32))
    log_f = jnp.log(forget)
    k = 1.0 - forget
    q = jax.nn.silu(q.astype(jnp.float32))
    i = i.astype(jnp.float32)

    def to_chunks(t):
        return t.reshape(bsz, n, CHUNK, C_HEADS, C_HEAD_DIM).transpose(1, 0, 3, 2, 4)

    causal = jnp.tril(jnp.ones((CHUNK, CHUNK), dtype=bool))

    def step(state, inp):
        qc, kc, ic, lfc = inp
        b = jnp.cumsum(lfc, axis=2)
        o_inter = jnp.einsum('bhtk,bhkv->bhtv', qc * jnp.exp(b), state)
        diff = b[:, :, :, None, :] - b[:, :, None, :, :]
        decay = jnp.exp(jnp.where(causal[:, :, None], diff, -jnp.inf))
        attn = jnp.einsum('bhtk,bhsk,bhtsk->bhts', qc, kc, decay)
        o = o_inter + jnp.einsum('bhts,bhsv->bhtv', attn, ic)
        b_last = b[:, :, -1:, :]
        k_dec = kc * jnp.exp(b_last - b)
        new_state = jnp.exp(b_last[:, :, 0, :])[..., None] * state + \
            jnp.einsum('bhsk,bhsv->bhkv', k_dec, ic)
        return new_state, o

    state0 = jnp.zeros((bsz, C_HEADS, C_HEAD_DIM, C_HEAD_DIM), jnp.float32)
    _, o = lax.scan(step, state0, (to_chunks(q), to_chunks(k), to_chunks(i), to_chunks(log_f)))
    o = o.transpose(1, 0, 3, 2, 4).reshape(bsz, s, C_HEADS, C_HEAD_DIM).astype(h.dtype)
    o = rms_norm(o, o_norm_g.reshape(C_HEADS, C_HEAD_DIM)).reshape(bsz, s, C_WIDTH)
    return (o * jax.nn.silu(g)) @ w_out

def moe_swiglu(h, w_router, b_router, w_gu, w_down):
    logits = (h @ w_router).astype(jnp.float32) + b_router.astype(jnp.float32)
    top_logit, top_idx = lax.top_k(logits, TOP_K)
    top_w = jax.nn.softmax(top_logit, axis=-1)
    gates = jnp.sum(jax.nn.one_hot(top_idx, N_EXPERTS, dtype=jnp.float32) * top_w[..., None], axis=-2)
    gates = gates.astype(h.dtype)
    out = jnp.zeros_like(h)
    for e in range(N_EXPERTS):
        out = out + gates[..., e:e + 1] * swiglu(h, w_gu[e], w_down[e])
    return out

def setup_inputs(seed: int = 0) -> dict:
    key = jax.random.key(seed)
    ks = iter(jax.random.split(key, 32))
    f32 = jnp.float32

    def nrm(shape, scale):
        return jax.random.normal(next(ks), shape, f32) * scale

    return {
        "x": nrm((BATCH, SEQ, D_MODEL), 1.0),
        "p": nrm((DEPTH, BATCH, SEQ, PLE_DIM), 1.0),
        "norm_g": 1.0 + nrm((DEPTH, 4, D_MODEL), 0.1),
        "w_in_ab": nrm((N_EVEN, D_MODEL, AB_IN), D_MODEL ** -0.5),
        "a_ln_g": 1.0 + nrm((N_EVEN, A_WIDTH), 0.1),
        "a_ln_b": nrm((N_EVEN, A_WIDTH), 0.1),
        "a_ws": nrm((N_EVEN, A_HEADS, GMLP_BLOCK, GMLP_BLOCK), GMLP_BLOCK ** -0.5),
        "a_bs": 1.0 + nrm((N_EVEN, A_HEADS, GMLP_BLOCK), 0.1),
        "b_conv": nrm((N_EVEN, CONV_W, B_WIDTH), CONV_W ** -0.5),
        "w_out_ab": nrm((N_EVEN, MIX_WIDTH, D_MODEL), MIX_WIDTH ** -0.5),
        "ffn_w_gu": nrm((N_EVEN, D_MODEL, 2 * D_FF), D_MODEL ** -0.5),
        "ffn_w_down": nrm((N_EVEN, D_FF, D_MODEL), D_FF ** -0.5),
        "w_in_c": nrm((N_ODD, D_MODEL, 4 * C_WIDTH), D_MODEL ** -0.5),
        "lb_param": nrm((DEPTH, C_WIDTH), 0.5),
        "c_onorm_g": 1.0 + nrm((N_ODD, C_WIDTH), 0.1),
        "w_out_c": nrm((N_ODD, C_WIDTH, D_MODEL), C_WIDTH ** -0.5),
        "w_router": nrm((N_ODD, D_MODEL, N_EXPERTS), D_MODEL ** -0.5),
        "b_router": nrm((N_ODD, N_EXPERTS), 0.01),
        "e_w_gu": nrm((N_ODD, N_EXPERTS, D_MODEL, 2 * E_FF), D_MODEL ** -0.5),
        "e_w_down": nrm((N_ODD, N_EXPERTS, E_FF, D_MODEL), E_FF ** -0.5),
        "ple_w_proj": nrm((DEPTH, PLE_DIM, D_MODEL), PLE_DIM ** -0.5),
        "ple_w_gate": nrm((DEPTH, D_MODEL, D_MODEL), D_MODEL ** -0.5),
    }

def reference(x, p, norm_g, w_in_ab, a_ln_g, a_ln_b, a_ws, a_bs, b_conv, w_out_ab,
              ffn_w_gu, ffn_w_down, w_in_c, lb_param, c_onorm_g, w_out_c,
              w_router, b_router, e_w_gu, e_w_down, ple_w_proj, ple_w_gate):
    sm = jax.nn.softmax(lb_param.astype(jnp.float32), axis=0)
    lower_bounds = jnp.cumsum(sm, axis=0) - sm[0:1]

    for layer in range(DEPTH):
        j = layer // 2
        hn = rms_norm(x, norm_g[layer, 0])
        if layer % 2 == 0:
            mix = mixer_ab(hn, w_in_ab[j], a_ln_g[j], a_ln_b[j], a_ws[j], a_bs[j],
                           b_conv[j], w_out_ab[j])
        else:
            mix = hgrn2(hn, w_in_c[j], lower_bounds[layer], c_onorm_g[j], w_out_c[j])
        x = x + rms_norm(mix, norm_g[layer, 1])

        hn = rms_norm(x, norm_g[layer, 2])
        if layer % 2 == 0:
            ffn = swiglu(hn, ffn_w_gu[j], ffn_w_down[j])
        else:
            ffn = moe_swiglu(hn, w_router[j], b_router[j], e_w_gu[j], e_w_down[j])
        x = x + rms_norm(ffn, norm_g[layer, 3])

        gate = jax.nn.sigmoid(x @ ple_w_gate[layer])
        x = x + gate * (p[layer] @ ple_w_proj[layer])
    return x


_drawn_inputs = setup_inputs


def setup_inputs(seed=0):
    import zlib

    import numpy as np

    out = dict(_drawn_inputs(seed))
    spreads = {}
    factors = {}
    for name, (base, spread) in spreads.items():
        noise = np.random.default_rng([zlib.crc32(name.encode()), seed]).standard_normal(out[name].shape)
        drawn = base * np.exp(spread * noise) if base else spread * noise
        out[name] = __import__('jax').numpy.asarray(drawn.astype(out[name].dtype))
    for name, factor in factors.items():
        out[name] = (out[name] * factor).astype(out[name].dtype)
    return out
```

```python
from contextlib import ExitStack

import concourse.bass as bass
from concourse import mybir

ALU = mybir.AluOpType
ACT = mybir.ActivationFunctionType
AXX = mybir.AxisListType.X
F32 = mybir.dt.float32
F32R = mybir.dt.float32r
BF16 = mybir.dt.bfloat16
I32 = mybir.dt.int32
U8 = mybir.dt.uint8

P = 128
RING = 6
RAW = 3
GW = 2048
N = 512
EPS = 1e-6

V_N00, V_N02, V_N10, V_N12, V_LB0, V_LB1, V_ABS, V_CONV, V_ROWS = 0, 8, 16, 24, 32, 40, 48, 56, 68


def trunk(nc, x_d, p_d, norm_g, w_in_ab, a_ln_g, a_ln_b, a_ws, a_bs, b_conv, w_out_ab, ffn_w_gu,
          ffn_w_down, w_in_c, lb_param, c_onorm_g, w_out_c, w_router, b_router, e_w_gu, e_w_down,
          ple_w_proj, ple_w_gate, out_d):
    _, SEQ, D = x_d.shape
    T = SEQ // P
    KT = D // P
    HK = KT // 2
    FF = ffn_w_down.shape[1]
    FB = FF // 256
    E = e_w_down.shape[1]
    EF = e_w_down.shape[2]
    EU = EF // N
    ITEM = 6 * EU
    XTRA = T * P * 2 // (P + 1)
    ITEMS = E + XTRA
    HEADS, HD = 8, 128
    AH, AD = a_ws.shape[1], a_ln_g.shape[1] // a_ws.shape[1]
    AW = AH * AD

    G_AB = 0
    G_OUT = G_AB + 2 * 5
    G_FFN = G_OUT + 4
    G_PLE0 = G_FFN + 3 * FB
    G_INC = G_PLE0 + 5
    G_OUTC = G_INC + 16
    G_MOE = G_OUTC + 4
    assert G_MOE % RING == 0 and ITEM % RING == 0 and G_MOE % RAW == 0

    with ExitStack() as ctx:
        def sb(name, shape, dt=F32):
            return ctx.enter_context(nc.sbuf_tensor(name, shape, dt))

        def sem(name):
            return ctx.enter_context(nc.semaphore(name))

        raw = sb("raw", [P, RAW, GW])
        w_hi = sb("w_hi", [P, RING, GW], F32R)
        w_lo = sb("w_lo", [P, RING, GW], F32R)
        x = sb("x", [P, T, D])
        xn = sb("xn", [P, T, D])
        xT_hi = sb("xT_hi", [P, KT, SEQ], F32R)
        xT_lo = sb("xT_lo", [P, KT, SEQ], F32R)
        gain = sb("gain", [P, D])
        hT_hi = sb("hT_hi", [P, N], F32R)
        hT_lo = sb("hT_lo", [P, N], F32R)
        SC = sb("SC", [P, 9 * 1024 + 8])
        ident = sb("ident", [P, P])
        ones = sb("ones", [P, P])
        before = sb("before", [P, P])
        iota_c = sb("iota_c", [P, P])
        seg = sb("seg", [P, 7, P], U8)
        zeros = sb("zeros", [P, N], BF16)
        junk = sb("junk", [P, T * D], BF16)
        vrow = sb("vrow", [V_ROWS, P])
        vcol = sb("vcol", [P, V_ROWS])
        wr = sb("wr", [P, KT, E])
        wr_hi = sb("wr_hi", [P, KT, E], F32R)
        wr_lo = sb("wr_lo", [P, KT, E], F32R)
        br = sb("br", [P, E])
        ss = sb("ss", [P, 16])
        nr = sb("nr", [P, 3, 16])
        lbc = sb("lbc", [P, 4, HEADS])
        rt = sb("rt", [P, 400])
        tab = sb("tab", [P, 2, T, ITEMS + 1])
        cur = sb("cur", [P, 2, T])
        itab = sb("itab", [1, 8], I32)
        PS = ctx.enter_context(nc.psum_tensor("PS", [P, 8, N], F32))

        def area(k, n=1):
            return SC[:, 1024 * k:1024 * (k + n)]

        av = area(0).rearrange("p (t n) -> p t n", t=T)
        xb = area(1).rearrange("p (t n) -> p t n", t=T)
        bg = area(2).rearrange("p (t n) -> p t n", t=T)
        ws = area(3).rearrange("p (h j) -> p h j", h=AH)
        wsT = area(4).rearrange("p (h i) -> p h i", h=AH)
        lng = SC[:, 5 * 1024:5 * 1024 + AW]
        lnb = SC[:, 5 * 1024 + AW:6 * 1024]
        vc = area(6).rearrange("p (t n) -> p t n", t=T)
        sq = area(7).rearrange("p (t n) -> p t n", t=T)
        cT = SC[:, 8 * 1024:8 * 1024 + HK * (SEQ + 2)].rearrange("p (k s) -> p k s", k=HK)
        conv = area(6).rearrange("p (k s) -> p k s", k=HK)
        ybT = area(7).rearrange("p (k s) -> p k s", k=HK)
        uu = xn[:, 0, :].rearrange("p (t n) -> p t n", t=T)
        ya = xn[:, 1, :].rearrange("p (t n) -> p t n", t=T)
        sg = SC[:, 3 * 1024:3 * 1024 + N]
        hh = SC[:, 3 * 1024 + N:4 * 1024]
        pn = SC[:, 4 * 1024 + 512:5 * 1024].rearrange("p (t n) -> p t n", t=T)
        pgate = area(6, 2)
        qT = area(0, 2).rearrange("p (h s) -> p h s", h=HEADS)
        kT = area(2, 2).rearrange("p (h s) -> p h s", h=HEADS)
        attn = area(4, 2).rearrange("p (h t n) -> p h t n", h=HEADS, t=T)
        attx = area(6).rearrange("p (h n) -> p h n", h=HEADS)
        iv = area(7, 2).rearrange("p (t n) -> p t n", t=T)
        f_nat = area(4, 2).rearrange("p (t n) -> p t n", t=T)
        q_nat = area(7, 2).rearrange("p (t n) -> p t n", t=T)
        fT = xn[:, :, :].rearrange("p t n -> p (t n)").rearrange("p (h s) -> p h s", h=HEADS)
        tot = area(6)
        oo = area(0, 2).rearrange("p (t n) -> p t n", t=T)
        osq = area(2, 2)
        gg = xn
        acc = area(0, 2).rearrange("p (t n) -> p t n", t=T)
        ye = area(2)
        sel = SC[:, 4 * 1024:4 * 1024 + T * P].rearrange("p (t c) -> p t c", t=T)
        selT = SC[:, 4 * 1024 + 256:4 * 1024 + 512].rearrange("p (t c) -> p t c", t=T)

        raw_full = [sem(f"raw_full{i}") for i in range(RAW)]
        hi_done, lo_done, used = sem("hi_done"), sem("lo_done"), sem("used")
        gain_full, gain_free = sem("gain_full"), sem("gain_free")
        x_full, small_full, ws_full, ln_full, p_full = (
            sem("x_full"), sem("small_full"), sem("ws_full"), sem("ln_full"), sem("p_full"))
        consts, seg_in = sem("consts"), sem("seg_in")
        s_vT, s_vcol, s_wsT, s_wsE, s_wr = sem("vrow_turned"), sem("vcol_ready"), sem("ws_turned"), sem("wsT_ready"), sem("wr_split")
        xT_psum, xT_act, xT_ready = sem("xT_psum"), sem("xT_act"), sem("xT_ready")
        xn_ready = sem("xn_ready")
        ss_ready, rstd_ready = sem("ss_ready"), sem("rstd_ready")
        x_ready = sem("x_ready")
        v_gelu, vn_ready, xb_ready, c_ready, bg_ready, u_ready = (
            sem("v_gelu"), sem("vn_ready"), sem("xb_ready"), sem("c_ready"), sem("bg_ready"), sem("u_ready"))
        cT_psum, cT_ready, bgT_psum, yb_ready, gm_done, ya_ready = (
            sem("cT_psum"), sem("cT_ready"), sem("bgT_psum"), sem("yb_ready"), sem("gm_done"), sem("ya_ready"))
        yT_psum, ybT_hi = sem("yT_psum"), sem("ybT_hi")
        silu_done, h_ready, cur_step = sem("silu_done"), sem("h_ready"), sem("cur_step")
        hT_psum, hT_act, hT_ready = sem("hT_psum"), sem("hT_act"), sem("hT_ready")
        pT_psum, pT_act, pT_ready = sem("pT_psum"), sem("pT_act"), sem("pT_ready")
        gate_act = sem("gate_act")
        f_evac, q_evac, i_evac, g_evac = (
            sem("f_evac"), sem("q_evac"), sem("i_evac"), sem("g_evac"))
        fT_psum, fT_act, k_ready, qT_psum, qT_act = (
            sem("fT_psum"), sem("fT_act"), sem("k_ready"), sem("qT_psum"), sem("qT_act"))
        qk_ready, at_done = sem("qk_ready"), sem("at_done")
        o_done, o_sq, o_ready = sem("o_done"), sem("o_sq"), sem("o_ready")
        exp_ask, exp_done = sem("exp_ask"), sem("exp_done")
        lg_done, lg_max, lg_exp, sel_cnt, cnt_done, table_ready = (
            sem("lg_done"), sem("lg_max"), sem("lg_exp"), sem("sel_cnt"), sem("cnt_done"), sem("table_ready"))
        sel_ready, tsel_psum, selT_ready = sem("sel_ready"), sem("tsel_psum"), sem("selT_ready")
        gat_done, xg_act, xg_ready = sem("gathered"), sem("xg_act"), sem("xg_ready")
        ye_ready, sc_done, acc_done = sem("ye_ready"), sem("scattered"), sem("acc_done")
        act_step, dve_step, pool_step = sem("act_step"), sem("dve_step"), sem("pool_step")
        stored = sem("stored")

        block = ctx.enter_context(nc.Block())

        @block.sync
        def _(sp):
            def load(g, src, turns=0):
                if g >= RAW:
                    sp.wait_ge(lo_done, turns * RING + (g - RAW + 1))
                sp.dma_start(raw[:, g % RAW, :], src).then_inc(raw_full[g % RAW], 16)

            for t in range(T):
                sp.dma_start(x[:, t, :], x_d[0, t * P:(t + 1) * P, :]).then_inc(x_full, 16)
            g = G_AB
            for c in (1, 2, 3, 4, 0):
                for h in range(2):
                    load(g, w_in_ab[2 * c + h])
                    g += 1
            for h in (1, 0):
                for c in range(2):
                    load(g, w_out_ab[2 * c + h])
                    g += 1

            def load_gu(g, b, turns=0):
                for h in range(2):
                    load(g + h, ffn_w_gu[bass.ds(2 * b + h, 1), :, :].rearrange("g p n -> p (g n)"), turns)

            def load_down(g, b, turns=0):
                load(g, ffn_w_down[0][bass.ds(b * 256, 256), :].rearrange("(p r) n -> p (r n)", p=P), turns)

            load_gu(g, 0)
            with sp.Fori(0, (FB - 1) // 2) as it:
                for j in range(2):
                    load_gu(G_FFN + 2 + 3 * j, 2 * it + j + 1, it)
                    load_down(G_FFN + 4 + 3 * j, 2 * it + j, it)
            load_down(G_PLE0 - 1, FB - 1)

            def load_ple(layer, g, turns=0):
                load(g, ple_w_proj[layer].rearrange("(p r) n -> p (r n)", p=P), turns)
                for j in range(4):
                    load(g + 1 + j, ple_w_gate[4 * layer + j], turns)

            load_ple(0, G_PLE0)
            g = G_INC
            for c in (2, 3, 0, 1, 4, 5, 6, 7):
                for h in range(2):
                    load(g, w_in_c[2 * c + h])
                    g += 1
            for c in range(2):
                for h in range(2):
                    load(g, w_out_c[2 * c + h])
                    g += 1

            def load_item(i, e):
                dn = e_w_down[0].rearrange("e f n -> e (f n)")

                def unit_gu(g, u, turns):
                    for q in range(4):
                        src = e_w_gu[bass.ds(e, 1), bass.ds(u * 4 + q, 1), :, :]
                        load(g + q, src.rearrange("e g p n -> p (e g n)"), turns)

                def unit_down(g, u, turns):
                    for j in range(2):
                        src = dn[bass.ds(e, 1), bass.ds(u * (N * D) + j * 256 * D, 256 * D)]
                        load(g + j, src.rearrange("e (p m) -> p (e m)", p=P), turns)

                unit_gu(G_MOE, 0, i * EU)
                with sp.Fori(0, EU - 1) as u:
                    unit_gu(G_MOE + 4, u + 1, i * EU + u)
                    unit_down(G_MOE + 8, u, i * EU + u)
                unit_down(G_MOE + ITEM - 2, EU - 1, i * EU)

            with sp.Fori(0, E) as i:
                load_item(i, i)
            sp.wait_ge(table_ready, 1)
            n_items = sp.value_load(itab[0:1, 0:1], min_val=E, max_val=ITEMS)
            with sp.If(n_items > E):
                with sp.Fori(E, n_items) as i:
                    e = sp.value_load(itab[0:1, bass.ds(i - E + 1, 1)], min_val=0, max_val=E - 1)
                    load_item(i, e)
            load_ple(1, G_MOE, n_items * EU)
            sp.wait_ge(x_ready, 6 * T)
            for t in range(T):
                sp.dma_start(out_d[0, t * P:(t + 1) * P, :], x[:, t, :]).then_inc(stored, 16)
            sp.wait_ge(stored, 16 * T)

        @block.gpsimd
        def _(pool):
            count = [0]

            def step(ins):
                count[0] += 1
                ins.then_inc(pool_step, 1)
                pool.wait_ge(pool_step, count[0])

            rows = [(V_N00, norm_g[0, 0]), (V_N02, norm_g[0, 2]), (V_N10, norm_g[1, 0]), (V_N12, norm_g[1, 2]),
                    (V_LB0, lb_param[0]), (V_LB1, lb_param[1])]
            for r, v in rows:
                pool.dma_start(vrow[r:r + 8, :], v.rearrange("(k p) -> k p", p=P)).then_inc(small_full, 16)
            pool.dma_start(vrow[V_ABS:V_ABS + 8, :], a_bs[0]).then_inc(small_full, 16)
            pool.dma_start(vrow[V_CONV:V_ROWS, :], b_conv[0].rearrange("w (k p) -> (w k) p", p=P)).then_inc(small_full, 16)
            pool.dma_start(wr[:, :, :], w_router[0].rearrange("(k p) e -> p k e", p=P)).then_inc(small_full, 16)
            pool.dma_start(br[:, :], b_router[0:1, :].broadcast_to([P, E])).then_inc(small_full, 16)
            pool.dma_start(ws, a_ws[0].rearrange("h i j -> i h j")).then_inc(ws_full, 16)
            pool.dma_start(lng, a_ln_g[0:1, :].broadcast_to([P, AW])).then_inc(ln_full, 16)
            pool.dma_start(lnb, a_ln_b[0:1, :].broadcast_to([P, AW])).then_inc(ln_full, 16)
            step(pool.memset(ident[:, :], 0.0))
            step(pool.affine_select(out=ident[:, :], in_=ident[:, :], compare_op=ALU.not_equal, fill=1.0, base=0,
                                    pattern=[[-1, P]], channel_multiplier=1))
            step(pool.memset(ones[:, :], 1.0))
            step(pool.affine_select(out=before[:, :], in_=ones[:, :], compare_op=ALU.is_gt, fill=0.0, base=0,
                                    pattern=[[1, P]], channel_multiplier=-1))
            pool.memset(zeros[:, :], 0.0).then_inc(consts, 1)
            pool.iota(iota_c[:, :].bitcast(I32), pattern=[[1, P]], base=0, channel_multiplier=0).then_inc(seg_in, 1)
            pool.iota(rt[:, 0:P].bitcast(I32), pattern=[[0, P]], base=0, channel_multiplier=1).then_inc(seg_in, 1)
            gains = [norm_g[0, 1:2], norm_g[0, 3:4], c_onorm_g[0:1], norm_g[1, 1:2], norm_g[1, 3:4]]
            for n, v in enumerate(gains):
                if n:
                    pool.wait_ge(gain_free, n)
                pool.dma_start(gain[:, :], v.broadcast_to([P, D])).then_inc(gain_full, 16)
                if n == 1:
                    pool.dma_start(pn, p_d[0, 0].rearrange("(t p) n -> p t n", p=P)).then_inc(p_full, 16)
                if n == 4:
                    pool.dma_start(pn[:, :, :], p_d[1, 0].rearrange("(t p) n -> p t n", p=P)).then_inc(p_full, 16)

        @block.tensor
        def _(pe):
            def split_matmul(out, a_hi, a_lo, b_hi, b_lo, start, stop):
                pe.matmul(out, a_hi, b_hi, start=start, stop=False, skip_group_check=True)
                pe.matmul(out, a_lo, b_hi, start=False, stop=False, skip_group_check=True)
                return pe.matmul(out, a_hi, b_lo, start=False, stop=stop, skip_group_check=True)

            def half_granule(g, pair, h, first, last, turns=0):
                pe.wait_ge(lo_done, turns * RING + (g + 1))
                for t in range(T):
                    for j in range(HK):
                        r = slice(j * N, (j + 1) * N)
                        tok = slice(t * P, (t + 1) * P)
                        m = split_matmul(PS[:, 2 * pair + t, :], xT_hi[:, HK * h + j, tok], xT_lo[:, HK * h + j, tok],
                                         w_hi[:, g % RING, r], w_lo[:, g % RING, r],
                                         first and j == 0, last and j == HK - 1)
                m.then_inc(used, 1)

            def turn_x(src):
                for b in range(4):
                    for j in range(2):
                        kt = 2 * b + j
                        for t in range(T):
                            c = (j * T + t) * P
                            m = pe.transpose(PS[:, 4 + b, c:c + P], src[:, t, kt * P:(kt + 1) * P], ident[:, :])
                    m.then_inc(xT_psum, 1)

            pe.wait_ge(consts, 1)
            pe.wait_ge(small_full, 160)
            pe.transpose(PS[:, 0, 0:V_ROWS], vrow[:, :], ident[0:V_ROWS, 0:V_ROWS]).then_inc(s_vT, 1)
            pe.wait_ge(ws_full, 16)
            for h in range(AH):
                m = pe.transpose(PS[:, 1 + h // 4, (h % 4) * P:(h % 4 + 1) * P], ws[:, h, :], ident[:, :])
            m.then_inc(s_wsT, 1)
            pe.wait_ge(xn_ready, 1)
            turn_x(xn)
            pe.wait_ge(xT_ready, 1)
            pe.wait_ge(s_wsE, 1)
            for n in range(4):
                for h in range(2):
                    half_granule(G_AB + 2 * n + h, n, h, h == 0, h == 1)
            pe.wait_ge(c_ready, 1)
            for k in range(HK):
                for t in range(T):
                    c = (k % 2) * SEQ + t * P
                    m = pe.transpose(PS[:, 2 + k // 2, c:c + P], xb[:, t, k * P:(k + 1) * P], ident[:, :])
            m.then_inc(cT_psum, 1)
            pe.wait_ge(v_gelu, 1)
            for h in range(2):
                half_granule(G_AB + 8 + h, 0, h, h == 0, h == 1)
            pe.wait_ge(bg_ready, 1)
            for k in range(HK):
                for t in range(T):
                    c = (k % 2) * SEQ + t * P
                    m = pe.transpose(PS[:, 4 + k // 2, c:c + P], bg[:, t, k * P:(k + 1) * P], ident[:, :])
            m.then_inc(bgT_psum, 1)
            pe.wait_ge(vn_ready, 1)
            for h in range(AH):
                o = PS[:, 6 + h // 4, (h % 4) * P:(h % 4 + 1) * P].rearrange("p (t d) -> p t d", t=T)
                m = pe.matmul(o, wsT[:, h, :], vc[:, :, h * AD:(h + 1) * AD], start=True, stop=True,
                              skip_group_check=True)
            m.then_inc(gm_done, 1)
            pe.wait_ge(ya_ready, 1)
            pe.wait_ge(cT_ready, 1)
            for k in range(HK):
                for t in range(T):
                    c = (k % 2) * SEQ + t * P
                    m = pe.transpose(PS[:, 2 + k // 2, c:c + P], ya[:, t, k * P:(k + 1) * P], ident[:, :])
            m.then_inc(yT_psum, 1)
            pe.wait_ge(yb_ready, 1)
            for c in range(2):
                half_granule(G_OUT + c, 2 + c, 1, True, False)
            pe.wait_ge(xT_ready, 2)
            for c in range(2):
                half_granule(G_OUT + 2 + c, 2 + c, 0, False, True)

            def clear(banks):
                for b in banks:
                    pe.matmul(PS[:, b, :], zeros[:, 0:P], zeros[:, :], start=True, stop=False, skip_group_check=True)

            def ffn_gu(g, turns=0):
                half_granule(g, 0, 0, True, False, turns)
                half_granule(g + 1, 0, 1, False, True, turns)

            def ffn_turn(n):
                pe.wait_ge(h_ready, n)
                hv = hh.rearrange("p (t q r) -> p t r q", t=T, r=2)
                for r in range(2):
                    for t in range(T):
                        c = (r * T + t) * P
                        m = pe.transpose(PS[:, 2, c:c + P], hv[:, t, r, :], ident[:, :])
                m.then_inc(hT_psum, 1)

            def ffn_down(g, n, last, turns=0):
                pe.wait_ge(hT_ready, n)
                pe.wait_ge(lo_done, turns * RING + (g + 1))
                for c in range(2):
                    for t in range(T):
                        for r in range(2):
                            a = slice((r * T + t) * P, (r * T + t + 1) * P)
                            w = slice(r * D + c * N, r * D + (c + 1) * N)
                            m = split_matmul(PS[:, 4 + 2 * c + t, :], hT_hi[:, a], hT_lo[:, a],
                                             w_hi[:, g % RING, w], w_lo[:, g % RING, w], False, last and r == 1)
                m.then_inc(used, 1)

            pe.wait_ge(xn_ready, 2)
            turn_x(xn)
            pe.wait_ge(xT_ready, 3)
            ffn_gu(G_FFN)
            clear(range(4, 8))
            ffn_turn(1)
            with pe.Fori(0, (FB - 1) // 2) as it:
                for j in range(2):
                    ffn_gu(G_FFN + 2 + 3 * j, it)
                    ffn_down(G_FFN + 4 + 3 * j, 2 * it + (j + 1), False, it)
                    ffn_turn(2 * it + (j + 2))
            ffn_down(G_PLE0 - 1, FB, True)

            def ple(layer, g, turned, turns=0):
                pe.wait_ge(p_full, 16 * (layer + 1))
                if layer == 1:
                    pe.wait_ge(acc_done, n_items * T + T)
                for kk in range(2):
                    for t in range(T):
                        c = (kk * T + t) * P
                        m = pe.transpose(PS[:, 3, c:c + P], pn[:, t, kk::2], ident[:, :])
                m.then_inc(pT_psum, 1)
                pe.wait_ge(pT_ready, layer + 1)
                pe.wait_ge(lo_done, turns * RING + (g + 1))
                for c in range(2):
                    for t in range(T):
                        for kk in range(2):
                            a = slice((kk * T + t) * P, (kk * T + t + 1) * P)
                            w = slice(kk * D + c * N, kk * D + (c + 1) * N)
                            m = split_matmul(PS[:, 2 * c + t, :], hT_hi[:, a], hT_lo[:, a],
                                             w_hi[:, g % RING, w], w_lo[:, g % RING, w], kk == 0, kk == 1)
                m.then_inc(used, 1)
                pe.wait_ge(x_ready, turned)
                turn_x(x)
                pe.wait_ge(xT_ready, 4 if layer == 0 else 8)
                for j in range(4):
                    half_granule(g + 1 + j, 2 + j // 2, j % 2, j % 2 == 0, j % 2 == 1, turns)

            ple(0, G_PLE0, 2 * T)

            pe.wait_ge(xn_ready, 3)
            turn_x(xn)
            pe.wait_ge(xT_ready, 5)

            def proj(n, evac=None):
                c, h = n // 2, n % 2
                if evac:
                    pe.wait_ge(*evac)
                half_granule(G_INC + n, c % 2, h, h == 0, h == 1)

            def turn_heads(src, signal):
                for hd in range(HEADS):
                    for t in range(T):
                        c = (hd % 2) * SEQ + t * P
                        m = pe.transpose(PS[:, 4 + hd // 2, c:c + P], src[:, t, hd * P:(hd + 1) * P], ident[:, :])
                    if hd % 2:
                        m.then_inc(signal, 1)

            def level(n):
                pe.wait_ge(qk_ready, n + 1)
                for hd in range(HEADS):
                    for t in range(T):
                        tok = slice(t * P, (t + 1) * P)
                        c = (hd % 2) * SEQ + t * P
                        m = pe.matmul(PS[:, 4 + hd // 2, c:c + P], kT[:, hd, tok], qT[:, hd, tok],
                                      start=True, stop=True, skip_group_check=True)
                m.then_inc(at_done, 1)

            for n in range(4):
                proj(n)
            proj(4, (f_evac, 1))
            proj(5)
            pe.wait_ge(f_evac, 2)
            turn_heads(f_nat, fT_psum)
            proj(6)
            proj(7)
            pe.wait_ge(q_evac, 2)
            pe.wait_ge(fT_act, 4)
            turn_heads(q_nat, qT_psum)
            proj(8)
            level(0)
            proj(9)
            level(1)
            proj(10)
            level(2)
            proj(11)
            level(3)
            proj(12, (i_evac, 1))
            level(4)
            proj(13)
            level(5)
            proj(14, (i_evac, 2))
            level(6)
            proj(15)
            level(7)
            pe.wait_ge(qk_ready, 9)
            for hd in range(HEADS):
                m = pe.matmul(PS[:, 4 + hd // 4, (hd % 4) * P:(hd % 4 + 1) * P], kT[:, hd, 0:P], qT[:, hd, P:SEQ],
                              start=True, stop=True, skip_group_check=True)
            m.then_inc(at_done, 1)
            pe.wait_ge(g_evac, 2)
            pe.wait_ge(qk_ready, 10)
            for t in range(T):
                for hd in range(HEADS):
                    o = PS[:, 2 * t + hd // 4, (hd % 4) * P:(hd % 4 + 1) * P]
                    m = pe.matmul(o, attn[:, hd, t, :], iv[:, t, hd * HD:(hd + 1) * HD], start=True, stop=(t == 0),
                                  skip_group_check=True)
                    if t == 1:
                        m = pe.matmul(o, attx[:, hd, :], iv[:, 0, hd * HD:(hd + 1) * HD], start=False, stop=True,
                                      skip_group_check=True)
            m.then_inc(o_done, 1)
            pe.wait_ge(o_ready, 1)
            turn_x(oo)
            pe.wait_ge(xT_ready, 6)
            for c in range(2):
                for h in range(2):
                    half_granule(G_OUTC + 2 * c + h, 2 + c, h, h == 0, h == 1)

            pe.wait_ge(xn_ready, 4)
            turn_x(xn)
            pe.wait_ge(xT_ready, 7)
            pe.wait_ge(s_wr, 2)
            for t in range(T):
                for k in range(KT):
                    tok = slice(t * P, (t + 1) * P)
                    m = split_matmul(PS[:, 0, t * E:(t + 1) * E], xT_hi[:, k, tok], xT_lo[:, k, tok],
                                     wr_hi[:, k, :], wr_lo[:, k, :], k == 0, k == KT - 1)
            m.then_inc(lg_done, 1)
            pe.wait_ge(sel_cnt, 1)
            chosen = rt[:, 0:2 * E].rearrange("p (t e) -> p t e", t=T)
            pe.matmul(PS[:, 1, 0:E], before[:, :], chosen[:, 0, :], start=True, stop=True, skip_group_check=True)
            pe.matmul(PS[:, 1, E:2 * E], before[:, :], chosen[:, 1, :], start=True, stop=False, skip_group_check=True)
            pe.matmul(PS[:, 1, E:2 * E], ones[:, :], chosen[:, 0, :], start=False, stop=True, skip_group_check=True)
            pe.matmul(PS[:, 1, 2 * E:3 * E], ones[:, :], chosen[:, 0, :], start=True, stop=False, skip_group_check=True)
            pe.matmul(PS[:, 1, 2 * E:3 * E], ones[:, :], chosen[:, 1, :], start=False, stop=True,
                      skip_group_check=True).then_inc(cnt_done, 1)

            def gather(n):
                pe.wait_ge(sel_ready, n)
                for k in range(KT):
                    for t in range(T):
                        m = pe.matmul(PS[:, 6 + k // 4, (k % 4) * P:(k % 4 + 1) * P], xn[:, t, k * P:(k + 1) * P],
                                      sel[:, t, :], start=(t == 0), stop=(t == T - 1), skip_group_check=True)
                m.then_inc(gat_done, 1)

            def unit_gu(g, turns):
                for side in range(2):
                    for h in range(2):
                        pe.wait_ge(lo_done, turns * RING + (g + 2 * side + h + 1))
                        for j in range(HK):
                            r = slice(j * N, (j + 1) * N)
                            s = (g + 2 * side + h) % RING
                            m = split_matmul(PS[:, side, :], xT_hi[:, HK * h + j, 0:P], xT_lo[:, HK * h + j, 0:P],
                                             w_hi[:, s, r], w_lo[:, s, r], h == 0 and j == 0, h == 1 and j == HK - 1)
                        m.then_inc(used, 1)

            def unit_turn(n):
                pe.wait_ge(h_ready, n)
                hv = hh.rearrange("p (j q r) -> p j r q", j=2, r=2)
                for j in range(2):
                    for r in range(2):
                        c = (j * 2 + r) * P
                        m = pe.transpose(PS[:, 2, c:c + P], hv[:, j, r, :], ident[:, :])
                m.then_inc(hT_psum, 1)

            def unit_down(g, n, last, turns):
                pe.wait_ge(hT_ready, n)
                for j in range(2):
                    pe.wait_ge(lo_done, turns * RING + (g + j + 1))
                    for r in range(2):
                        for c in range(2):
                            a = slice((j * 2 + r) * P, (j * 2 + r + 1) * P)
                            w = slice(r * D + c * N, r * D + (c + 1) * N)
                            s = (g + j) % RING
                            m = split_matmul(PS[:, 4 + c, :], hT_hi[:, a], hT_lo[:, a],
                                             w_hi[:, s, w], w_lo[:, s, w], False, last and j == 1 and r == 1)
                    m.then_inc(used, 1)

            gather(1)
            pe.wait_ge(table_ready, 1)
            n_items = pe.value_load(itab[0:1, 0:1], min_val=E, max_val=ITEMS)
            pe.wait_ge(xg_ready, 1)
            with pe.Fori(0, n_items) as i:
                unit_gu(G_MOE, i * EU)
                pe.wait_ge(acc_done, i * T + T)
                unit_turn(i * EU + (FB + 1))
                for t in range(T):
                    m = pe.transpose(PS[:, 3, t * P:(t + 1) * P], sel[:, t, :], ident[:, :])
                m.then_inc(tsel_psum, 1)
                clear((4, 5))
                with pe.Fori(0, EU - 1) as u:
                    unit_gu(G_MOE + 4, i * EU + u)
                    unit_down(G_MOE + 8, i * EU + u + (FB + 1), False, i * EU + u)
                    unit_turn(i * EU + u + (FB + 2))
                gather(i + 2)
                unit_down(G_MOE + ITEM - 2, i * EU + (FB + EU), True, i * EU)
                pe.wait_ge(ye_ready, i + 1)
                pe.wait_ge(selT_ready, i + 1)
                pe.wait_ge(xg_ready, i + 2)
                for t, b in ((0, 6), (1, 2)):
                    for c in range(2):
                        m = pe.matmul(PS[:, b + c, :], selT[:, t, :], ye[:, c * N:(c + 1) * N], start=True, stop=True,
                                      skip_group_check=True)
                    m.then_inc(sc_done, 1)
            ple(1, G_MOE, 5 * T, n_items * EU)

        @block.scalar
        def _(act):
            def hi(g, turns=0):
                if g >= RING:
                    act.wait_ge(used, turns * RING + (g - RING + 1))
                act.wait_ge(raw_full[g % RAW], turns * (16 * RING // RAW) + 16 * (g // RAW + 1))
                act.activation(w_hi[:, g % RING, :], raw[:, g % RAW, :], ACT.Copy).then_inc(hi_done, 1)

            def product(g, turns=0):
                act.wait_ge(used, turns * RING + g)

            def his(a, b):
                for g in range(a, b):
                    hi(g)

            def xT(n, v, base):
                for b in range(4):
                    act.wait_ge(xT_psum, 4 * base + b + 1)
                    for j in range(2):
                        kt = 2 * b + j
                        src = PS[:, 4 + b, j * SEQ:(j + 1) * SEQ]
                        m = act.activation(xT_hi[:, kt, :], src, ACT.Copy,
                                           scale=1.0 if v is None else vcol[:, v + kt:v + kt + 1])
                    m.then_inc(xT_act, 1)

            def square_y(src):
                for c in range(2):
                    for t in range(T):
                        m = act.activation(junk[:, (2 * c + t) * N:(2 * c + t + 1) * N], src(c, t), ACT.Square,
                                           accum_out=ss[:, 2 * c + t:2 * c + t + 1])
                m.then_inc(ss_ready, 1)

            def square_x():
                for t in range(T):
                    m = act.activation(junk[:, t * D:(t + 1) * D], x[:, t, :], ACT.Square, accum_out=ss[:, 4 + t:5 + t])
                m.then_inc(ss_ready, 1)

            def scale_x(n):
                act.wait_ge(rstd_ready, n)
                for t in range(T):
                    m = act.activation(xn[:, t, :], x[:, t, :], ACT.Copy, scale=nr[:, 1, t:t + 1])
                m.then_inc(xn_ready, 1)

            in_psum = lambda c, t: PS[:, 4 + 2 * c + t, :]

            act.wait_ge(x_full, 16 * T)
            square_x()
            act.wait_ge(small_full, 160)
            act.activation(wr_hi[:, :, :], wr[:, :, :], ACT.Copy).then_inc(s_wr, 1)
            scale_x(1)
            his(0, 3)
            act.wait_ge(s_vcol, 1)
            xT(0, V_N00, 0)
            act.wait_ge(exp_ask, 1)
            act.activation(lbc[:, 0:2, :], lbc[:, 2:4, :], ACT.Exp).then_inc(exp_done, 1)
            his(3, 7)
            product(G_AB + 2)
            act.activation(av, PS[:, 0:2, :], ACT.Gelu_apprx_tanh).then_inc(v_gelu, 1)
            his(7, 9)
            product(G_AB + 4)
            act.activation(xb, PS[:, 2:4, :], ACT.Copy).then_inc(xb_ready, 1)
            his(9, 12)
            product(G_AB + 8)
            act.activation(bg, PS[:, 6:8, :], ACT.Copy).then_inc(bg_ready, 1)
            act.wait_ge(cT_psum, 1)
            act.activation(cT[:, :, 2:SEQ + 2], PS[:, 2:4, :].rearrange("p b (k s) -> p (b k) s", k=2),
                           ACT.Copy).then_inc(cT_ready, 1)
            his(12, 14)
            product(G_AB + 10)
            act.activation(uu, PS[:, 0:2, :], ACT.Gelu_apprx_tanh).then_inc(u_ready, 1)
            act.wait_ge(ybT_hi, 1)
            act.activation(xT_hi[:, HK:KT, :], ybT, ACT.Copy).then_inc(xT_act, 1)
            act.wait_ge(yT_psum, 1)
            act.activation(xT_hi[:, 0:HK, :], PS[:, 2:4, :].rearrange("p b (k s) -> p (b k) s", k=2),
                           ACT.Copy).then_inc(xT_act, 1)
            his(14, 18)
            product(G_FFN)
            square_y(in_psum)
            act.wait_ge(x_ready, T)
            square_x()
            scale_x(3)
            xT(1, V_N02, 1)
            his(18, 20)

            def silu():
                act.activation(sg.rearrange("p (t n) -> p t n", t=T), PS[:, 0:2, 0:256], ACT.Silu).then_inc(silu_done, 1)

            def hT(n):
                act.wait_ge(hT_psum, n)
                act.activation(hT_hi[:, :], PS[:, 2, :], ACT.Copy).then_inc(hT_act, 1)

            hi(20)
            product(G_FFN + 2)
            silu()
            hT(1)
            with act.Fori(0, (FB - 1) // 2) as it:
                for j in range(2):
                    hi(21 + 3 * j, it)
                    hi(22 + 3 * j, it)
                    product(G_FFN + 4 + 3 * j, it)
                    silu()
                    hi(23 + 3 * j, it)
                    hT(2 * it + (j + 2))
            product(G_PLE0)
            square_y(in_psum)

            def pT(n):
                act.wait_ge(pT_psum, n)
                act.activation(hT_hi[:, :], PS[:, 3, :], ACT.Copy).then_inc(pT_act, 1)

            def gate(g, turns=0):
                for c in range(2):
                    product(g + 3 + 2 * c, turns)
                    act.activation(pgate[:, c * 1024:(c + 1) * 1024], PS[:, 4 + 2 * c:6 + 2 * c, :].rearrange("p b n -> p (b n)"),
                                   ACT.Sigmoid).then_inc(gate_act, 1)

            pT(1)
            his(51, 52)
            act.wait_ge(x_ready, 2 * T)
            xT(2, None, 2)
            his(52, 54)
            hi(54)
            gate(G_PLE0)
            act.wait_ge(x_ready, 3 * T)
            square_x()
            scale_x(5)
            xT(3, V_N10, 3)
            his(55, 59)
            product(G_INC + 2)
            act.activation(f_nat[:, :, 0:N], PS[:, 0:2, :], ACT.Copy).then_inc(f_evac, 1)
            his(59, 61)
            product(G_INC + 4)
            act.activation(f_nat[:, :, N:D], PS[:, 2:4, :], ACT.Copy).then_inc(f_evac, 1)
            his(61, 62)
            product(G_INC + 6)
            act.activation(q_nat[:, :, 0:N], PS[:, 0:2, :], ACT.Copy).then_inc(q_evac, 1)
            for b in range(4):
                act.wait_ge(fT_psum, b + 1)
                act.activation(fT[:, 2 * b:2 * b + 2, :], PS[:, 4 + b, :].rearrange("p (h s) -> p h s", h=2),
                               ACT.Sigmoid).then_inc(fT_act, 1)
            his(62, 64)
            product(G_INC + 8)
            act.activation(q_nat[:, :, N:D], PS[:, 2:4, :], ACT.Copy).then_inc(q_evac, 1)
            for b in range(4):
                act.wait_ge(qT_psum, b + 1)
                act.activation(qT[:, 2 * b:2 * b + 2, :], PS[:, 4 + b, :].rearrange("p (h s) -> p h s", h=2),
                               ACT.Silu).then_inc(qT_act, 1)
            his(64, 66)
            product(G_INC + 10)
            act.activation(iv[:, :, 0:N], PS[:, 0:2, :], ACT.Copy).then_inc(i_evac, 1)
            his(66, 68)
            product(G_INC + 12)
            act.activation(iv[:, :, N:D], PS[:, 2:4, :], ACT.Copy).then_inc(i_evac, 1)
            his(68, 70)
            product(G_INC + 14)
            act.wait_ge(qk_ready, 4)
            act.activation(gg[:, :, 0:N], PS[:, 0:2, :], ACT.Silu).then_inc(g_evac, 1)
            his(70, 72)
            product(G_INC + 16)
            act.activation(gg[:, :, N:D], PS[:, 2:4, :], ACT.Silu).then_inc(g_evac, 1)
            his(72, 74)
            act.wait_ge(o_done, 1)
            act.activation(osq, PS[:, 0:4, :].rearrange("p b n -> p (b n)"), ACT.Square).then_inc(o_sq, 1)
            xT(4, None, 4)
            his(74, 76)
            product(G_MOE)
            square_y(in_psum)
            act.wait_ge(x_ready, 4 * T)
            square_x()
            scale_x(7)
            xT(5, V_N12, 5)
            act.wait_ge(lg_max, 1)
            act.activation(rt[:, 2 * E:4 * E], rt[:, 4 * E:6 * E], ACT.Exp).then_inc(lg_exp, 1)

            def xg(n):
                act.wait_ge(gat_done, n)
                for k in range(KT):
                    m = act.activation(xT_hi[:, k, 0:P], PS[:, 6 + k // 4, (k % 4) * P:(k % 4 + 1) * P], ACT.Copy,
                                       scale=vcol[:, V_N12 + k:V_N12 + k + 1])
                m.then_inc(xg_act, 1)

            def unit_silu():
                act.activation(sg, PS[:, 0, :], ACT.Silu).then_inc(silu_done, 1)

            act.wait_ge(table_ready, 1)
            n_items = act.value_load(itab[0:1, 0:1], min_val=E, max_val=ITEMS)
            xg(1)
            with act.Fori(0, n_items) as i:
                for q in range(4, 8):
                    hi(G_MOE + q, i * EU)
                product(G_MOE + 4, i * EU)
                unit_silu()
                hT(i * EU + (FB + 1))
                act.wait_ge(tsel_psum, i + 1)
                act.activation(selT, PS[:, 3, 0:T * P].rearrange("p (t c) -> p t c", t=T), ACT.Copy).then_inc(selT_ready, 1)
                with act.Fori(0, EU - 1) as u:
                    for q in range(8, 13):
                        hi(G_MOE + q, i * EU + u)
                    product(G_MOE + 8, i * EU + u)
                    unit_silu()
                    hi(G_MOE + 13, i * EU + u)
                    hT(i * EU + u + (FB + 2))
                xg(i + 2)
                for q in range(ITEM + 2, ITEM + 4):
                    hi(G_MOE + q, i * EU)
                product(G_MOE + ITEM, i * EU)
                act.activation(ye, PS[:, 4:6, :].rearrange("p b n -> p (b n)"), ACT.Copy).then_inc(ye_ready, 1)
            hi(G_MOE + 4, n_items * EU)
            act.wait_ge(acc_done, n_items * T + T)
            square_y(lambda c, t: acc[:, t, c * N:(c + 1) * N])
            pT(2)
            act.wait_ge(x_ready, 5 * T)
            xT(7, None, 6)
            gate(G_MOE, n_items * EU)

        @block.vector
        def _(dve):
            count = [0]

            def step(ins):
                count[0] += 1
                ins.then_inc(dve_step, 1)
                dve.wait_ge(dve_step, count[0])

            def lo(g, turns=0):
                dve.wait_ge(hi_done, turns * RING + (g + 1))
                dve.tensor_tensor(w_lo[:, g % RING, :], raw[:, g % RAW, :], w_hi[:, g % RING, :].bitcast(F32),
                                  ALU.subtract).then_inc(lo_done, 1)

            def los(a, b):
                for g in range(a, b):
                    lo(g)

            def rsqrt(n):
                v, y, a = (nr[:, k, 0:n] for k in range(3))
                step(dve.tensor_single_scalar(a.bitcast(I32), v.bitcast(I32), 1, op=ALU.logical_shift_right))
                step(dve.tensor_scalar(y.bitcast(I32), a.bitcast(I32), -1.0, float(0x5F3759DF), ALU.mult, ALU.add))
                for _ in range(3):
                    step(dve.tensor_tensor(a, y, y, ALU.mult))
                    step(dve.scalar_tensor_tensor(out=a, in0=a, scalar=-0.5, in1=v, op0=ALU.mult, op1=ALU.mult))
                    step(dve.scalar_tensor_tensor(out=y, in0=a, scalar=1.5, in1=y, op0=ALU.add, op1=ALU.mult))

            def norm_x(n):
                dve.wait_ge(ss_ready, n)
                step(dve.tensor_scalar(nr[:, 0, 0:T], ss[:, 4:4 + T], 1.0 / D, EPS, ALU.mult, ALU.add))
                rsqrt(T)
                dve.sem_inc(rstd_ready, 1)

            def norm_y(n, gains, src, xr):
                dve.wait_ge(ss_ready, n)
                step(dve.tensor_tensor(nr[:, 2, 0:T], ss[:, 0:T], ss[:, T:2 * T], ALU.add))
                step(dve.tensor_scalar(nr[:, 0, 0:T], nr[:, 2, 0:T], 1.0 / D, EPS, ALU.mult, ALU.add))
                rsqrt(T)
                dve.sem_inc(rstd_ready, 1)
                dve.wait_ge(gain_full, 16 * gains)
                for t in range(T):
                    for c in range(2):
                        cols = slice(c * N, (c + 1) * N)
                        y = src(c, t)
                        tmp = SC[:, 5 * 1024 + c * N:5 * 1024 + (c + 1) * N]
                        m = dve.scalar_tensor_tensor(out=tmp, in0=y, scalar=nr[:, 1, t:t + 1], in1=gain[:, cols],
                                                     op0=ALU.mult, op1=ALU.mult)
                        step(m)
                        if t == T - 1 and c == 1 and gains < 5:
                            dve.sem_inc(gain_free, 1)
                        m = dve.tensor_tensor(x[:, t, cols], x[:, t, cols], tmp, ALU.add)
                        if c == 0:
                            step(m)
                    m.then_inc(x_ready, 1)
                    dve.wait_ge(x_ready, xr - T + t + 1)

            def xT(n, v, base):
                for b in range(4):
                    dve.wait_ge(xT_act, base + b + 1)
                    for j in range(2):
                        kt = 2 * b + j
                        src = PS[:, 4 + b, j * SEQ:(j + 1) * SEQ]
                        up = xT_hi[:, kt, :].bitcast(F32)
                        if v is None:
                            m = dve.tensor_tensor(xT_lo[:, kt, :], src, up, ALU.subtract)
                        else:
                            m = dve.scalar_tensor_tensor(out=xT_lo[:, kt, :], in0=src, scalar=vcol[:, v + kt:v + kt + 1],
                                                         in1=up, op0=ALU.mult, op1=ALU.subtract)
                m.then_inc(xT_ready, 1)

            in_psum = lambda c, t: PS[:, 4 + 2 * c + t, :]

            dve.memset(cT[:, :, 0:2], 0.0)
            norm_x(1)
            dve.wait_ge(s_vT, 1)
            step(dve.tensor_copy(vcol[:, :], PS[:, 0, 0:V_ROWS]))
            dve.sem_inc(s_vcol, 1)
            l0, l1 = vcol[:, V_LB0:V_LB0 + 8], vcol[:, V_LB1:V_LB1 + 8]
            step(dve.tensor_tensor(lbc[:, 0, :], l0, l1, ALU.max))
            step(dve.tensor_tensor(lbc[:, 2, :], l0, lbc[:, 0, :], ALU.subtract))
            step(dve.tensor_tensor(lbc[:, 3, :], l1, lbc[:, 0, :], ALU.subtract))
            dve.sem_inc(exp_ask, 1)
            dve.wait_ge(s_wr, 1)
            dve.tensor_tensor(wr_lo[:, :, :], wr[:, :, :], wr_hi[:, :, :].bitcast(F32), ALU.subtract).then_inc(s_wr, 1)
            dve.wait_ge(s_wsT, 1)
            step(dve.tensor_copy(wsT, PS[:, 1:3, :].rearrange("p b (h i) -> p (b h) i", h=4)))
            dve.memset(wsT[64:P, :, 0:64], 0.0).then_inc(s_wsE, 1)
            los(0, 3)
            xT(1, V_N00, 0)
            dve.wait_ge(seg_in, 2)
            ii, ir, cmp = iota_c[:, :].bitcast(I32), rt[:, 0:P].bitcast(I32), rt[:, P:2 * P]
            xr_ = rt[:, 2 * P:3 * P].bitcast(I32)
            step(dve.tensor_tensor(xr_, ii, ir, ALU.bitwise_xor))
            step(dve.tensor_tensor(cmp, ii, ir, ALU.is_gt))
            step(dve.tensor_copy(rt[:, 0:P], xr_))
            step(dve.tensor_tensor(cmp, cmp, rt[:, 0:P], ALU.mult))
            for lv in range(7):
                dve.tensor_scalar(seg[:, lv, :], cmp, float(2 ** lv), None, ALU.is_ge)
            step(dve.tensor_copy(rt[:, 0:P], ii))
            step(dve.tensor_copy(iota_c[:, :], rt[:, 0:P]))
            dve.wait_ge(exp_done, 1)
            step(dve.tensor_tensor(lbc[:, 2, :], lbc[:, 0, :], lbc[:, 1, :], ALU.add))
            step(dve.reciprocal(lbc[:, 3, :], lbc[:, 2, :]))
            step(dve.tensor_tensor(lbc[:, 0, :], lbc[:, 0, :], lbc[:, 3, :], ALU.mult))
            step(dve.tensor_tensor(lbc[:, 1, :], lbc[:, 1, :], lbc[:, 3, :], ALU.mult))
            step(dve.tensor_tensor(lbc[:, 2, :], lbc[:, 0, :], lbc[:, 1, :], ALU.add))
            step(dve.tensor_tensor(lbc[:, 0, :], lbc[:, 2, :], lbc[:, 0, :], ALU.subtract))
            step(dve.tensor_scalar(lbc[:, 1, :], lbc[:, 0, :], -1.0, 1.0, ALU.mult, ALU.add))
            los(3, 8)
            heads = "p t (h d) -> p (t h) d"
            AG = T * AH
            m1, m2 = rt[:, 0:AG], rt[:, AG:2 * AG]
            dve.wait_ge(v_gelu, 1)
            vh, ch, qh = av.rearrange(heads, h=AH), vc.rearrange(heads, h=AH), sq.rearrange(heads, h=AH)
            step(dve.tensor_reduce(m1, vh, AXX, ALU.add))
            step(dve.tensor_scalar(m1, m1, 1.0 / AD, None, ALU.mult))
            step(dve.tensor_tensor(ch, vh, m1.unsqueeze(2).broadcast_to([P, AG, AD]), ALU.subtract))
            lo(8)
            dve.wait_ge(xb_ready, 1)
            dve.wait_ge(used, G_AB + 6)
            dve.tensor_tensor(xb, PS[:, 4:6, :], xb, ALU.mult).then_inc(c_ready, 1)
            step(dve.tensor_tensor(qh, ch, ch, ALU.mult))
            step(dve.tensor_reduce(m2, qh, AXX, ALU.add))
            step(dve.tensor_scalar(nr[:, 0, 0:AG], m2, 1.0 / AD, EPS, ALU.mult, ALU.add))
            rsqrt(AG)
            lo(9)
            step(dve.tensor_tensor(ch, ch, nr[:, 1, 0:AG].unsqueeze(2).broadcast_to([P, AG, AD]), ALU.mult))
            dve.wait_ge(ln_full, 32)
            step(dve.tensor_tensor(vc, vc, lng.unsqueeze(1).broadcast_to([P, T, AW]), ALU.mult))
            dve.tensor_tensor(vc, vc, lnb.unsqueeze(1).broadcast_to([P, T, AW]), ALU.add).then_inc(vn_ready, 1)
            los(10, 12)
            dve.wait_ge(cT_ready, 1)
            dve.wait_ge(gm_done, 1)
            for tap in range(3):
                for k in range(HK):
                    w = vcol[:, V_CONV + tap * HK + k:V_CONV + tap * HK + k + 1]
                    src = cT[:, k, tap:tap + SEQ]
                    if tap == 0:
                        m = dve.tensor_scalar(conv[:, k, :], src, w, None, ALU.mult)
                    else:
                        m = dve.scalar_tensor_tensor(out=conv[:, k, :], in0=src, scalar=w, in1=conv[:, k, :],
                                                     op0=ALU.mult, op1=ALU.add)
                step(m)
            dve.wait_ge(bgT_psum, 1)
            step(dve.tensor_tensor(ybT, conv, PS[:, 4:6, :].rearrange("p b (k s) -> p (b k) s", k=2), ALU.mult))
            dve.sem_inc(ybT_hi, 1)
            dve.wait_ge(u_ready, 1)
            for h in range(AH):
                src = PS[:, 6 + h // 4, (h % 4) * P:(h % 4 + 1) * P].rearrange("p (t d) -> p t d", t=T)
                cols = slice(h * AD, (h + 1) * AD)
                m = dve.scalar_tensor_tensor(out=ya[:, :, cols], in0=src, scalar=vcol[:, V_ABS + h:V_ABS + h + 1],
                                             in1=uu[:, :, cols], op0=ALU.add, op1=ALU.mult)
            m.then_inc(ya_ready, 1)
            dve.wait_ge(xT_act, 5)
            dve.tensor_tensor(xT_lo[:, HK:KT, :], ybT, xT_hi[:, HK:KT, :].bitcast(F32), ALU.subtract).then_inc(yb_ready, 1)
            dve.wait_ge(xT_act, 6)
            dve.tensor_tensor(xT_lo[:, 0:HK, :], PS[:, 2:4, :].rearrange("p b (k s) -> p (b k) s", k=2),
                              xT_hi[:, 0:HK, :].bitcast(F32), ALU.subtract).then_inc(xT_ready, 1)
            los(12, 18)
            norm_y(2, 1, in_psum, T)
            norm_x(3)
            xT(3, V_N02, 6)
            los(18, 21)

            def hidden(n):
                dve.wait_ge(silu_done, n)
                dve.tensor_tensor(hh.rearrange("p (t n) -> p t n", t=T), sg.rearrange("p (t n) -> p t n", t=T),
                                  PS[:, 0:2, 256:512], ALU.mult).then_inc(h_ready, 1)

            def hT(n):
                dve.wait_ge(hT_act, n)
                dve.tensor_tensor(hT_lo[:, :], PS[:, 2, :], hT_hi[:, :].bitcast(F32), ALU.subtract).then_inc(hT_ready, 1)

            hidden(1)
            hT(1)
            with dve.Fori(0, (FB - 1) // 2) as it:
                for j in range(2):
                    lo(21 + 3 * j, it)
                    lo(22 + 3 * j, it)
                    hidden(2 * it + (j + 2))
                    lo(23 + 3 * j, it)
                    hT(2 * it + (j + 2))

            def pT(n):
                dve.wait_ge(pT_act, n)
                dve.tensor_tensor(hT_lo[:, :], PS[:, 3, :], hT_hi[:, :].bitcast(F32), ALU.subtract).then_inc(pT_ready, 1)

            def embed(n, xr):
                for c in range(2):
                    dve.wait_ge(gate_act, 2 * n + c + 1)
                    g = pgate[:, c * 1024:(c + 1) * 1024]
                    step(dve.tensor_tensor(g, g, PS[:, 2 * c:2 * c + 2, :].rearrange("p b n -> p (b n)"), ALU.mult))
                    for t in range(T):
                        cols = slice(c * N, (c + 1) * N)
                        m = dve.tensor_tensor(x[:, t, cols], x[:, t, cols], g[:, t * N:(t + 1) * N], ALU.add)
                    m.then_inc(x_ready, 1)
                dve.wait_ge(x_ready, xr)

            norm_y(4, 2, in_psum, 2 * T)
            pT(1)
            los(51, 52)
            xT(4, None, 10)
            los(52, 55)
            embed(0, 3 * T)
            norm_x(5)
            xT(5, V_N10, 14)
            los(55, 62)
            for hd in range(HEADS):
                dve.wait_ge(fT_act, hd // 2 + 1)
                m = dve.tensor_scalar(fT[:, hd, :], fT[:, hd, :], lbc[:, 1, hd:hd + 1], lbc[:, 0, hd:hd + 1],
                                      ALU.mult, ALU.add)
            step(m)
            step(dve.tensor_scalar(kT, fT, -1.0, 1.0, ALU.mult, ALU.add))
            los(62, 64)
            dve.wait_ge(qT_act, 4)
            dve.sem_inc(qk_ready, 1)

            def meet(lv):
                at = attn.rearrange("p h t n -> p (h t) n")
                src = PS[:, 4:8, :].rearrange("p b (g n) -> p (b g) n", g=4)
                dve.wait_ge(at_done, lv + 1)
                if lv == 0:
                    step(dve.tensor_tensor(at, src, ident[:, :].unsqueeze(1).broadcast_to([P, 2 * HEADS, P]), ALU.mult))
                else:
                    step(dve.copy_predicated(at, seg[:, lv - 1, :].unsqueeze(1).broadcast_to([P, 2 * HEADS, P]), src))

            flat = "p h s -> p (h s)"
            qf, kf, ff = qT.rearrange(flat), kT.rearrange(flat), fT.rearrange(flat)
            totals = (junk[:, :].bitcast(F32), tot)
            prev = ff
            meet(0)
            step(dve.tensor_tensor(qT, qT, fT, ALU.mult))
            dve.sem_inc(qk_ready, 1)
            lo(64)
            for lv in range(1, 8):
                width, blocks = 2 ** (lv - 1), HEADS * SEQ // 2 ** (lv - 1)
                meet(lv)
                pv = prev.rearrange("p (m e) -> p m e", e=2)
                q4 = qf.rearrange("p (m e w) -> p m e w", e=2, w=width)
                k4 = kf.rearrange("p (m e w) -> p m e w", e=2, w=width)
                shape = [P, blocks // 2, width]
                dve.tensor_tensor(q4[:, :, 1, :], q4[:, :, 1, :], pv[:, :, 0].unsqueeze(2).broadcast_to(shape), ALU.mult)
                step(dve.tensor_tensor(k4[:, :, 0, :], k4[:, :, 0, :], pv[:, :, 1].unsqueeze(2).broadcast_to(shape),
                                       ALU.mult))
                dve.sem_inc(qk_ready, 1)
                lo(64 + lv)
                if lv < 7:
                    prev = totals[lv % 2][:, 0:blocks // 2]
                    step(dve.tensor_tensor(prev, pv[:, :, 0], pv[:, :, 1], ALU.mult))
            dve.wait_ge(at_done, 9)
            step(dve.tensor_copy(attx, PS[:, 4:6, :].rearrange("p b (h n) -> p (b h) n", h=4)))
            dve.sem_inc(qk_ready, 1)
            dve.wait_ge(g_evac, 2)
            dve.wait_ge(gain_full, 48)
            step(dve.tensor_tensor(gg[:, :, :], gg[:, :, :], gain[:, :].unsqueeze(1).broadcast_to([P, T, D]), ALU.mult))
            dve.sem_inc(gain_free, 1)
            los(72, 74)
            dve.wait_ge(o_sq, 1)
            OG = T * HEADS
            step(dve.tensor_reduce(rt[:, 0:OG], osq.rearrange("p (g n) -> p g n", n=HD), AXX, ALU.add))
            step(dve.tensor_scalar(nr[:, 0, 0:OG], rt[:, 0:OG], 1.0 / HD, EPS, ALU.mult, ALU.add))
            rsqrt(OG)
            step(dve.tensor_tensor(oo.rearrange("p t (h n) -> p (t h) n", n=HD),
                                   PS[:, 0:4, :].rearrange("p b (h n) -> p (b h) n", n=HD),
                                   nr[:, 1, 0:OG].unsqueeze(2).broadcast_to([P, OG, HD]), ALU.mult))
            dve.tensor_tensor(oo, oo, gg[:, :, :], ALU.mult).then_inc(o_ready, 1)
            xT(6, None, 18)
            los(74, 76)
            norm_y(6, 4, in_psum, 4 * T)
            norm_x(7)
            xT(7, V_N12, 22)
            chosen, ex, lm, lg = (rt[:, k * T * E:(k + 1) * T * E] for k in range(4))
            mx, rank = rt[:, 64:64 + T], rt[:, 80:80 + T * E]
            later = rt[:, 256:256 + E * E].rearrange("p (a b) -> p a b", a=E)
            pair = rt[:, 128:128 + E * E].rearrange("p (a b) -> p a b", a=E)
            same = rt[:, 192:192 + E * E].rearrange("p (a b) -> p a b", a=E)

            def by_row(v):
                return v.unsqueeze(2).broadcast_to([P, E, E])

            def by_col(v):
                return v.unsqueeze(1).broadcast_to([P, E, E])

            step(dve.tensor_tensor(later, by_col(iota_c[:, 0:E]), by_row(iota_c[:, 0:E]), ALU.is_lt))
            dve.wait_ge(lg_done, 1)
            tE = "p (t e) -> p t e"
            step(dve.tensor_tensor(lg.rearrange(tE, t=T), PS[:, 0, 0:T * E].rearrange(tE, t=T),
                                   br[:, :].unsqueeze(1).broadcast_to([P, T, E]), ALU.add))
            for t in range(T):
                l = lg[:, t * E:(t + 1) * E]
                step(dve.tensor_reduce(mx[:, t:t + 1], l, AXX, ALU.max))
                step(dve.tensor_scalar(lm[:, t * E:(t + 1) * E], l, mx[:, t:t + 1], None, ALU.subtract))
            dve.sem_inc(lg_max, 1)
            for t in range(T):
                l = lg[:, t * E:(t + 1) * E]
                step(dve.tensor_tensor(pair, by_col(l), by_row(l), ALU.is_gt))
                step(dve.tensor_tensor(same, by_col(l), by_row(l), ALU.is_equal))
                step(dve.tensor_tensor(same, same, later, ALU.mult))
                step(dve.tensor_tensor(pair, pair, same, ALU.add))
                step(dve.tensor_reduce(rank[:, t * E:(t + 1) * E], pair, AXX, ALU.add))
            step(dve.tensor_scalar(chosen, rank, 2.0, None, ALU.is_lt))
            dve.sem_inc(sel_cnt, 1)
            gates = rt[:, 320:320 + T * E]
            dve.wait_ge(lg_exp, 1)
            step(dve.tensor_tensor(ex, ex, chosen, ALU.mult))
            step(dve.tensor_reduce(mx, ex.rearrange(tE, t=T), AXX, ALU.add))
            step(dve.reciprocal(mx, mx))
            step(dve.tensor_tensor(gates.rearrange(tE, t=T), ex.rearrange(tE, t=T), mx.unsqueeze(2).broadcast_to([P, T, E]),
                                   ALU.mult))
            slot = rt[:, 96:96 + T * E]
            step(dve.memset(tab[:, :, :, :], -1.0))
            dve.wait_ge(cnt_done, 1)
            step(dve.scalar_tensor_tensor(out=slot, in0=PS[:, 1, 0:T * E], scalar=1.0, in1=chosen, op0=ALU.add, op1=ALU.mult))
            step(dve.tensor_scalar(slot, slot, -1.0, None, ALU.add))
            step(dve.tensor_copy(tab[:, 0, :, 0:E], slot.rearrange(tE, t=T)))
            dve.tensor_copy(tab[:, 1, :, 0:E], gates.rearrange(tE, t=T))

            def select(col):
                dve.tensor_copy(cur[:, 0, :].unsqueeze(2), tab[:, 0, :, bass.ds(col, 1)]).then_inc(cur_step, 1)

            def compare():
                for t in range(T):
                    m = dve.tensor_scalar(sel[:, t, :], iota_c[:, :], cur[:, 0, t:t + 1], None, ALU.is_equal)
                m.then_inc(sel_ready, 1)

            select(0)
            dve.wait_ge(cur_step, 1)
            compare()
            over, place, one, tmp = (rt[:, 336 + k * E:336 + (k + 1) * E] for k in range(4))
            head = rt[:, 368:368 + 1 + XTRA]
            step(dve.tensor_scalar(over, PS[:, 1, T * E:(T + 1) * E], float(P), None, ALU.is_gt))
            step(dve.tensor_tensor(pair, later, by_col(over), ALU.mult))
            step(dve.tensor_reduce(place, pair, AXX, ALU.add))
            step(dve.tensor_reduce(head[:, 0:1], over, AXX, ALU.add))
            step(dve.tensor_scalar(head[:, 0:1], head[:, 0:1], float(E), None, ALU.add))
            for j in range(XTRA):
                step(dve.scalar_tensor_tensor(out=one, in0=place, scalar=float(j), in1=over, op0=ALU.is_equal, op1=ALU.mult))
                step(dve.tensor_tensor(tmp, one, iota_c[:, 0:E], ALU.mult))
                step(dve.tensor_reduce(head[:, 1 + j:2 + j], tmp, AXX, ALU.add))
                for k, v in ((0, slot), (1, gates)):
                    p3 = pair[:, 0:T, :]
                    step(dve.tensor_tensor(p3, v.rearrange(tE, t=T), one.unsqueeze(1).broadcast_to([P, T, E]), ALU.mult))
                    m = dve.tensor_reduce(tab[:, k, :, E + j:E + j + 1], p3, AXX, ALU.add)
                    step(m)
            step(dve.tensor_scalar(tab[:, 0, :, E:E + XTRA], tab[:, 0, :, E:E + XTRA], -float(P), None, ALU.add))
            dve.tensor_copy(itab[0:1, 0:1 + XTRA], head[0:1, :]).then_inc(table_ready, 1)
            dve.wait_ge(table_ready, 1)
            n_items = dve.value_load(itab[0:1, 0:1], min_val=E, max_val=ITEMS)
            for t in range(T):
                dve.memset(acc[:, t, :], 0.0).then_inc(acc_done, 1)

            def xg(n):
                dve.wait_ge(xg_act, n)
                for k in range(KT):
                    m = dve.scalar_tensor_tensor(out=xT_lo[:, k, 0:P], in0=PS[:, 6 + k // 4, (k % 4) * P:(k % 4 + 1) * P],
                                                 scalar=vcol[:, V_N12 + k:V_N12 + k + 1],
                                                 in1=xT_hi[:, k, 0:P].bitcast(F32), op0=ALU.mult, op1=ALU.subtract)
                m.then_inc(xg_ready, 1)

            def unit_hidden(n):
                dve.wait_ge(silu_done, n)
                dve.tensor_tensor(hh, sg, PS[:, 1, :], ALU.mult).then_inc(h_ready, 1)

            xg(1)
            with dve.Fori(0, n_items) as i:
                for q in range(4, 8):
                    lo(G_MOE + q, i * EU)
                unit_hidden(i * EU + (FB + 1))
                hT(i * EU + (FB + 1))
                dve.wait_ge(tsel_psum, i + 1)
                select(i + 1)
                dve.wait_ge(cur_step, i * 2 + 2)
                compare()
                with dve.Fori(0, EU - 1) as u:
                    for q in range(8, 13):
                        lo(G_MOE + q, i * EU + u)
                    unit_hidden(i * EU + u + (FB + 2))
                    lo(G_MOE + 13, i * EU + u)
                    hT(i * EU + u + (FB + 2))
                xg(i + 2)
                for q in range(ITEM + 2, ITEM + 4):
                    lo(G_MOE + q, i * EU)
                dve.tensor_copy(cur[:, 1, :].unsqueeze(2), tab[:, 1, :, bass.ds(i, 1)]).then_inc(cur_step, 1)
                dve.wait_ge(cur_step, i * 2 + 3)
                dve.wait_ge(acc_done, i * T + T)
                for t, b in ((0, 6), (1, 2)):
                    dve.wait_ge(sc_done, i * T + (t + 1))
                    dve.scalar_tensor_tensor(out=acc[:, t, :], in0=PS[:, b:b + 2, :].rearrange("p b n -> p (b n)"),
                                             scalar=cur[:, 1, t:t + 1], in1=acc[:, t, :], op0=ALU.mult,
                                             op1=ALU.add).then_inc(acc_done, 1)
            lo(G_MOE + 4, n_items * EU)
            dve.wait_ge(acc_done, n_items * T + T)
            norm_y(8, 5, lambda c, t: acc[:, t, c * N:(c + 1) * N], 5 * T)
            pT(2)
            xT(8, None, 26)
            embed(1, 6 * T)


_INS = ["x", "p", "norm_g", "w_in_ab", "a_ln_g", "a_ln_b", "a_ws", "a_bs", "b_conv", "w_out_ab", "ffn_w_gu",
        "ffn_w_down", "w_in_c", "lb_param", "c_onorm_g", "w_out_c", "w_router", "b_router", "e_w_gu", "e_w_down",
        "ple_w_proj", "ple_w_gate"]


def granules(w, sides=1, columns=512):
    n, rows, m = w.shape
    w = w.reshape(n, 2, 4, P, sides, m // sides // columns, columns)
    w = w.transpose(0, 5, 1, 3, 2, 4, 6)
    return w.reshape(n, 2 * m // sides // columns, P, 4 * sides * columns)


def expert_granules(w):
    n, rows, m = w.shape
    w = w.reshape(n, 2, 4, P, 2, m // 1024, 512)
    w = w.transpose(0, 5, 4, 1, 3, 2, 6)
    return w.reshape(n, 4 * (m // 1024), P, GW)


def kernel(**inputs):
    import numpy as _np
    import concourse.bacc as _bacc
    from concourse import mybir as _mybir
    from concourse.bass_utils import run_bass_kernel_spmd as _run

    data = {name: _np.asarray(inputs[name]) for name in _INS}
    for name in ("w_in_ab", "w_out_ab", "w_in_c", "w_out_c", "ple_w_gate"):
        data[name] = granules(data[name]).reshape(-1, P, GW)
    data["ffn_w_gu"] = granules(data["ffn_w_gu"], 2, 256).reshape(-1, P, GW)
    data["e_w_gu"] = expert_granules(data["e_w_gu"][0])

    nc = _bacc.Bacc("TRN2", target_bir_lowering=False, num_devices=1)
    arrays, args = {}, []
    for name in _INS:
        a = _np.ascontiguousarray(data[name])
        arrays[f"in_{name}"] = a
        args.append(nc.dram_tensor(f"in_{name}", a.shape, _mybir.dt.from_np(a.dtype), kind="ExternalInput").ap())
    out = nc.dram_tensor("out_0", inputs["x"].shape, _mybir.dt.float32, kind="ExternalOutput").ap()
    trunk(nc, *args, out)
    r = _run(nc, [arrays], core_ids=[0])
    return r.results[0]["out_0"]
```

```python
from contextlib import ExitStack

import concourse.bass as bass
from concourse import mybir

ALU = mybir.AluOpType
ACT = mybir.ActivationFunctionType
AXX = mybir.AxisListType.X
F32 = mybir.dt.float32
F32R = mybir.dt.float32r
BF16 = mybir.dt.bfloat16
I32 = mybir.dt.int32
U8 = mybir.dt.uint8

P = 128
RING = 6
RAW = 3
GW = 2048
HW = GW // 2
N = 512
EPS = 1e-6

V_N00, V_N02, V_N10, V_N12, V_LB0, V_LB1, V_ABS, V_CONV, V_ROWS = 0, 8, 16, 24, 32, 40, 48, 56, 68


def trunk(nc, x_d, p_d, norm_g, w_in_ab, a_ln_g, a_ln_b, a_ws, a_bs, b_conv, w_out_ab, ffn_w_gu,
          ffn_w_down, w_in_c, lb_param, c_onorm_g, w_out_c, w_router, b_router, e_w_gu, e_w_down,
          ple_w_proj, ple_w_gate, out_d):
    _, SEQ, D = x_d.shape
    T = SEQ // P
    KT = D // P
    HK = KT // 2
    FF = ffn_w_down.shape[1]
    FB = FF // 256
    E = e_w_down.shape[1]
    EF = e_w_down.shape[2]
    EU = EF // N
    ITEM = 6 * EU
    XTRA = T * P * 2 // (P + 1)
    ITEMS = E + XTRA
    HEADS, HD = 8, 128
    AH, AD = a_ws.shape[1], a_ln_g.shape[1] // a_ws.shape[1]
    AW = AH * AD

    G_AB = 0
    G_OUT = G_AB + 2 * 5
    G_FFN = G_OUT + 4
    G_PLE0 = G_FFN + 3 * FB
    G_INC = G_PLE0 + 5
    G_OUTC = G_INC + 16
    G_MOE = G_OUTC + 4
    assert G_MOE % RING == 0 and ITEM % RING == 0 and G_MOE % RAW == 0

    with ExitStack() as ctx:
        def sb(name, shape, dt=F32):
            return ctx.enter_context(nc.sbuf_tensor(name, shape, dt))

        def sem(name):
            return ctx.enter_context(nc.semaphore(name))

        raw = sb("raw", [P, RAW, GW])
        w_hi = sb("w_hi", [P, RING, GW], F32R)
        w_lo = sb("w_lo", [P, RING, GW], F32R)
        x = sb("x", [P, T, D])
        xn = sb("xn", [P, T, D])
        xT_hi = sb("xT_hi", [P, KT, SEQ], F32R)
        xT_lo = sb("xT_lo", [P, KT, SEQ], F32R)
        gain = sb("gain", [P, D])
        hT_hi = sb("hT_hi", [P, N], F32R)
        hT_lo = sb("hT_lo", [P, N], F32R)
        SC = sb("SC", [P, 9 * 1024 + 8])
        ident = sb("ident", [P, P])
        ones = sb("ones", [P, P])
        before = sb("before", [P, P])
        iota_c = sb("iota_c", [P, P])
        seg = sb("seg", [P, 7, P], U8)
        zeros = sb("zeros", [P, N], BF16)
        junk = sb("junk", [P, T * D], BF16)
        vcol = sb("vcol", [P, V_ROWS])
        wr_hi = sb("wr_hi", [P, KT, E], F32R)
        wr_lo = sb("wr_lo", [P, KT, E], F32R)
        br = sb("br", [P, E])
        ss = sb("ss", [P, 8])
        nr = sb("nr", [P, 3, 16])
        lbc = sb("lbc", [P, 4, HEADS])
        rt = sb("rt", [P, 384])
        tab = sb("tab", [P, 2, T, ITEMS + 2])
        selT = sb("selT", [P, T, P], F32R)
        cur = sb("cur", [P, 2, T])
        itab = sb("itab", [1, 8], I32)
        PS = ctx.enter_context(nc.psum_tensor("PS", [P, 8, N], F32))

        def area(k, n=1):
            return SC[:, 1024 * k:1024 * (k + n)]

        vrow = SC[0:V_ROWS, 0:P]
        wr = SC[:, 1024:1024 + KT * E].rearrange("p (k e) -> p k e", k=KT)
        av = area(0).rearrange("p (t n) -> p t n", t=T)
        xb = area(1).rearrange("p (t n) -> p t n", t=T)
        bg = area(2).rearrange("p (t n) -> p t n", t=T)
        ws = area(3).rearrange("p (h j) -> p h j", h=AH)
        wsT = area(4).rearrange("p (h i) -> p h i", h=AH)
        lng = SC[:, 5 * 1024:5 * 1024 + AW]
        lnb = SC[:, 5 * 1024 + AW:6 * 1024]
        vc = area(6).rearrange("p (t n) -> p t n", t=T)
        sq = area(7).rearrange("p (t n) -> p t n", t=T)
        cT = SC[:, 8 * 1024:8 * 1024 + HK * (SEQ + 2)].rearrange("p (k s) -> p k s", k=HK)
        conv = area(6).rearrange("p (k s) -> p k s", k=HK)
        ybT = area(7).rearrange("p (k s) -> p k s", k=HK)
        uu = xn[:, 0, :].rearrange("p (t n) -> p t n", t=T)
        ya = xn[:, 1, :].rearrange("p (t n) -> p t n", t=T)
        sg = SC[:, 3 * 1024:3 * 1024 + N]
        hh = SC[:, 3 * 1024 + N:4 * 1024]
        pn = SC[:, 4 * 1024 + 512:5 * 1024].rearrange("p (t n) -> p t n", t=T)
        pgate = area(6, 2)
        qT = area(0, 2).rearrange("p (h s) -> p h s", h=HEADS)
        kT = area(2, 2).rearrange("p (h s) -> p h s", h=HEADS)
        attn = area(4, 2).rearrange("p (h t n) -> p h t n", h=HEADS, t=T)
        attx = area(6).rearrange("p (h n) -> p h n", h=HEADS)
        iv = area(7, 2).rearrange("p (t n) -> p t n", t=T)
        f_nat = area(4, 2).rearrange("p (t n) -> p t n", t=T)
        q_nat = area(7, 2).rearrange("p (t n) -> p t n", t=T)
        fT = xn[:, :, :].rearrange("p t n -> p (t n)").rearrange("p (h s) -> p h s", h=HEADS)
        tot = area(6)
        oo = area(0, 2).rearrange("p (t n) -> p t n", t=T)
        osq = area(2, 2)
        gg = xn
        acc = area(0, 2).rearrange("p (t n) -> p t n", t=T)
        ye_hi, ye_lo = xT_hi[:, :, P:2 * P], xT_lo[:, :, P:2 * P]
        sel = SC[:, 4 * 1024:4 * 1024 + T * P].rearrange("p (t c) -> p t c", t=T)

        raw_full = [(sem(f"raw_full{i}a"), sem(f"raw_full{i}b")) for i in range(RAW)]
        hi_done, lo_done, used = sem("hi_done"), sem("lo_done"), sem("used")
        gain_full, gain_free = sem("gain_full"), sem("gain_free")
        x_full, small_full, ws_full, ln_full, p_full = (
            sem("x_full"), sem("small_full"), sem("ws_full"), sem("ln_full"), sem("p_full"))
        consts, seg_in = sem("consts"), sem("seg_in")
        s_vT, s_vcol, s_wsT, s_wsE, s_wr = sem("vrow_turned"), sem("vcol_ready"), sem("ws_turned"), sem("wsT_ready"), sem("wr_split")
        xT_psum, xT_act, xT_ready = sem("xT_psum"), sem("xT_act"), sem("xT_ready")
        xn_ready = sem("xn_ready")
        ss_ready, rstd_ready = sem("ss_ready"), sem("rstd_ready")
        x_ready = sem("x_ready")
        v_gelu, vn_ready, xb_ready, c_ready, bg_ready, u_ready = (
            sem("v_gelu"), sem("vn_ready"), sem("xb_ready"), sem("c_ready"), sem("bg_ready"), sem("u_ready"))
        cT_psum, cT_ready, bgT_psum, yb_ready, gm_done, ya_ready = (
            sem("cT_psum"), sem("cT_ready"), sem("bgT_psum"), sem("yb_ready"), sem("gm_done"), sem("ya_ready"))
        yT_psum, ybT_hi = sem("yT_psum"), sem("ybT_hi")
        silu_done, h_ready, cur_step = sem("silu_done"), sem("h_ready"), sem("cur_step")
        hT_psum, hT_act, hT_ready = sem("hT_psum"), sem("hT_act"), sem("hT_ready")
        pT_psum, pT_act, pT_ready = sem("pT_psum"), sem("pT_act"), sem("pT_ready")
        gate_act = sem("gate_act")
        f_evac, q_evac, i_evac, g_evac = (
            sem("f_evac"), sem("q_evac"), sem("i_evac"), sem("g_evac"))
        fT_psum, fT_act, k_ready, qT_psum, qT_act = (
            sem("fT_psum"), sem("fT_act"), sem("k_ready"), sem("qT_psum"), sem("qT_act"))
        qk_ready, at_done = sem("qk_ready"), sem("at_done")
        o_done, o_sq, o_ready = sem("o_done"), sem("o_sq"), sem("o_ready")
        exp_ask, exp_done = sem("exp_ask"), sem("exp_done")
        lg_done, lg_max, lg_exp, sel_cnt, cnt_done, table_ready = (
            sem("lg_done"), sem("lg_max"), sem("lg_exp"), sem("sel_cnt"), sem("cnt_done"), sem("table_ready"))
        sel_ready, tsel_psum, selT_ready = sem("sel_ready"), sem("tsel_psum"), sem("selT_ready")
        gat_done, xg_act, xg_ready = sem("gathered"), sem("xg_act"), sem("xg_ready")
        ye_act, ye_ready, sc_done, acc_done = sem("ye_act"), sem("ye_ready"), sem("scattered"), sem("acc_done")
        act_step, dve_step, pool_step = sem("act_step"), sem("dve_step"), sem("pool_step")
        stored = sem("stored")

        block = ctx.enter_context(nc.Block())

        @block.sync
        def _(sp):
            def load(g, src, turns=0):
                for s in range(2):
                    part = slice(s * HW, (s + 1) * HW)
                    if g >= RAW:
                        sp.wait_ge(lo_done, turns * 2 * RING + (2 * (g - RAW) + s + 1))
                    sp.dma_start(raw[:, g % RAW, part], src[:, part]).then_inc(raw_full[g % RAW][s], 16)

            for t in range(T):
                sp.dma_start(x[:, t, :], x_d[0, t * P:(t + 1) * P, :]).then_inc(x_full, 16)
            g = G_AB
            for c in (1, 2, 3, 4, 0):
                for h in range(2):
                    load(g, w_in_ab[2 * c + h])
                    g += 1
            for h in (1, 0):
                for c in range(2):
                    load(g, w_out_ab[2 * c + h])
                    g += 1

            def load_gu(g, b, turns=0):
                for h in range(2):
                    load(g + h, ffn_w_gu[bass.ds(2 * b + h, 1), :, :].rearrange("g p n -> p (g n)"), turns)

            def load_down(g, b, turns=0):
                load(g, ffn_w_down[0][bass.ds(b * 256, 256), :].rearrange("(p r) n -> p (r n)", p=P), turns)

            load_gu(g, 0)
            with sp.Fori(0, (FB - 1) // 2) as it:
                for j in range(2):
                    load_gu(G_FFN + 2 + 3 * j, 2 * it + j + 1, it)
                    load_down(G_FFN + 4 + 3 * j, 2 * it + j, it)
            load_down(G_PLE0 - 1, FB - 1)

            def load_ple(layer, g, turns=0):
                load(g, ple_w_proj[layer].rearrange("(p r) n -> p (r n)", p=P), turns)
                for j in range(4):
                    load(g + 1 + j, ple_w_gate[4 * layer + j], turns)

            load_ple(0, G_PLE0)
            g = G_INC
            for c in (2, 3, 0, 1, 4, 5, 6, 7):
                for h in range(2):
                    load(g, w_in_c[2 * c + h])
                    g += 1
            for c in range(2):
                for h in range(2):
                    load(g, w_out_c[2 * c + h])
                    g += 1

            dn = e_w_down[0].rearrange("e f n -> e (f n)")

            def unit_gu(g, e, u, turns):
                for q in range(4):
                    src = e_w_gu[bass.ds(e, 1), bass.ds(u * 4 + q, 1), :, :]
                    load(g + q, src.rearrange("e g p n -> p (e g n)"), turns)

            def unit_down(g, e, u, turns):
                for j in range(2):
                    src = dn[bass.ds(e, 1), bass.ds(u * (N * D) + j * 256 * D, 256 * D)]
                    load(g + j, src.rearrange("e (p m) -> p (e m)", p=P), turns)

            def load_item(i, e, following):
                with sp.Fori(0, EU - 1) as u:
                    unit_gu(G_MOE + 4, e, u + 1, i * EU + u)
                    unit_down(G_MOE + 8, e, u, i * EU + u)
                if following is not None:
                    unit_gu(G_MOE + ITEM - 2, following, 0, i * EU)
                    unit_down(G_MOE + ITEM + 2, e, EU - 1, i * EU)
                else:
                    unit_down(G_MOE + ITEM - 2, e, EU - 1, i * EU)

            unit_gu(G_MOE, 0, 0, 0)
            with sp.Fori(0, E - 1) as i:
                load_item(i, i, i + 1)
            sp.wait_ge(table_ready, 1)
            last_item = sp.value_load(itab[0:1, 0:1], min_val=E - 1, max_val=ITEMS - 1)
            with sp.If(last_item > E - 1):
                with sp.Fori(E - 1, last_item) as i:
                    e = sp.value_load(itab[0:1, bass.ds(i - (E - 2), 1)], min_val=0, max_val=E - 1)
                    following = sp.value_load(itab[0:1, bass.ds(i - (E - 3), 1)], min_val=0, max_val=E - 1)
                    load_item(i, e, following)
            e = sp.value_load(itab[0:1, bass.ds(last_item - (E - 2), 1)], min_val=0, max_val=E - 1)
            load_item(last_item, e, None)
            load_ple(1, G_MOE, last_item * EU + EU)
            sp.wait_ge(x_ready, 6 * T)
            for t in range(T):
                sp.dma_start(out_d[0, t * P:(t + 1) * P, :], x[:, t, :]).then_inc(stored, 16)
            sp.wait_ge(stored, 16 * T)

        @block.gpsimd
        def _(pool):
            count = [0]

            def step(ins):
                count[0] += 1
                ins.then_inc(pool_step, 1)
                pool.wait_ge(pool_step, count[0])

            rows = [(V_N00, norm_g[0, 0]), (V_N02, norm_g[0, 2]), (V_N10, norm_g[1, 0]), (V_N12, norm_g[1, 2]),
                    (V_LB0, lb_param[0]), (V_LB1, lb_param[1])]
            for r, v in rows:
                pool.dma_start(vrow[r:r + 8, :], v.rearrange("(k p) -> k p", p=P)).then_inc(small_full, 16)
            pool.dma_start(vrow[V_ABS:V_ABS + 8, :], a_bs[0]).then_inc(small_full, 16)
            pool.dma_start(vrow[V_CONV:V_ROWS, :], b_conv[0].rearrange("w (k p) -> (w k) p", p=P)).then_inc(small_full, 16)
            pool.dma_start(wr[:, :, :], w_router[0].rearrange("(k p) e -> p k e", p=P)).then_inc(small_full, 16)
            pool.dma_start(br[:, :], b_router[0:1, :].broadcast_to([P, E])).then_inc(small_full, 16)
            pool.dma_start(ws, a_ws[0].rearrange("h i j -> i h j")).then_inc(ws_full, 16)
            pool.dma_start(lng, a_ln_g[0:1, :].broadcast_to([P, AW])).then_inc(ln_full, 16)
            pool.dma_start(lnb, a_ln_b[0:1, :].broadcast_to([P, AW])).then_inc(ln_full, 16)
            step(pool.memset(ident[:, :], 0.0))
            step(pool.affine_select(out=ident[:, :], in_=ident[:, :], compare_op=ALU.not_equal, fill=1.0, base=0,
                                    pattern=[[-1, P]], channel_multiplier=1))
            step(pool.memset(ones[:, :], 1.0))
            step(pool.affine_select(out=before[:, :], in_=ones[:, :], compare_op=ALU.is_gt, fill=0.0, base=0,
                                    pattern=[[1, P]], channel_multiplier=-1))
            pool.memset(zeros[:, :], 0.0).then_inc(consts, 1)
            pool.iota(iota_c[:, :].bitcast(I32), pattern=[[1, P]], base=0, channel_multiplier=0).then_inc(seg_in, 1)
            pool.iota(rt[:, 0:P].bitcast(I32), pattern=[[0, P]], base=0, channel_multiplier=1).then_inc(seg_in, 1)
            gains = [norm_g[0, 1:2], norm_g[0, 3:4], c_onorm_g[0:1], norm_g[1, 1:2], norm_g[1, 3:4]]
            for n, v in enumerate(gains):
                if n:
                    pool.wait_ge(gain_free, n)
                pool.dma_start(gain[:, :], v.broadcast_to([P, D])).then_inc(gain_full, 16)
                if n == 1:
                    pool.dma_start(pn, p_d[0, 0].rearrange("(t p) n -> p t n", p=P)).then_inc(p_full, 16)
                if n == 4:
                    pool.dma_start(pn[:, :, :], p_d[1, 0].rearrange("(t p) n -> p t n", p=P)).then_inc(p_full, 16)

        @block.tensor
        def _(pe):
            def split_matmul(out, a_hi, a_lo, b_hi, b_lo, start, stop):
                pe.matmul(out, a_hi, b_hi, start=start, stop=False, skip_group_check=True)
                pe.matmul(out, a_lo, b_hi, start=False, stop=False, skip_group_check=True)
                return pe.matmul(out, a_hi, b_lo, start=False, stop=stop, skip_group_check=True)

            def half_granule(g, pair, h, first, last, turns=0):
                for s in range(2):
                    pe.wait_ge(lo_done, turns * 2 * RING + (2 * g + s + 1))
                    for t, j in ((t, j) for t in range(T) for j in (2 * s, 2 * s + 1)):
                        r = slice(j * N, (j + 1) * N)
                        tok = slice(t * P, (t + 1) * P)
                        m = split_matmul(PS[:, 2 * pair + t, :], xT_hi[:, HK * h + j, tok], xT_lo[:, HK * h + j, tok],
                                         w_hi[:, g % RING, r], w_lo[:, g % RING, r],
                                         first and j == 0, last and j == HK - 1)
                    m.then_inc(used, 1)

            def turn_x(src):
                for b in range(4):
                    for j in range(2):
                        kt = 2 * b + j
                        for t in range(T):
                            c = (j * T + t) * P
                            m = pe.transpose(PS[:, 4 + b, c:c + P], src[:, t, kt * P:(kt + 1) * P], ident[:, :])
                    m.then_inc(xT_psum, 1)

            pe.wait_ge(consts, 1)
            pe.wait_ge(small_full, 160)
            pe.transpose(PS[:, 0, 0:V_ROWS], vrow, ident[0:V_ROWS, 0:V_ROWS]).then_inc(s_vT, 1)
            pe.wait_ge(ws_full, 16)
            for h in range(AH):
                m = pe.transpose(PS[:, 1 + h // 4, (h % 4) * P:(h % 4 + 1) * P], ws[:, h, :], ident[:, :])
            m.then_inc(s_wsT, 1)
            pe.wait_ge(xn_ready, 1)
            turn_x(xn)
            pe.wait_ge(xT_ready, 1)
            pe.wait_ge(s_wsE, 1)
            for n in range(4):
                for h in range(2):
                    half_granule(G_AB + 2 * n + h, n, h, h == 0, h == 1)
            pe.wait_ge(c_ready, 1)
            for k in range(HK):
                for t in range(T):
                    c = (k % 2) * SEQ + t * P
                    m = pe.transpose(PS[:, 2 + k // 2, c:c + P], xb[:, t, k * P:(k + 1) * P], ident[:, :])
            m.then_inc(cT_psum, 1)
            pe.wait_ge(v_gelu, 1)
            for h in range(2):
                half_granule(G_AB + 8 + h, 0, h, h == 0, h == 1)
            pe.wait_ge(bg_ready, 1)
            for k in range(HK):
                for t in range(T):
                    c = (k % 2) * SEQ + t * P
                    m = pe.transpose(PS[:, 4 + k // 2, c:c + P], bg[:, t, k * P:(k + 1) * P], ident[:, :])
            m.then_inc(bgT_psum, 1)
            pe.wait_ge(vn_ready, 1)
            for h in range(AH):
                o = PS[:, 6 + h // 4, (h % 4) * P:(h % 4 + 1) * P].rearrange("p (t d) -> p t d", t=T)
                m = pe.matmul(o, wsT[:, h, :], vc[:, :, h * AD:(h + 1) * AD], start=True, stop=True,
                              skip_group_check=True)
            m.then_inc(gm_done, 1)
            pe.wait_ge(ya_ready, 1)
            pe.wait_ge(cT_ready, 1)
            for k in range(HK):
                for t in range(T):
                    c = (k % 2) * SEQ + t * P
                    m = pe.transpose(PS[:, 2 + k // 2, c:c + P], ya[:, t, k * P:(k + 1) * P], ident[:, :])
            m.then_inc(yT_psum, 1)
            pe.wait_ge(yb_ready, 1)
            for c in range(2):
                half_granule(G_OUT + c, 2 + c, 1, True, False)
            pe.wait_ge(xT_ready, 2)
            for c in range(2):
                half_granule(G_OUT + 2 + c, 2 + c, 0, False, True)

            def clear(banks):
                for b in banks:
                    pe.matmul(PS[:, b, :], zeros[:, 0:P], zeros[:, :], start=True, stop=False, skip_group_check=True)

            def ffn_gu(g, turns=0):
                half_granule(g, 0, 0, True, False, turns)
                half_granule(g + 1, 0, 1, False, True, turns)

            def ffn_turn(n):
                pe.wait_ge(h_ready, n)
                hv = hh.rearrange("p (t q r) -> p t r q", t=T, r=2)
                for r in range(2):
                    for t in range(T):
                        c = (r * T + t) * P
                        m = pe.transpose(PS[:, 2, c:c + P], hv[:, t, r, :], ident[:, :])
                m.then_inc(hT_psum, 1)

            def ffn_down(g, n, last, turns=0):
                pe.wait_ge(hT_ready, n)
                for r in range(2):
                    pe.wait_ge(lo_done, turns * 2 * RING + (2 * g + r + 1))
                    for c in range(2):
                        for t in range(T):
                            a = slice((r * T + t) * P, (r * T + t + 1) * P)
                            w = slice(r * D + c * N, r * D + (c + 1) * N)
                            m = split_matmul(PS[:, 4 + 2 * c + t, :], hT_hi[:, a], hT_lo[:, a],
                                             w_hi[:, g % RING, w], w_lo[:, g % RING, w], False, last and r == 1)
                    m.then_inc(used, 1)

            pe.wait_ge(xn_ready, 2)
            turn_x(xn)
            pe.wait_ge(xT_ready, 3)
            ffn_gu(G_FFN)
            clear(range(4, 8))
            ffn_turn(1)
            with pe.Fori(0, (FB - 1) // 2) as it:
                for j in range(2):
                    ffn_gu(G_FFN + 2 + 3 * j, it)
                    ffn_down(G_FFN + 4 + 3 * j, 2 * it + (j + 1), False, it)
                    ffn_turn(2 * it + (j + 2))
            ffn_down(G_PLE0 - 1, FB, True)

            def ple(layer, g, turned, turns=0):
                pe.wait_ge(p_full, 16 * (layer + 1))
                if layer == 1:
                    pe.wait_ge(acc_done, last_item * T + 3 * T)
                for kk in range(2):
                    for t in range(T):
                        c = (kk * T + t) * P
                        m = pe.transpose(PS[:, 3, c:c + P], pn[:, t, kk::2], ident[:, :])
                m.then_inc(pT_psum, 1)
                pe.wait_ge(pT_ready, layer + 1)
                for kk in range(2):
                    pe.wait_ge(lo_done, turns * 2 * RING + (2 * g + kk + 1))
                    for c in range(2):
                        for t in range(T):
                            a = slice((kk * T + t) * P, (kk * T + t + 1) * P)
                            w = slice(kk * D + c * N, kk * D + (c + 1) * N)
                            m = split_matmul(PS[:, 2 * c + t, :], hT_hi[:, a], hT_lo[:, a],
                                             w_hi[:, g % RING, w], w_lo[:, g % RING, w], kk == 0, kk == 1)
                    m.then_inc(used, 1)
                pe.wait_ge(x_ready, turned)
                turn_x(x)
                pe.wait_ge(xT_ready, 4 if layer == 0 else 8)
                for j in range(4):
                    half_granule(g + 1 + j, 2 + j // 2, j % 2, j % 2 == 0, j % 2 == 1, turns)

            ple(0, G_PLE0, 2 * T)

            pe.wait_ge(xn_ready, 3)
            turn_x(xn)
            pe.wait_ge(xT_ready, 5)

            def proj(n, evac=None):
                c, h = n // 2, n % 2
                if evac:
                    pe.wait_ge(*evac)
                half_granule(G_INC + n, c % 2, h, h == 0, h == 1)

            def turn_heads(src, signal):
                for hd in range(HEADS):
                    for t in range(T):
                        c = (hd % 2) * SEQ + t * P
                        m = pe.transpose(PS[:, 4 + hd // 2, c:c + P], src[:, t, hd * P:(hd + 1) * P], ident[:, :])
                    if hd % 2:
                        m.then_inc(signal, 1)

            def level(n):
                pe.wait_ge(qk_ready, n + 1)
                for hd in range(HEADS):
                    for t in range(T):
                        tok = slice(t * P, (t + 1) * P)
                        c = (hd % 2) * SEQ + t * P
                        m = pe.matmul(PS[:, 4 + hd // 2, c:c + P], kT[:, hd, tok], qT[:, hd, tok],
                                      start=True, stop=True, skip_group_check=True)
                m.then_inc(at_done, 1)

            for n in range(4):
                proj(n)
            proj(4, (f_evac, 1))
            proj(5)
            pe.wait_ge(f_evac, 2)
            turn_heads(f_nat, fT_psum)
            proj(6)
            proj(7)
            pe.wait_ge(q_evac, 2)
            pe.wait_ge(fT_act, 4)
            turn_heads(q_nat, qT_psum)
            proj(8)
            level(0)
            proj(9)
            level(1)
            proj(10)
            level(2)
            proj(11)
            level(3)
            proj(12, (i_evac, 1))
            level(4)
            proj(13)
            level(5)
            proj(14, (i_evac, 2))
            level(6)
            proj(15)
            level(7)
            pe.wait_ge(qk_ready, 9)
            for hd in range(HEADS):
                m = pe.matmul(PS[:, 4 + hd // 4, (hd % 4) * P:(hd % 4 + 1) * P], kT[:, hd, 0:P], qT[:, hd, P:SEQ],
                              start=True, stop=True, skip_group_check=True)
            m.then_inc(at_done, 1)
            pe.wait_ge(g_evac, 2)
            pe.wait_ge(qk_ready, 10)
            for t in range(T):
                for hd in range(HEADS):
                    o = PS[:, 2 * t + hd // 4, (hd % 4) * P:(hd % 4 + 1) * P]
                    m = pe.matmul(o, attn[:, hd, t, :], iv[:, t, hd * HD:(hd + 1) * HD], start=True, stop=(t == 0),
                                  skip_group_check=True)
                    if t == 1:
                        m = pe.matmul(o, attx[:, hd, :], iv[:, 0, hd * HD:(hd + 1) * HD], start=False, stop=True,
                                      skip_group_check=True)
            m.then_inc(o_done, 1)
            pe.wait_ge(o_ready, 1)
            turn_x(oo)
            pe.wait_ge(xT_ready, 6)
            for c in range(2):
                for h in range(2):
                    half_granule(G_OUTC + 2 * c + h, 2 + c, h, h == 0, h == 1)

            pe.wait_ge(xn_ready, 4)
            turn_x(xn)
            pe.wait_ge(xT_ready, 7)
            pe.wait_ge(s_wr, 2)
            for t in range(T):
                for k in range(KT):
                    tok = slice(t * P, (t + 1) * P)
                    m = split_matmul(PS[:, 0, t * E:(t + 1) * E], xT_hi[:, k, tok], xT_lo[:, k, tok],
                                     wr_hi[:, k, :], wr_lo[:, k, :], k == 0, k == KT - 1)
            m.then_inc(lg_done, 1)
            pe.wait_ge(sel_cnt, 1)
            chosen = rt[:, 0:2 * E].rearrange("p (t e) -> p t e", t=T)
            pe.matmul(PS[:, 1, 0:E], before[:, :], chosen[:, 0, :], start=True, stop=True, skip_group_check=True)
            pe.matmul(PS[:, 1, E:2 * E], before[:, :], chosen[:, 1, :], start=True, stop=False, skip_group_check=True)
            pe.matmul(PS[:, 1, E:2 * E], ones[:, :], chosen[:, 0, :], start=False, stop=True, skip_group_check=True)
            pe.matmul(PS[:, 1, 2 * E:3 * E], ones[:, :], chosen[:, 0, :], start=True, stop=False, skip_group_check=True)
            pe.matmul(PS[:, 1, 2 * E:3 * E], ones[:, :], chosen[:, 1, :], start=False, stop=True,
                      skip_group_check=True).then_inc(cnt_done, 1)

            def gather(half):
                for k in range(HK * half, HK * (half + 1)):
                    for t in range(T):
                        m = pe.matmul(PS[:, 6 + half, (k % 4) * P:(k % 4 + 1) * P], xn[:, t, k * P:(k + 1) * P],
                                      sel[:, t, :], start=(t == 0), stop=(t == T - 1), skip_group_check=True)
                m.then_inc(gat_done, 1)

            def turn_sel():
                for t in range(T):
                    m = pe.transpose(PS[:, 3, t * P:(t + 1) * P], sel[:, t, :], ident[:, :])
                m.then_inc(tsel_psum, 1)

            def scatter():
                for t in range(T):
                    for c in range(2):
                        o, q = PS[:, 4 - 4 * t + c, :], slice(HK * c, HK * (c + 1))
                        pe.matmul(o, selT[:, t, :], ye_hi[:, q, :], start=True, stop=False, skip_group_check=True)
                        m = pe.matmul(o, selT[:, t, :], ye_lo[:, q, :], start=False, stop=True, skip_group_check=True)
                    m.then_inc(sc_done, 1)

            def unit_gu(g, turns):
                for side in range(2):
                    for h in range(2):
                        for j in range(HK):
                            if j % 2 == 0:
                                pe.wait_ge(lo_done, turns * 2 * RING + (2 * (g + 2 * side + h) + j // 2 + 1))
                            r = slice(j * N, (j + 1) * N)
                            s = (g + 2 * side + h) % RING
                            m = split_matmul(PS[:, side, :], xT_hi[:, HK * h + j, 0:P], xT_lo[:, HK * h + j, 0:P],
                                             w_hi[:, s, r], w_lo[:, s, r], h == 0 and j == 0, h == 1 and j == HK - 1)
                            if j % 2:
                                m.then_inc(used, 1)

            def unit_turn(n):
                pe.wait_ge(h_ready, n)
                hv = hh.rearrange("p (j q r) -> p j r q", j=2, r=2)
                for j in range(2):
                    for r in range(2):
                        c = (j * 2 + r) * P
                        m = pe.transpose(PS[:, 2, c:c + P], hv[:, j, r, :], ident[:, :])
                m.then_inc(hT_psum, 1)

            def unit_down(g, n, last, turns):
                pe.wait_ge(hT_ready, n)
                for j in range(2):
                    for r in range(2):
                        pe.wait_ge(lo_done, turns * 2 * RING + (2 * (g + j) + r + 1))
                        for c in range(2):
                            a = slice((j * 2 + r) * P, (j * 2 + r + 1) * P)
                            w = slice(r * D + c * N, r * D + (c + 1) * N)
                            s = (g + j) % RING
                            m = split_matmul(PS[:, 4 + c, :], hT_hi[:, a], hT_lo[:, a],
                                             w_hi[:, s, w], w_lo[:, s, w], False, last and j == 1 and r == 1)
                        m.then_inc(used, 1)

            def item(i, last):
                unit_turn(i * EU + (FB + 1))
                if not last:
                    pe.wait_ge(sel_ready, i + 2)
                    gather(0)
                pe.wait_ge(ye_ready, i + 1)
                pe.wait_ge(selT_ready, i + 1)
                scatter()
                if not last:
                    gather(1)
                pe.wait_ge(acc_done, i * T + (T + 1))
                clear((4,))
                pe.wait_ge(acc_done, i * T + 2 * T)
                clear((5,))
                with pe.Fori(0, EU - 1) as u:
                    unit_gu(G_MOE + 4, i * EU + u)
                    unit_down(G_MOE + 8, i * EU + u + (FB + 1), False, i * EU + u)
                    unit_turn(i * EU + u + (FB + 2))
                if last:
                    unit_down(G_MOE + ITEM - 2, i * EU + (FB + EU), True, i * EU)
                else:
                    pe.wait_ge(selT_ready, i + 2)
                    turn_sel()
                    pe.wait_ge(xg_ready, i + 2)
                    unit_gu(G_MOE + ITEM - 2, i * EU)
                    unit_down(G_MOE + ITEM + 2, i * EU + (FB + EU), True, i * EU)

            pe.wait_ge(sel_ready, 1)
            gather(0)
            gather(1)
            turn_sel()
            pe.wait_ge(table_ready, 1)
            last_item = pe.value_load(itab[0:1, 0:1], min_val=E - 1, max_val=ITEMS - 1)
            pe.wait_ge(xg_ready, 1)
            unit_gu(G_MOE, 0)
            with pe.Fori(0, last_item) as i:
                item(i, False)
            item(last_item, True)
            pe.wait_ge(ye_ready, last_item + 2)
            pe.wait_ge(selT_ready, last_item + 2)
            scatter()
            ple(1, G_MOE, 5 * T, last_item * EU + EU)

        @block.scalar
        def _(act):
            def hi(g, turns=0):
                for s in range(2):
                    part = slice(s * HW, (s + 1) * HW)
                    if g >= RING:
                        act.wait_ge(used, turns * 2 * RING + (2 * (g - RING) + s + 1))
                    act.wait_ge(raw_full[g % RAW][s], turns * (16 * RING // RAW) + 16 * (g // RAW + 1))
                    act.activation(w_hi[:, g % RING, part], raw[:, g % RAW, part], ACT.Copy).then_inc(hi_done, 1)

            def product(g, turns=0):
                act.wait_ge(used, turns * 2 * RING + 2 * g)

            def his(a, b):
                for g in range(a, b):
                    hi(g)

            def xT(n, v, base):
                for b in range(4):
                    act.wait_ge(xT_psum, 4 * base + b + 1)
                    for j in range(2):
                        kt = 2 * b + j
                        src = PS[:, 4 + b, j * SEQ:(j + 1) * SEQ]
                        m = act.activation(xT_hi[:, kt, :], src, ACT.Copy,
                                           scale=1.0 if v is None else vcol[:, v + kt:v + kt + 1])
                    m.then_inc(xT_act, 1)

            def square_y(src):
                for c in range(2):
                    for t in range(T):
                        m = act.activation(junk[:, (2 * c + t) * N:(2 * c + t + 1) * N], src(c, t), ACT.Square,
                                           accum_out=ss[:, 2 * c + t:2 * c + t + 1])
                m.then_inc(ss_ready, 1)

            def square_x():
                for t in range(T):
                    m = act.activation(junk[:, t * D:(t + 1) * D], x[:, t, :], ACT.Square, accum_out=ss[:, 4 + t:5 + t])
                m.then_inc(ss_ready, 1)

            def scale_x(n):
                act.wait_ge(rstd_ready, n)
                for t in range(T):
                    m = act.activation(xn[:, t, :], x[:, t, :], ACT.Copy, scale=nr[:, 1, t:t + 1])
                m.then_inc(xn_ready, 1)

            in_psum = lambda c, t: PS[:, 4 + 2 * c + t, :]

            act.wait_ge(x_full, 16 * T)
            square_x()
            act.wait_ge(small_full, 160)
            act.activation(wr_hi[:, :, :], wr[:, :, :], ACT.Copy).then_inc(s_wr, 1)
            scale_x(1)
            his(0, 3)
            act.wait_ge(s_vcol, 1)
            xT(0, V_N00, 0)
            act.wait_ge(exp_ask, 1)
            act.activation(lbc[:, 0:2, :], lbc[:, 2:4, :], ACT.Exp).then_inc(exp_done, 1)
            his(3, 7)
            product(G_AB + 2)
            act.activation(av, PS[:, 0:2, :], ACT.Gelu_apprx_tanh).then_inc(v_gelu, 1)
            his(7, 9)
            product(G_AB + 4)
            act.activation(xb, PS[:, 2:4, :], ACT.Copy).then_inc(xb_ready, 1)
            his(9, 12)
            product(G_AB + 8)
            act.activation(bg, PS[:, 6:8, :], ACT.Copy).then_inc(bg_ready, 1)
            act.wait_ge(cT_psum, 1)
            act.activation(cT[:, :, 2:SEQ + 2], PS[:, 2:4, :].rearrange("p b (k s) -> p (b k) s", k=2),
                           ACT.Copy).then_inc(cT_ready, 1)
            his(12, 14)
            product(G_AB + 10)
            act.activation(uu, PS[:, 0:2, :], ACT.Gelu_apprx_tanh).then_inc(u_ready, 1)
            act.wait_ge(ybT_hi, 1)
            act.activation(xT_hi[:, HK:KT, :], ybT, ACT.Copy).then_inc(xT_act, 1)
            act.wait_ge(yT_psum, 1)
            act.activation(xT_hi[:, 0:HK, :], PS[:, 2:4, :].rearrange("p b (k s) -> p (b k) s", k=2),
                           ACT.Copy).then_inc(xT_act, 1)
            his(14, 18)
            product(G_FFN)
            square_y(in_psum)
            act.wait_ge(x_ready, T)
            square_x()
            scale_x(3)
            xT(1, V_N02, 1)
            his(18, 20)

            def silu():
                act.activation(sg.rearrange("p (t n) -> p t n", t=T), PS[:, 0:2, 0:256], ACT.Silu).then_inc(silu_done, 1)

            def hT(n):
                act.wait_ge(hT_psum, n)
                act.activation(hT_hi[:, :], PS[:, 2, :], ACT.Copy).then_inc(hT_act, 1)

            hi(20)
            product(G_FFN + 2)
            silu()
            hT(1)
            with act.Fori(0, (FB - 1) // 2) as it:
                for j in range(2):
                    hi(21 + 3 * j, it)
                    hi(22 + 3 * j, it)
                    product(G_FFN + 4 + 3 * j, it)
                    silu()
                    hi(23 + 3 * j, it)
                    hT(2 * it + (j + 2))
            product(G_PLE0)
            square_y(in_psum)

            def pT(n):
                act.wait_ge(pT_psum, n)
                act.activation(hT_hi[:, :], PS[:, 3, :], ACT.Copy).then_inc(pT_act, 1)

            def gate(g, turns=0):
                for c in range(2):
                    product(g + 3 + 2 * c, turns)
                    act.activation(pgate[:, c * 1024:(c + 1) * 1024], PS[:, 4 + 2 * c:6 + 2 * c, :].rearrange("p b n -> p (b n)"),
                                   ACT.Sigmoid).then_inc(gate_act, 1)

            pT(1)
            his(51, 52)
            act.wait_ge(x_ready, 2 * T)
            xT(2, None, 2)
            his(52, 54)
            hi(54)
            gate(G_PLE0)
            act.wait_ge(x_ready, 3 * T)
            square_x()
            scale_x(5)
            xT(3, V_N10, 3)
            his(55, 59)
            product(G_INC + 2)
            act.activation(f_nat[:, :, 0:N], PS[:, 0:2, :], ACT.Copy).then_inc(f_evac, 1)
            his(59, 61)
            product(G_INC + 4)
            act.activation(f_nat[:, :, N:D], PS[:, 2:4, :], ACT.Copy).then_inc(f_evac, 1)
            his(61, 62)
            product(G_INC + 6)
            act.activation(q_nat[:, :, 0:N], PS[:, 0:2, :], ACT.Copy).then_inc(q_evac, 1)
            for b in range(4):
                act.wait_ge(fT_psum, b + 1)
                act.activation(fT[:, 2 * b:2 * b + 2, :], PS[:, 4 + b, :].rearrange("p (h s) -> p h s", h=2),
                               ACT.Sigmoid).then_inc(fT_act, 1)
            his(62, 64)
            product(G_INC + 8)
            act.activation(q_nat[:, :, N:D], PS[:, 2:4, :], ACT.Copy).then_inc(q_evac, 1)
            for b in range(4):
                act.wait_ge(qT_psum, b + 1)
                act.activation(qT[:, 2 * b:2 * b + 2, :], PS[:, 4 + b, :].rearrange("p (h s) -> p h s", h=2),
                               ACT.Silu).then_inc(qT_act, 1)
            his(64, 66)
            product(G_INC + 10)
            act.activation(iv[:, :, 0:N], PS[:, 0:2, :], ACT.Copy).then_inc(i_evac, 1)
            his(66, 68)
            product(G_INC + 12)
            act.activation(iv[:, :, N:D], PS[:, 2:4, :], ACT.Copy).then_inc(i_evac, 1)
            his(68, 70)
            product(G_INC + 14)
            act.wait_ge(qk_ready, 4)
            act.activation(gg[:, :, 0:N], PS[:, 0:2, :], ACT.Silu).then_inc(g_evac, 1)
            his(70, 72)
            product(G_INC + 16)
            act.activation(gg[:, :, N:D], PS[:, 2:4, :], ACT.Silu).then_inc(g_evac, 1)
            his(72, 74)
            act.wait_ge(o_done, 1)
            act.activation(osq, PS[:, 0:4, :].rearrange("p b n -> p (b n)"), ACT.Square).then_inc(o_sq, 1)
            xT(4, None, 4)
            his(74, 76)
            product(G_MOE)
            square_y(in_psum)
            act.wait_ge(x_ready, 4 * T)
            square_x()
            scale_x(7)
            xT(5, V_N12, 5)
            act.wait_ge(lg_max, 1)
            act.activation(rt[:, 2 * E:4 * E], rt[:, 4 * E:6 * E], ACT.Exp).then_inc(lg_exp, 1)

            def xg(n):
                act.wait_ge(gat_done, n * 2)
                for k in range(KT):
                    m = act.activation(xT_hi[:, k, 0:P], PS[:, 6 + k // 4, (k % 4) * P:(k % 4 + 1) * P], ACT.Copy,
                                       scale=vcol[:, V_N12 + k:V_N12 + k + 1])
                m.then_inc(xg_act, 1)

            def unit_silu():
                act.activation(sg, PS[:, 0, :], ACT.Silu).then_inc(silu_done, 1)

            act.wait_ge(table_ready, 1)
            last_item = act.value_load(itab[0:1, 0:1], min_val=E - 1, max_val=ITEMS - 1)
            def output(g, turns):
                product(g, turns)
                act.activation(ye_hi, PS[:, 4:6, :].rearrange("p b (k c) -> p (b k) c", k=HK), ACT.Copy).then_inc(ye_act, 1)

            def item(i, last):
                product(G_MOE + 2, i * EU)
                unit_silu()
                hi(G_MOE + 7, i * EU)
                output(G_MOE + 4, i * EU)
                hT(i * EU + (FB + 1))
                hi(G_MOE + 8, i * EU)
                hi(G_MOE + 9, i * EU)
                act.wait_ge(tsel_psum, i + 1)
                act.wait_ge(sc_done, i * T + T)
                act.activation(selT[:, :, :], PS[:, 3, 0:T * P].rearrange("p (t c) -> p t c", t=T),
                               ACT.Copy).then_inc(selT_ready, 1)

                def unit(u, end):
                    for q in (10, 11, 12):
                        hi(G_MOE + q, i * EU + u)
                    product(G_MOE + 8, i * EU + u)
                    unit_silu()
                    if end:
                        xg(i + 2)
                    hi(G_MOE + 13, i * EU + u)
                    hi(G_MOE + 14, i * EU + u)
                    hT(i * EU + u + (FB + 2))
                    hi(G_MOE + 15, i * EU + u)

                with act.Fori(0, EU - 2) as u:
                    unit(u, False)
                unit(EU - 2, not last)
                for q in ((4,) if last else (4, 5, 6)):
                    hi(G_MOE + ITEM + q, i * EU)

            xg(1)
            for q in (4, 5, 6):
                hi(G_MOE + q)
            product(G_MOE + 4)
            with act.Fori(0, last_item) as i:
                item(i, False)
            item(last_item, True)
            output(G_MOE, last_item * EU + EU)
            act.wait_ge(acc_done, last_item * T + 3 * T)
            square_y(lambda c, t: acc[:, t, c * N:(c + 1) * N])
            pT(2)
            act.wait_ge(x_ready, 5 * T)
            xT(7, None, 6)
            gate(G_MOE, last_item * EU + EU)

        @block.vector
        def _(dve):
            count = [0]

            def step(ins):
                count[0] += 1
                ins.then_inc(dve_step, 1)
                dve.wait_ge(dve_step, count[0])

            def lo(g, turns=0):
                for s in range(2):
                    part = slice(s * HW, (s + 1) * HW)
                    dve.wait_ge(hi_done, turns * 2 * RING + (2 * g + s + 1))
                    dve.tensor_tensor(w_lo[:, g % RING, part], raw[:, g % RAW, part], w_hi[:, g % RING, part].bitcast(F32),
                                      ALU.subtract).then_inc(lo_done, 1)

            def los(a, b):
                for g in range(a, b):
                    lo(g)

            def rsqrt(n):
                v, y, a = (nr[:, k, 0:n] for k in range(3))
                step(dve.tensor_single_scalar(a.bitcast(I32), v.bitcast(I32), 1, op=ALU.logical_shift_right))
                step(dve.tensor_scalar(y.bitcast(I32), a.bitcast(I32), -1.0, float(0x5F3759DF), ALU.mult, ALU.add))
                for _ in range(3):
                    step(dve.tensor_tensor(a, y, y, ALU.mult))
                    step(dve.scalar_tensor_tensor(out=a, in0=a, scalar=-0.5, in1=v, op0=ALU.mult, op1=ALU.mult))
                    step(dve.scalar_tensor_tensor(out=y, in0=a, scalar=1.5, in1=y, op0=ALU.add, op1=ALU.mult))

            def norm_x(n):
                dve.wait_ge(ss_ready, n)
                step(dve.tensor_scalar(nr[:, 0, 0:T], ss[:, 4:4 + T], 1.0 / D, EPS, ALU.mult, ALU.add))
                rsqrt(T)
                dve.sem_inc(rstd_ready, 1)

            def norm_y(n, gains, src, xr):
                dve.wait_ge(ss_ready, n)
                step(dve.tensor_tensor(nr[:, 2, 0:T], ss[:, 0:T], ss[:, T:2 * T], ALU.add))
                step(dve.tensor_scalar(nr[:, 0, 0:T], nr[:, 2, 0:T], 1.0 / D, EPS, ALU.mult, ALU.add))
                rsqrt(T)
                dve.sem_inc(rstd_ready, 1)
                dve.wait_ge(gain_full, 16 * gains)
                for t in range(T):
                    for c in range(2):
                        cols = slice(c * N, (c + 1) * N)
                        y = src(c, t)
                        tmp = SC[:, 5 * 1024 + c * N:5 * 1024 + (c + 1) * N]
                        m = dve.scalar_tensor_tensor(out=tmp, in0=y, scalar=nr[:, 1, t:t + 1], in1=gain[:, cols],
                                                     op0=ALU.mult, op1=ALU.mult)
                        step(m)
                        if t == T - 1 and c == 1 and gains < 5:
                            dve.sem_inc(gain_free, 1)
                        m = dve.tensor_tensor(x[:, t, cols], x[:, t, cols], tmp, ALU.add)
                        if c == 0:
                            step(m)
                    m.then_inc(x_ready, 1)
                    dve.wait_ge(x_ready, xr - T + t + 1)

            def xT(n, v, base):
                for b in range(4):
                    dve.wait_ge(xT_act, base + b + 1)
                    for j in range(2):
                        kt = 2 * b + j
                        src = PS[:, 4 + b, j * SEQ:(j + 1) * SEQ]
                        up = xT_hi[:, kt, :].bitcast(F32)
                        if v is None:
                            m = dve.tensor_tensor(xT_lo[:, kt, :], src, up, ALU.subtract)
                        else:
                            m = dve.scalar_tensor_tensor(out=xT_lo[:, kt, :], in0=src, scalar=vcol[:, v + kt:v + kt + 1],
                                                         in1=up, op0=ALU.mult, op1=ALU.subtract)
                m.then_inc(xT_ready, 1)

            in_psum = lambda c, t: PS[:, 4 + 2 * c + t, :]

            dve.memset(cT[:, :, 0:2], 0.0)
            norm_x(1)
            dve.wait_ge(s_vT, 1)
            step(dve.tensor_copy(vcol[:, :], PS[:, 0, 0:V_ROWS]))
            dve.sem_inc(s_vcol, 1)
            l0, l1 = vcol[:, V_LB0:V_LB0 + 8], vcol[:, V_LB1:V_LB1 + 8]
            step(dve.tensor_tensor(lbc[:, 0, :], l0, l1, ALU.max))
            step(dve.tensor_tensor(lbc[:, 2, :], l0, lbc[:, 0, :], ALU.subtract))
            step(dve.tensor_tensor(lbc[:, 3, :], l1, lbc[:, 0, :], ALU.subtract))
            dve.sem_inc(exp_ask, 1)
            dve.wait_ge(s_wr, 1)
            dve.tensor_tensor(wr_lo[:, :, :], wr[:, :, :], wr_hi[:, :, :].bitcast(F32), ALU.subtract).then_inc(s_wr, 1)
            dve.wait_ge(s_wsT, 1)
            step(dve.tensor_copy(wsT, PS[:, 1:3, :].rearrange("p b (h i) -> p (b h) i", h=4)))
            dve.memset(wsT[64:P, :, 0:64], 0.0).then_inc(s_wsE, 1)
            los(0, 3)
            xT(1, V_N00, 0)
            dve.wait_ge(seg_in, 2)
            ii, ir, cmp = iota_c[:, :].bitcast(I32), rt[:, 0:P].bitcast(I32), rt[:, P:2 * P]
            xr_ = rt[:, 2 * P:3 * P].bitcast(I32)
            step(dve.tensor_tensor(xr_, ii, ir, ALU.bitwise_xor))
            step(dve.tensor_tensor(cmp, ii, ir, ALU.is_gt))
            step(dve.tensor_copy(rt[:, 0:P], xr_))
            step(dve.tensor_tensor(cmp, cmp, rt[:, 0:P], ALU.mult))
            for lv in range(7):
                dve.tensor_scalar(seg[:, lv, :], cmp, float(2 ** lv), None, ALU.is_ge)
            step(dve.tensor_copy(rt[:, 0:P], ii))
            step(dve.tensor_copy(iota_c[:, :], rt[:, 0:P]))
            dve.wait_ge(exp_done, 1)
            step(dve.tensor_tensor(lbc[:, 2, :], lbc[:, 0, :], lbc[:, 1, :], ALU.add))
            step(dve.reciprocal(lbc[:, 3, :], lbc[:, 2, :]))
            step(dve.tensor_tensor(lbc[:, 0, :], lbc[:, 0, :], lbc[:, 3, :], ALU.mult))
            step(dve.tensor_tensor(lbc[:, 1, :], lbc[:, 1, :], lbc[:, 3, :], ALU.mult))
            step(dve.tensor_tensor(lbc[:, 2, :], lbc[:, 0, :], lbc[:, 1, :], ALU.add))
            step(dve.tensor_tensor(lbc[:, 0, :], lbc[:, 2, :], lbc[:, 0, :], ALU.subtract))
            step(dve.tensor_scalar(lbc[:, 1, :], lbc[:, 0, :], -1.0, 1.0, ALU.mult, ALU.add))
            los(3, 8)
            heads = "p t (h d) -> p (t h) d"
            AG = T * AH
            m1, m2 = rt[:, 0:AG], rt[:, AG:2 * AG]
            dve.wait_ge(v_gelu, 1)
            vh, ch, qh = av.rearrange(heads, h=AH), vc.rearrange(heads, h=AH), sq.rearrange(heads, h=AH)
            step(dve.tensor_reduce(m1, vh, AXX, ALU.add))
            step(dve.tensor_scalar(m1, m1, 1.0 / AD, None, ALU.mult))
            step(dve.tensor_tensor(ch, vh, m1.unsqueeze(2).broadcast_to([P, AG, AD]), ALU.subtract))
            lo(8)
            dve.wait_ge(xb_ready, 1)
            dve.wait_ge(used, 2 * (G_AB + 6))
            dve.tensor_tensor(xb, PS[:, 4:6, :], xb, ALU.mult).then_inc(c_ready, 1)
            step(dve.tensor_tensor(qh, ch, ch, ALU.mult))
            step(dve.tensor_reduce(m2, qh, AXX, ALU.add))
            step(dve.tensor_scalar(nr[:, 0, 0:AG], m2, 1.0 / AD, EPS, ALU.mult, ALU.add))
            rsqrt(AG)
            lo(9)
            step(dve.tensor_tensor(ch, ch, nr[:, 1, 0:AG].unsqueeze(2).broadcast_to([P, AG, AD]), ALU.mult))
            dve.wait_ge(ln_full, 32)
            step(dve.tensor_tensor(vc, vc, lng.unsqueeze(1).broadcast_to([P, T, AW]), ALU.mult))
            dve.tensor_tensor(vc, vc, lnb.unsqueeze(1).broadcast_to([P, T, AW]), ALU.add).then_inc(vn_ready, 1)
            los(10, 12)
            dve.wait_ge(cT_ready, 1)
            dve.wait_ge(gm_done, 1)
            for tap in range(3):
                for k in range(HK):
                    w = vcol[:, V_CONV + tap * HK + k:V_CONV + tap * HK + k + 1]
                    src = cT[:, k, tap:tap + SEQ]
                    if tap == 0:
                        m = dve.tensor_scalar(conv[:, k, :], src, w, None, ALU.mult)
                    else:
                        m = dve.scalar_tensor_tensor(out=conv[:, k, :], in0=src, scalar=w, in1=conv[:, k, :],
                                                     op0=ALU.mult, op1=ALU.add)
                step(m)
            dve.wait_ge(bgT_psum, 1)
            step(dve.tensor_tensor(ybT, conv, PS[:, 4:6, :].rearrange("p b (k s) -> p (b k) s", k=2), ALU.mult))
            dve.sem_inc(ybT_hi, 1)
            dve.wait_ge(u_ready, 1)
            for h in range(AH):
                src = PS[:, 6 + h // 4, (h % 4) * P:(h % 4 + 1) * P].rearrange("p (t d) -> p t d", t=T)
                cols = slice(h * AD, (h + 1) * AD)
                m = dve.scalar_tensor_tensor(out=ya[:, :, cols], in0=src, scalar=vcol[:, V_ABS + h:V_ABS + h + 1],
                                             in1=uu[:, :, cols], op0=ALU.add, op1=ALU.mult)
            m.then_inc(ya_ready, 1)
            dve.wait_ge(xT_act, 5)
            dve.tensor_tensor(xT_lo[:, HK:KT, :], ybT, xT_hi[:, HK:KT, :].bitcast(F32), ALU.subtract).then_inc(yb_ready, 1)
            dve.wait_ge(xT_act, 6)
            dve.tensor_tensor(xT_lo[:, 0:HK, :], PS[:, 2:4, :].rearrange("p b (k s) -> p (b k) s", k=2),
                              xT_hi[:, 0:HK, :].bitcast(F32), ALU.subtract).then_inc(xT_ready, 1)
            los(12, 18)
            norm_y(2, 1, in_psum, T)
            norm_x(3)
            xT(3, V_N02, 6)
            los(18, 21)

            def hidden(n):
                dve.wait_ge(silu_done, n)
                dve.tensor_tensor(hh.rearrange("p (t n) -> p t n", t=T), sg.rearrange("p (t n) -> p t n", t=T),
                                  PS[:, 0:2, 256:512], ALU.mult).then_inc(h_ready, 1)

            def hT(n):
                dve.wait_ge(hT_act, n)
                dve.tensor_tensor(hT_lo[:, :], PS[:, 2, :], hT_hi[:, :].bitcast(F32), ALU.subtract).then_inc(hT_ready, 1)

            hidden(1)
            hT(1)
            with dve.Fori(0, (FB - 1) // 2) as it:
                for j in range(2):
                    lo(21 + 3 * j, it)
                    lo(22 + 3 * j, it)
                    hidden(2 * it + (j + 2))
                    lo(23 + 3 * j, it)
                    hT(2 * it + (j + 2))

            def pT(n):
                dve.wait_ge(pT_act, n)
                dve.tensor_tensor(hT_lo[:, :], PS[:, 3, :], hT_hi[:, :].bitcast(F32), ALU.subtract).then_inc(pT_ready, 1)

            def embed(n, xr):
                for c in range(2):
                    dve.wait_ge(gate_act, 2 * n + c + 1)
                    g = pgate[:, c * 1024:(c + 1) * 1024]
                    step(dve.tensor_tensor(g, g, PS[:, 2 * c:2 * c + 2, :].rearrange("p b n -> p (b n)"), ALU.mult))
                    for t in range(T):
                        cols = slice(c * N, (c + 1) * N)
                        m = dve.tensor_tensor(x[:, t, cols], x[:, t, cols], g[:, t * N:(t + 1) * N], ALU.add)
                    m.then_inc(x_ready, 1)
                dve.wait_ge(x_ready, xr)

            norm_y(4, 2, in_psum, 2 * T)
            pT(1)
            los(51, 52)
            xT(4, None, 10)
            los(52, 55)
            embed(0, 3 * T)
            norm_x(5)
            xT(5, V_N10, 14)
            los(55, 62)
            for hd in range(HEADS):
                dve.wait_ge(fT_act, hd // 2 + 1)
                m = dve.tensor_scalar(fT[:, hd, :], fT[:, hd, :], lbc[:, 1, hd:hd + 1], lbc[:, 0, hd:hd + 1],
                                      ALU.mult, ALU.add)
            step(m)
            step(dve.tensor_scalar(kT, fT, -1.0, 1.0, ALU.mult, ALU.add))
            los(62, 64)
            dve.wait_ge(qT_act, 4)
            dve.sem_inc(qk_ready, 1)

            def meet(lv):
                at = attn.rearrange("p h t n -> p (h t) n")
                src = PS[:, 4:8, :].rearrange("p b (g n) -> p (b g) n", g=4)
                dve.wait_ge(at_done, lv + 1)
                if lv == 0:
                    step(dve.tensor_tensor(at, src, ident[:, :].unsqueeze(1).broadcast_to([P, 2 * HEADS, P]), ALU.mult))
                else:
                    step(dve.copy_predicated(at, seg[:, lv - 1, :].unsqueeze(1).broadcast_to([P, 2 * HEADS, P]), src))

            flat = "p h s -> p (h s)"
            qf, kf, ff = qT.rearrange(flat), kT.rearrange(flat), fT.rearrange(flat)
            totals = (junk[:, :].bitcast(F32), tot)
            prev = ff
            meet(0)
            step(dve.tensor_tensor(qT, qT, fT, ALU.mult))
            dve.sem_inc(qk_ready, 1)
            lo(64)
            for lv in range(1, 8):
                width, blocks = 2 ** (lv - 1), HEADS * SEQ // 2 ** (lv - 1)
                meet(lv)
                pv = prev.rearrange("p (m e) -> p m e", e=2)
                q4 = qf.rearrange("p (m e w) -> p m e w", e=2, w=width)
                k4 = kf.rearrange("p (m e w) -> p m e w", e=2, w=width)
                shape = [P, blocks // 2, width]
                dve.tensor_tensor(q4[:, :, 1, :], q4[:, :, 1, :], pv[:, :, 0].unsqueeze(2).broadcast_to(shape), ALU.mult)
                step(dve.tensor_tensor(k4[:, :, 0, :], k4[:, :, 0, :], pv[:, :, 1].unsqueeze(2).broadcast_to(shape),
                                       ALU.mult))
                dve.sem_inc(qk_ready, 1)
                lo(64 + lv)
                if lv < 7:
                    prev = totals[lv % 2][:, 0:blocks // 2]
                    step(dve.tensor_tensor(prev, pv[:, :, 0], pv[:, :, 1], ALU.mult))
            dve.wait_ge(at_done, 9)
            step(dve.tensor_copy(attx, PS[:, 4:6, :].rearrange("p b (h n) -> p (b h) n", h=4)))
            dve.sem_inc(qk_ready, 1)
            dve.wait_ge(g_evac, 2)
            dve.wait_ge(gain_full, 48)
            step(dve.tensor_tensor(gg[:, :, :], gg[:, :, :], gain[:, :].unsqueeze(1).broadcast_to([P, T, D]), ALU.mult))
            dve.sem_inc(gain_free, 1)
            los(72, 74)
            dve.wait_ge(o_sq, 1)
            OG = T * HEADS
            step(dve.tensor_reduce(rt[:, 0:OG], osq.rearrange("p (g n) -> p g n", n=HD), AXX, ALU.add))
            step(dve.tensor_scalar(nr[:, 0, 0:OG], rt[:, 0:OG], 1.0 / HD, EPS, ALU.mult, ALU.add))
            rsqrt(OG)
            step(dve.tensor_tensor(oo.rearrange("p t (h n) -> p (t h) n", n=HD),
                                   PS[:, 0:4, :].rearrange("p b (h n) -> p (b h) n", n=HD),
                                   nr[:, 1, 0:OG].unsqueeze(2).broadcast_to([P, OG, HD]), ALU.mult))
            dve.tensor_tensor(oo, oo, gg[:, :, :], ALU.mult).then_inc(o_ready, 1)
            xT(6, None, 18)
            los(74, 76)
            norm_y(6, 4, in_psum, 4 * T)
            norm_x(7)
            xT(7, V_N12, 22)
            chosen, ex, lm, lg = (rt[:, k * T * E:(k + 1) * T * E] for k in range(4))
            mx, rank = rt[:, 64:64 + T], rt[:, 80:80 + T * E]
            later = rt[:, 256:256 + E * E].rearrange("p (a b) -> p a b", a=E)
            pair = rt[:, 128:128 + E * E].rearrange("p (a b) -> p a b", a=E)
            same = rt[:, 192:192 + E * E].rearrange("p (a b) -> p a b", a=E)

            def by_row(v):
                return v.unsqueeze(2).broadcast_to([P, E, E])

            def by_col(v):
                return v.unsqueeze(1).broadcast_to([P, E, E])

            step(dve.tensor_tensor(later, by_col(iota_c[:, 0:E]), by_row(iota_c[:, 0:E]), ALU.is_lt))
            dve.wait_ge(lg_done, 1)
            tE = "p (t e) -> p t e"
            step(dve.tensor_tensor(lg.rearrange(tE, t=T), PS[:, 0, 0:T * E].rearrange(tE, t=T),
                                   br[:, :].unsqueeze(1).broadcast_to([P, T, E]), ALU.add))
            for t in range(T):
                l = lg[:, t * E:(t + 1) * E]
                step(dve.tensor_reduce(mx[:, t:t + 1], l, AXX, ALU.max))
                step(dve.tensor_scalar(lm[:, t * E:(t + 1) * E], l, mx[:, t:t + 1], None, ALU.subtract))
            dve.sem_inc(lg_max, 1)
            for t in range(T):
                l = lg[:, t * E:(t + 1) * E]
                step(dve.tensor_tensor(pair, by_col(l), by_row(l), ALU.is_gt))
                step(dve.tensor_tensor(same, by_col(l), by_row(l), ALU.is_equal))
                step(dve.tensor_tensor(same, same, later, ALU.mult))
                step(dve.tensor_tensor(pair, pair, same, ALU.add))
                step(dve.tensor_reduce(rank[:, t * E:(t + 1) * E], pair, AXX, ALU.add))
            step(dve.tensor_scalar(chosen, rank, 2.0, None, ALU.is_lt))
            dve.sem_inc(sel_cnt, 1)
            gates = rt[:, 320:320 + T * E]
            dve.wait_ge(lg_exp, 1)
            step(dve.tensor_tensor(ex, ex, chosen, ALU.mult))
            step(dve.tensor_reduce(mx, ex.rearrange(tE, t=T), AXX, ALU.add))
            step(dve.reciprocal(mx, mx))
            step(dve.tensor_tensor(gates.rearrange(tE, t=T), ex.rearrange(tE, t=T), mx.unsqueeze(2).broadcast_to([P, T, E]),
                                   ALU.mult))
            slot = rt[:, 96:96 + T * E]
            step(dve.memset(tab[:, 0, :, :], -1.0))
            step(dve.memset(tab[:, 1, :, :], 0.0))
            dve.wait_ge(cnt_done, 1)
            step(dve.scalar_tensor_tensor(out=slot, in0=PS[:, 1, 0:T * E], scalar=1.0, in1=chosen, op0=ALU.add, op1=ALU.mult))
            step(dve.tensor_scalar(slot, slot, -1.0, None, ALU.add))
            step(dve.tensor_copy(tab[:, 0, :, 1:E + 1], slot.rearrange(tE, t=T)))
            dve.tensor_copy(tab[:, 1, :, 1:E + 1], gates.rearrange(tE, t=T))

            def select(col):
                dve.tensor_copy(cur[:, 0, :].unsqueeze(2), tab[:, 0, :, bass.ds(col, 1)]).then_inc(cur_step, 1)

            def compare():
                for t in range(T):
                    m = dve.tensor_scalar(sel[:, t, :], iota_c[:, :], cur[:, 0, t:t + 1], None, ALU.is_equal)
                m.then_inc(sel_ready, 1)

            select(1)
            dve.wait_ge(cur_step, 1)
            compare()
            over, place, one, tmp = (rt[:, 336 + k * E:336 + (k + 1) * E] for k in range(4))
            head = rt[:, 368:368 + 2 + XTRA]
            step(dve.tensor_scalar(over, PS[:, 1, T * E:(T + 1) * E], float(P), None, ALU.is_gt))
            step(dve.tensor_tensor(pair, later, by_col(over), ALU.mult))
            step(dve.tensor_reduce(place, pair, AXX, ALU.add))
            step(dve.tensor_reduce(head[:, 0:1], over, AXX, ALU.add))
            step(dve.tensor_scalar(head[:, 0:1], head[:, 0:1], float(E - 1), None, ALU.add))
            step(dve.memset(head[:, 1:2], float(E - 1)))
            for j in range(XTRA):
                step(dve.scalar_tensor_tensor(out=one, in0=place, scalar=float(j), in1=over, op0=ALU.is_equal, op1=ALU.mult))
                step(dve.tensor_tensor(tmp, one, iota_c[:, 0:E], ALU.mult))
                step(dve.tensor_reduce(head[:, 2 + j:3 + j], tmp, AXX, ALU.add))
                for k, v in ((0, slot), (1, gates)):
                    p3 = pair[:, 0:T, :]
                    step(dve.tensor_tensor(p3, v.rearrange(tE, t=T), one.unsqueeze(1).broadcast_to([P, T, E]), ALU.mult))
                    m = dve.tensor_reduce(tab[:, k, :, E + j + 1:E + j + 2], p3, AXX, ALU.add)
                    step(m)
            step(dve.tensor_scalar(tab[:, 0, :, E + 1:E + 1 + XTRA], tab[:, 0, :, E + 1:E + 1 + XTRA], -float(P), None, ALU.add))
            dve.tensor_copy(itab[0:1, 0:2 + XTRA], head[0:1, :]).then_inc(table_ready, 1)
            dve.wait_ge(table_ready, 1)
            last_item = dve.value_load(itab[0:1, 0:1], min_val=E - 1, max_val=ITEMS - 1)
            for t in range(T):
                dve.memset(acc[:, t, :], 0.0).then_inc(acc_done, 1)
            dve.memset(selT[:, :, :].bitcast(F32), 0.0).then_inc(selT_ready, 1)

            def xg(n):
                dve.wait_ge(xg_act, n)
                for k in range(KT):
                    m = dve.scalar_tensor_tensor(out=xT_lo[:, k, 0:P], in0=PS[:, 6 + k // 4, (k % 4) * P:(k % 4 + 1) * P],
                                                 scalar=vcol[:, V_N12 + k:V_N12 + k + 1],
                                                 in1=xT_hi[:, k, 0:P].bitcast(F32), op0=ALU.mult, op1=ALU.subtract)
                m.then_inc(xg_ready, 1)

            def unit_hidden(n):
                dve.wait_ge(silu_done, n)
                dve.tensor_tensor(hh, sg, PS[:, 1, :], ALU.mult).then_inc(h_ready, 1)

            def output(n):
                dve.wait_ge(ye_act, n)
                dve.tensor_tensor(ye_lo, PS[:, 4:6, :].rearrange("p b (k c) -> p (b k) c", k=HK), ye_hi.bitcast(F32),
                                  ALU.subtract).then_inc(ye_ready, 1)

            def add_output(i, steps):
                dve.tensor_copy(cur[:, 1, :].unsqueeze(2), tab[:, 1, :, bass.ds(i, 1)]).then_inc(cur_step, 1)
                dve.wait_ge(cur_step, steps)
                dve.wait_ge(acc_done, i * T + T)
                for t in range(T):
                    dve.wait_ge(sc_done, i * T + (t + 1))
                    b = 4 - 4 * t
                    dve.scalar_tensor_tensor(out=acc[:, t, :], in0=PS[:, b:b + 2, :].rearrange("p b n -> p (b n)"),
                                             scalar=cur[:, 1, t:t + 1], in1=acc[:, t, :], op0=ALU.mult,
                                             op1=ALU.add).then_inc(acc_done, 1)

            def item(i, last):
                unit_hidden(i * EU + (FB + 1))
                lo(G_MOE + 7, i * EU)
                output(i + 1)
                hT(i * EU + (FB + 1))
                add_output(i, i * 2 + (2 if last else 3))
                lo(G_MOE + 8, i * EU)
                lo(G_MOE + 9, i * EU)

                def unit(u, end):
                    for q in (10, 11, 12):
                        lo(G_MOE + q, i * EU + u)
                    unit_hidden(i * EU + u + (FB + 2))
                    if end:
                        xg(i + 2)
                    lo(G_MOE + 13, i * EU + u)
                    lo(G_MOE + 14, i * EU + u)
                    hT(i * EU + u + (FB + 2))
                    lo(G_MOE + 15, i * EU + u)

                with dve.Fori(0, EU - 2) as u:
                    unit(u, False)
                unit(EU - 2, not last)
                for q in ((4,) if last else (4, 5, 6)):
                    lo(G_MOE + ITEM + q, i * EU)

            xg(1)
            for q in (4, 5, 6):
                lo(G_MOE + q)
            with dve.Fori(0, last_item) as i:
                dve.wait_ge(tsel_psum, i + 1)
                select(i + 2)
                dve.wait_ge(cur_step, i * 2 + 2)
                compare()
                item(i, False)
            item(last_item, True)
            output(last_item + 2)
            add_output(last_item + 1, last_item * 2 + 3)
            dve.wait_ge(acc_done, last_item * T + 3 * T)
            norm_y(8, 5, lambda c, t: acc[:, t, c * N:(c + 1) * N], 5 * T)
            pT(2)
            xT(8, None, 26)
            embed(1, 6 * T)


_INS = ["x", "p", "norm_g", "w_in_ab", "a_ln_g", "a_ln_b", "a_ws", "a_bs", "b_conv", "w_out_ab", "ffn_w_gu",
        "ffn_w_down", "w_in_c", "lb_param", "c_onorm_g", "w_out_c", "w_router", "b_router", "e_w_gu", "e_w_down",
        "ple_w_proj", "ple_w_gate"]


def granules(w, sides=1, columns=512):
    n, rows, m = w.shape
    w = w.reshape(n, 2, 4, P, sides, m // sides // columns, columns)
    w = w.transpose(0, 5, 1, 3, 2, 4, 6)
    return w.reshape(n, 2 * m // sides // columns, P, 4 * sides * columns)


def expert_granules(w):
    n, rows, m = w.shape
    w = w.reshape(n, 2, 4, P, 2, m // 1024, 512)
    w = w.transpose(0, 5, 4, 1, 3, 2, 6)
    return w.reshape(n, 4 * (m // 1024), P, GW)


def kernel(**inputs):
    import numpy as _np
    import concourse.bacc as _bacc
    from concourse import mybir as _mybir
    from concourse.bass_utils import run_bass_kernel_spmd as _run

    data = {name: _np.asarray(inputs[name]) for name in _INS}
    for name in ("w_in_ab", "w_out_ab", "w_in_c", "w_out_c", "ple_w_gate"):
        data[name] = granules(data[name]).reshape(-1, P, GW)
    data["ffn_w_gu"] = granules(data["ffn_w_gu"], 2, 256).reshape(-1, P, GW)
    data["e_w_gu"] = expert_granules(data["e_w_gu"][0])

    nc = _bacc.Bacc("TRN2", target_bir_lowering=False, num_devices=1)
    arrays, args = {}, []
    for name in _INS:
        a = _np.ascontiguousarray(data[name])
        arrays[f"in_{name}"] = a
        args.append(nc.dram_tensor(f"in_{name}", a.shape, _mybir.dt.from_np(a.dtype), kind="ExternalInput").ap())
    out = nc.dram_tensor("out_0", inputs["x"].shape, _mybir.dt.float32, kind="ExternalOutput").ap()
    trunk(nc, *args, out)
    r = _run(nc, [arrays], core_ids=[0])
    return r.results[0]["out_0"]
```

```python
from contextlib import ExitStack

import concourse.bass as bass
from concourse import mybir

ALU = mybir.AluOpType
ACT = mybir.ActivationFunctionType
AXX = mybir.AxisListType.X
F32 = mybir.dt.float32
F32R = mybir.dt.float32r
BF16 = mybir.dt.bfloat16
I32 = mybir.dt.int32
U8 = mybir.dt.uint8

P = 128
RING = 6
RAW = 3
GW = 2048
HW = GW // 2
N = 512
EPS = 1e-6

V_N00, V_N02, V_N10, V_N12, V_LB0, V_LB1, V_ABS, V_CONV, V_COLS = 0, 8, 16, 24, 32, 40, 48, 56, 68


def trunk(nc, x_d, pT_d, columns_d, norm_g, w_in_ab, a_ln_g, a_ln_b, wsT_d, w_out_ab, ffn_w_gu,
          ffn_w_down, w_in_c, c_onorm_g, w_out_c, w_router, b_router, e_w_gu, e_w_down,
          ple_w_proj, ple_w_gate, out_d):
    _, SEQ, D = x_d.shape
    T = SEQ // P
    KT = D // P
    HK = KT // 2
    FF = ffn_w_down.shape[1]
    FB = FF // 256
    E = e_w_down.shape[1]
    EF = e_w_down.shape[2]
    EU = EF // N
    ITEM = 6 * EU
    XTRA = T * P * 2 // (P + 1)
    ITEMS = E + XTRA
    HEADS, HD = 8, 128
    AH, AD = wsT_d.shape[1], a_ln_g.shape[1] // wsT_d.shape[1]
    AW = AH * AD

    G_AB = 0
    G_OUT = G_AB + 2 * 5
    G_FFN = G_OUT + 4
    G_PLE0 = G_FFN + 3 * FB
    G_INC = G_PLE0 + 5
    G_OUTC = G_INC + 16
    G_MOE = G_OUTC + 4
    assert G_MOE % RING == 0 and ITEM % RING == 0 and G_MOE % RAW == 0

    with ExitStack() as ctx:
        def sb(name, shape, dt=F32):
            return ctx.enter_context(nc.sbuf_tensor(name, shape, dt))

        def sem(name):
            return ctx.enter_context(nc.semaphore(name))

        raw = sb("raw", [P, RAW, GW])
        w_hi = sb("w_hi", [P, RING, GW], F32R)
        w_lo = sb("w_lo", [P, RING, GW], F32R)
        x = sb("x", [P, T, D])
        xn = sb("xn", [P, T, D])
        xT_hi = sb("xT_hi", [P, KT, SEQ], F32R)
        xT_lo = sb("xT_lo", [P, KT, SEQ], F32R)
        gain = sb("gain", [P, D])
        hT_hi = sb("hT_hi", [P, N], F32R)
        hT_lo = sb("hT_lo", [P, N], F32R)
        SC = sb("SC", [P, 9 * 1024 + 8])
        ident = sb("ident", [P, P])
        ones = sb("ones", [P, P])
        before = sb("before", [P, P])
        iota_c = sb("iota_c", [P, P])
        seg = sb("seg", [P, 7, P], U8)
        zeros = sb("zeros", [P, N], BF16)
        junk = sb("junk", [P, T * D], BF16)
        vcol = sb("vcol", [P, V_COLS])
        wr_hi = sb("wr_hi", [P, KT, E], F32R)
        wr_lo = sb("wr_lo", [P, KT, E], F32R)
        br = sb("br", [P, E])
        ss = sb("ss", [P, 8])
        nr = sb("nr", [P, 3, 16])
        lbc = sb("lbc", [P, 4, HEADS])
        rt = sb("rt", [P, 384])
        tab = sb("tab", [P, 2, T, ITEMS + 2])
        selT = sb("selT", [P, T, P], F32R)
        cur = sb("cur", [P, 2, T])
        itab = sb("itab", [1, 8], I32)
        PS = ctx.enter_context(nc.psum_tensor("PS", [P, 8, N], F32))

        def area(k, n=1):
            return SC[:, 1024 * k:1024 * (k + n)]

        wr = SC[:, 1024:1024 + KT * E].rearrange("p (k e) -> p k e", k=KT)
        av = area(0).rearrange("p (t n) -> p t n", t=T)
        xb = area(1).rearrange("p (t n) -> p t n", t=T)
        bg = area(2).rearrange("p (t n) -> p t n", t=T)
        wsT = area(4).rearrange("p (h i) -> p h i", h=AH)
        lng = SC[:, 5 * 1024:5 * 1024 + AW]
        lnb = SC[:, 5 * 1024 + AW:6 * 1024]
        vc = area(6).rearrange("p (t n) -> p t n", t=T)
        sq = area(7).rearrange("p (t n) -> p t n", t=T)
        cT = SC[:, 8 * 1024:8 * 1024 + HK * (SEQ + 2)].rearrange("p (k s) -> p k s", k=HK)
        conv = area(5).rearrange("p (k s) -> p k s", k=HK)
        ybT = area(7).rearrange("p (k s) -> p k s", k=HK)
        uu = xn[:, 0, :].rearrange("p (t n) -> p t n", t=T)
        ya = xn[:, 1, :].rearrange("p (t n) -> p t n", t=T)
        yg = (area(5).rearrange("p (c n) -> p c n", c=2), area(8).rearrange("p (c n) -> p c n", c=2))
        pT_split = ((hT_hi[:, :].rearrange("p (k c) -> p k c", c=P), hT_lo[:, :].rearrange("p (k c) -> p k c", c=P)),
                    (xT_hi[:, 0:HK, P:2 * P], xT_lo[:, 0:HK, P:2 * P]))
        sg = junk[:, :].bitcast(F32)[:, 0:N]
        hh = junk[:, :].bitcast(F32)[:, N:2 * N]
        pT_in = SC[:, 4 * 1024 + 512:5 * 1024]
        pgate = area(6, 2).rearrange("p (t c n) -> p t c n", t=T, c=2)
        qT = area(0, 2).rearrange("p (h s) -> p h s", h=HEADS)
        kT = area(2, 2).rearrange("p (h s) -> p h s", h=HEADS)
        attn = area(4, 2).rearrange("p (h t n) -> p h t n", h=HEADS, t=T)
        attx = area(6).rearrange("p (h n) -> p h n", h=HEADS)
        iv = area(7, 2).rearrange("p (t n) -> p t n", t=T)
        f_nat = area(4, 2).rearrange("p (t n) -> p t n", t=T)
        q_nat = area(7, 2).rearrange("p (t n) -> p t n", t=T)
        fT = xn[:, :, :].rearrange("p t n -> p (t n)").rearrange("p (h s) -> p h s", h=HEADS)
        tot = area(6)
        oo = area(0, 2).rearrange("p (t n) -> p t n", t=T)
        osq = area(2, 2)
        gg = xn
        acc = area(0, 2).rearrange("p (t n) -> p t n", t=T)
        ye_hi, ye_lo = xT_hi[:, :, P:2 * P], xT_lo[:, :, P:2 * P]
        sel = SC[:, 4 * 1024:4 * 1024 + T * P].rearrange("p (t c) -> p t c", t=T)

        x_full = [sem(f"x_full{t}") for t in range(T)]
        raw_full = [(sem(f"raw_full{i}a"), sem(f"raw_full{i}b")) for i in range(RING)]
        hi_done, lo_done, used = sem("hi_done"), sem("lo_done"), sem("used")
        gain_full, gain_free = sem("gain_full"), sem("gain_free")
        columns_full, router_full, ws_full, ln_full, p_full = (
            sem("columns_full"), sem("router_full"), sem("ws_full"), sem("ln_full"), sem("p_full"))
        consts, seg_in = sem("consts"), sem("seg_in")
        s_wsE, s_wr = sem("wsT_ready"), sem("wr_split")
        xT_psum, xT_act, xT_ready = sem("xT_psum"), sem("xT_act"), sem("xT_ready")
        xn_ready = sem("xn_ready")
        ss_ready, rstd_ready = sem("ss_ready"), sem("rstd_ready")
        y_squared, weighed = sem("y_squared"), sem("weighed")
        x_ready = sem("x_ready")
        v_gelu, vn_ready, xb_ready, c_ready, bg_ready, u_ready = (
            sem("v_gelu"), sem("vn_ready"), sem("xb_ready"), sem("c_ready"), sem("bg_ready"), sem("u_ready"))
        cT_psum, cT_ready, bgT_psum, yb_ready, gm_done, ya_ready = (
            sem("cT_psum"), sem("cT_ready"), sem("bgT_psum"), sem("yb_ready"), sem("gm_done"), sem("ya_ready"))
        yT_psum, ybT_ready, yb_act, ya_act, yaT_ready = sem("yT_psum"), sem("ybT_ready"), sem("yb_act"), sem("ya_act"), sem("yaT_ready")
        y_tile0 = sem("y_tile0")
        silu_done, h_ready, cur_step = sem("silu_done"), sem("h_ready"), sem("cur_step")
        hT_psum, hT_act, hT_ready = sem("hT_psum"), sem("hT_act"), sem("hT_ready")
        pT_act, pT_ready = sem("pT_act"), sem("pT_ready")
        gate_act = sem("gate_act")
        f_evac, q_evac, i_evac, g_evac = (
            sem("f_evac"), sem("q_evac"), sem("i_evac"), sem("g_evac"))
        fT_psum, fT_act, k_ready, qT_psum, qT_act = (
            sem("fT_psum"), sem("fT_act"), sem("k_ready"), sem("qT_psum"), sem("qT_act"))
        qk_ready, at_done = sem("qk_ready"), sem("at_done")
        o_done, o_sq, o_ready = sem("o_done"), sem("o_sq"), sem("o_ready")
        exp_ask, exp_done = sem("exp_ask"), sem("exp_done")
        lg_done, lg_max, lg_exp, sel_cnt, cnt_done, table_ready = (
            sem("lg_done"), sem("lg_max"), sem("lg_exp"), sem("sel_cnt"), sem("cnt_done"), sem("table_ready"))
        sel_ready, tsel_psum, selT_ready = sem("sel_ready"), sem("tsel_psum"), sem("selT_ready")
        gat_done, xg_act, xg_ready = sem("gathered"), sem("xg_act"), sem("xg_ready")
        ye_act, ye_ready, sc_done, acc_done = sem("ye_act"), sem("ye_ready"), sem("scattered"), sem("acc_done")
        dve_step, pool_step = sem("dve_step"), sem("pool_step")
        stored = sem("stored")

        more_raw = [area(k, 2) for k in (2, 5, 7)]

        def raw_slot(g):
            return g % RAW if g < G_MOE else g % RING

        def raw_part(g, s):
            k = raw_slot(g)
            return raw[:, k, s * HW:(s + 1) * HW] if k < RAW else more_raw[k - RAW][:, s * HW:(s + 1) * HW]

        def raw_count(g, turns):
            if g < G_MOE:
                return turns * (16 * RING // RAW) + 16 * (g // RAW + 1)
            return turns * 16 + 16 * ((g - G_MOE) // RING + 1 + (G_MOE // RAW if g % RING < RAW else 0))

        def tile_bank(t, final):
            return 4 - 3 * t if final else 4 + 2 * t

        embed_banks = ((0, 1, 2, 3), (0, 3, 6, 7))

        block = ctx.enter_context(nc.Block())

        @block.sync
        def _(sp):
            def load(g, src, turns=0, first=False):
                back = RAW if g < G_MOE or first else RING
                for s in range(2):
                    part = slice(s * HW, (s + 1) * HW)
                    if g >= RAW:
                        sp.wait_ge(lo_done, turns * 2 * RING + (2 * (g - back) + s + 1))
                    sp.dma_start(raw_part(g, s), src[:, part]).then_inc(raw_full[raw_slot(g)][s], 16)

            for t in range(T):
                sp.dma_start(x[:, t, :], x_d[0, t * P:(t + 1) * P, :]).then_inc(x_full[t], 16)
            sp.dma_start(vcol[:, :], columns_d).then_inc(columns_full, 16)
            g = G_AB
            for c in (1, 2, 3, 4, 0):
                for h in range(2):
                    load(g, w_in_ab[2 * c + h])
                    g += 1
            for h in (1, 0):
                for c in range(2):
                    load(g, w_out_ab[2 * c + h])
                    g += 1

            def load_gu(g, b, turns=0):
                for h in range(2):
                    load(g + h, ffn_w_gu[bass.ds(2 * b + h, 1), :, :].rearrange("g p n -> p (g n)"), turns)

            def load_down(g, b, turns=0):
                load(g, ffn_w_down[0][bass.ds(b * 256, 256), :].rearrange("(p r) n -> p (r n)", p=P), turns)

            load_gu(g, 0)
            with sp.Fori(0, (FB - 1) // 2) as it:
                for j in range(2):
                    load_gu(G_FFN + 2 + 3 * j, 2 * it + j + 1, it)
                    load_down(G_FFN + 4 + 3 * j, 2 * it + j, it)
            load_down(G_PLE0 - 1, FB - 1)

            def load_proj(layer, g, turns=0):
                load(g, ple_w_proj[layer].rearrange("(p r) n -> p (r n)", p=P), turns)

            def load_gate(layer, g, turns=0):
                for j in range(4):
                    load(g + j, ple_w_gate[4 * layer + j], turns)

            load_proj(0, G_PLE0)
            load_gate(0, G_PLE0 + 1)
            g = G_INC
            for c in (2, 3, 0, 1, 4, 5, 6, 7):
                for h in range(2):
                    load(g, w_in_c[2 * c + h])
                    g += 1
            for c in range(2):
                for h in range(2):
                    load(g, w_out_c[2 * c + h])
                    g += 1

            dn = e_w_down[0].rearrange("e f n -> e (f n)")

            def unit_gu(g, e, u, turns, first=False):
                for q in range(4):
                    if first and q == RAW:
                        sp.wait_ge(o_ready, T)
                    src = e_w_gu[bass.ds(e, 1), bass.ds(u * 4 + q, 1), :, :]
                    load(g + q, src.rearrange("e g p n -> p (e g n)"), turns, first and q < RAW)

            def unit_down(g, e, u, turns):
                for j in range(2):
                    src = dn[bass.ds(e, 1), bass.ds(u * (N * D) + j * 256 * D, 256 * D)]
                    load(g + j, src.rearrange("e (p m) -> p (e m)", p=P), turns)

            def load_item(i, e, following):
                with sp.Fori(0, EU - 1) as u:
                    unit_gu(G_MOE + 4, e, u + 1, i * EU + u)
                    unit_down(G_MOE + 8, e, u, i * EU + u)
                if following is not None:
                    unit_gu(G_MOE + ITEM - 2, following, 0, i * EU)
                    unit_down(G_MOE + ITEM + 2, e, EU - 1, i * EU)
                else:
                    load_proj(1, G_MOE + ITEM - 2, i * EU)
                    unit_down(G_MOE + ITEM - 1, e, EU - 1, i * EU)

            unit_gu(G_MOE, 0, 0, 0, True)
            sp.wait_ge(x_ready, 4 * T)
            with sp.Fori(0, E - 1) as i:
                load_item(i, i, i + 1)
            sp.wait_ge(table_ready, 1)
            last_item = sp.value_load(itab[0:1, 0:1], min_val=E - 1, max_val=ITEMS - 1)
            with sp.If(last_item > E - 1):
                with sp.Fori(E - 1, last_item) as i:
                    e = sp.value_load(itab[0:1, bass.ds(i - (E - 2), 1)], min_val=0, max_val=E - 1)
                    following = sp.value_load(itab[0:1, bass.ds(i - (E - 3), 1)], min_val=0, max_val=E - 1)
                    load_item(i, e, following)
            e = sp.value_load(itab[0:1, bass.ds(last_item - (E - 2), 1)], min_val=0, max_val=E - 1)
            load_item(last_item, e, None)
            load_gate(1, G_MOE + 1, last_item * EU + EU)
            for t in range(T):
                sp.wait_ge(x_ready, 5 * T + t + 1)
                sp.dma_start(out_d[0, t * P:(t + 1) * P, :], x[:, t, :]).then_inc(stored, 16)
            sp.wait_ge(stored, 16 * T)

        @block.gpsimd
        def _(pool):
            count = [0]

            def step(ins):
                count[0] += 1
                ins.then_inc(pool_step, 1)
                pool.wait_ge(pool_step, count[0])

            step(pool.memset(ident[:, :], 0.0))
            step(pool.affine_select(out=ident[:, :], in_=ident[:, :], compare_op=ALU.not_equal, fill=1.0, base=0,
                                    pattern=[[-1, P]], channel_multiplier=1))
            step(pool.memset(ones[:, :], 1.0))
            step(pool.affine_select(out=before[:, :], in_=ones[:, :], compare_op=ALU.is_gt, fill=0.0, base=0,
                                    pattern=[[1, P]], channel_multiplier=-1))
            pool.memset(zeros[:, :], 0.0).then_inc(consts, 1)
            pool.iota(iota_c[:, :].bitcast(I32), pattern=[[1, P]], base=0, channel_multiplier=0).then_inc(seg_in, 1)
            pool.iota(rt[:, 0:P].bitcast(I32), pattern=[[0, P]], base=0, channel_multiplier=1).then_inc(seg_in, 1)
            pool.wait_ge(lo_done, 2)
            pool.dma_start(wr[:, :, :], w_router).then_inc(router_full, 16)
            pool.dma_start(br[:, :], b_router[0:1, :].broadcast_to([P, E])).then_inc(router_full, 16)
            pool.dma_start(wsT, wsT_d).then_inc(ws_full, 16)
            pool.dma_start(lng, a_ln_g[0:1, :].broadcast_to([P, AW])).then_inc(ln_full, 16)
            pool.dma_start(lnb, a_ln_b[0:1, :].broadcast_to([P, AW])).then_inc(ln_full, 16)
            gains = [norm_g[0, 1:2], norm_g[0, 3:4], c_onorm_g[0:1], norm_g[1, 1:2], norm_g[1, 3:4]]
            for n, v in enumerate(gains):
                if n:
                    pool.wait_ge(gain_free, n)
                pool.dma_start(gain[:, :], v.broadcast_to([P, D])).then_inc(gain_full, 16)
                if n == 1:
                    pool.dma_start(pT_in, pT_d[0]).then_inc(p_full, 16)
                if n == 4:
                    pool.dma_start(pT_in, pT_d[1]).then_inc(p_full, 16)

            pool.memset(selT[:, :, :].bitcast(F32), 0.0).then_inc(selT_ready, 1)
            pool.wait_ge(x_ready, 4 * T)
            for t in range(T):
                pool.memset(acc[:, t, :], 0.0).then_inc(acc_done, 1)

        @block.tensor
        def _(pe):
            def split_matmul(out, a_hi, a_lo, b_hi, b_lo, start, stop):
                pe.matmul(out, a_hi, b_hi, start=start, stop=False, skip_group_check=True)
                pe.matmul(out, a_lo, b_hi, start=False, stop=False, skip_group_check=True)
                return pe.matmul(out, a_hi, b_lo, start=False, stop=stop, skip_group_check=True)

            banks_of = ((0, 1), (2, 3), (4, 5), (6, 7), (4, 6), (5, 7), (4, 1), (5, 2))
            OUT, OUT_FINAL = 4, 6

            def part(g, s, t, pair, h, first, last):
                for j in (2 * s, 2 * s + 1):
                    r = slice(j * N, (j + 1) * N)
                    tok = slice(t * P, (t + 1) * P)
                    m = split_matmul(PS[:, banks_of[pair][t], :], xT_hi[:, HK * h + j, tok], xT_lo[:, HK * h + j, tok],
                                     w_hi[:, g % RING, r], w_lo[:, g % RING, r],
                                     first and j == 0, last and j == HK - 1)
                return m

            def half_granule(g, pair, h, first, last, turns=0):
                for s in range(2):
                    pe.wait_ge(lo_done, turns * 2 * RING + (2 * g + s + 1))
                    for t in range(T):
                        m = part(g, s, t, pair, h, first, last)
                    m.then_inc(used, 1)

            def tile_by_tile(granules, ready, turn=(), closing=False, turns=0):
                for t in range(T):
                    if ready is not None:
                        pe.wait_ge(xT_ready, ready + t + 1)
                    for g, pair, h, first, last in granules:
                        if g == granules[-1][0] and t < len(turn):
                            turn[t]()
                        for s in range(2):
                            if t == 0:
                                pe.wait_ge(lo_done, turns * 2 * RING + (2 * g + s + 1))
                            m = part(g, s, t, pair, h, first, last)
                            if t == T - 1:
                                m.then_inc(used, 1)
                    if t == 0 and closing:
                        m.then_inc(y_tile0, 1)

            def turn_x(src, t, final=False):
                for b in range(2):
                    for j in range(HK):
                        kt = HK * b + j
                        m = pe.transpose(PS[:, tile_bank(t, final) + b, j * P:(j + 1) * P], src[:, t, kt * P:(kt + 1) * P],
                                         ident[:, :])
                    m.then_inc(xT_psum, 1)

            def turn_xn(n, t):
                pe.wait_ge(xn_ready, T * n + t + 1)
                turn_x(xn, t)

            pe.wait_ge(consts, 1)
            turn_xn(0, 0)
            tile_by_tile([(G_AB + k, k // 2, k % 2, k % 2 == 0, k % 2 == 1) for k in range(4)], 0,
                         [lambda: turn_xn(0, 1)])
            for n in range(2, 4):
                for h in range(2):
                    half_granule(G_AB + 2 * n + h, n, h, h == 0, h == 1)
            pe.wait_ge(c_ready, 1)
            for k in range(HK):
                for t in range(T):
                    c = (k % 2) * SEQ + t * P
                    m = pe.transpose(PS[:, 2 + k // 2, c:c + P], xb[:, t, k * P:(k + 1) * P], ident[:, :])
            m.then_inc(cT_psum, 1)
            pe.wait_ge(v_gelu, 1)
            for h in range(2):
                half_granule(G_AB + 8 + h, 0, h, h == 0, h == 1)
            pe.wait_ge(bg_ready, 1)
            for k in range(HK):
                for t in range(T):
                    c = (k % 2) * SEQ + t * P
                    m = pe.transpose(PS[:, 4 + k // 2, c:c + P], bg[:, t, k * P:(k + 1) * P], ident[:, :])
            m.then_inc(bgT_psum, 1)
            pe.wait_ge(s_wsE, 1)
            pe.wait_ge(vn_ready, 1)
            pe.wait_ge(cT_ready, 1)
            for h in range(AH):
                o = PS[:, 2 + h // 4, (h % 4) * P:(h % 4 + 1) * P].rearrange("p (t d) -> p t d", t=T)
                m = pe.matmul(o, wsT[:, h, :], vc[:, :, h * AD:(h + 1) * AD], start=True, stop=True,
                              skip_group_check=True)
            m.then_inc(gm_done, 1)
            pe.wait_ge(yb_ready, 1)
            half_granule(G_OUT, OUT, 1, True, False)
            pe.wait_ge(ya_ready, 1)
            for k in range(HK):
                for t in range(T):
                    c = (k % 2) * SEQ + t * P
                    m = pe.transpose(PS[:, k // 2, c:c + P], ya[:, t, k * P:(k + 1) * P], ident[:, :])
            m.then_inc(yT_psum, 1)
            half_granule(G_OUT + 1, OUT + 1, 1, True, False)
            pe.wait_ge(yaT_ready, 1)
            tile_by_tile([(G_OUT + 2 + c, OUT + c, 0, False, True) for c in range(2)], None, closing=True)

            def clear(banks):
                for b in banks:
                    pe.matmul(PS[:, b, :], zeros[:, 0:P], zeros[:, :], start=True, stop=False, skip_group_check=True)

            def ffn_gu(g, turns=0):
                half_granule(g, 0, 0, True, False, turns)
                half_granule(g + 1, 0, 1, False, True, turns)

            def ffn_turn(n):
                pe.wait_ge(h_ready, n)
                hv = hh.rearrange("p (t q r) -> p t r q", t=T, r=2)
                for r in range(2):
                    for t in range(T):
                        c = (r * T + t) * P
                        m = pe.transpose(PS[:, 2, c:c + P], hv[:, t, r, :], ident[:, :])
                m.then_inc(hT_psum, 1)

            def ffn_down(g, n, turns=0):
                pe.wait_ge(hT_ready, n)
                for r in range(2):
                    pe.wait_ge(lo_done, turns * 2 * RING + (2 * g + r + 1))
                    for c in range(2):
                        for t in range(T):
                            a = slice((r * T + t) * P, (r * T + t + 1) * P)
                            w = slice(r * D + c * N, r * D + (c + 1) * N)
                            m = split_matmul(PS[:, 4 + 2 * t + c, :], hT_hi[:, a], hT_lo[:, a],
                                             w_hi[:, g % RING, w], w_lo[:, g % RING, w], False, False)
                    m.then_inc(used, 1)

            def ffn_last(g, n):
                pe.wait_ge(hT_ready, n)
                pe.wait_ge(lo_done, 2 * g + 2)
                for t in range(T):
                    for r in range(2):
                        for c in range(2):
                            a = slice((r * T + t) * P, (r * T + t + 1) * P)
                            w = slice(r * D + c * N, r * D + (c + 1) * N)
                            m = split_matmul(PS[:, 4 + 2 * t + c, :], hT_hi[:, a], hT_lo[:, a],
                                             w_hi[:, g % RING, w], w_lo[:, g % RING, w], False, r == 1)
                        if t == T - 1:
                            m.then_inc(used, 1)
                    if t == 0:
                        m.then_inc(y_tile0, 1)

            turn_xn(1, 0)
            tile_by_tile([(G_FFN, 0, 0, True, False), (G_FFN + 1, 0, 1, False, True)], T, [lambda: turn_xn(1, 1)])
            clear(range(4, 8))
            ffn_turn(1)
            with pe.Fori(0, (FB - 1) // 2) as it:
                for j in range(2):
                    ffn_gu(G_FFN + 2 + 3 * j, it)
                    ffn_down(G_FFN + 4 + 3 * j, 2 * it + (j + 1), it)
                    ffn_turn(2 * it + (j + 2))
            ffn_last(G_PLE0 - 1, FB)

            def ple_proj(layer, g, turns=0):
                pe.wait_ge(pT_ready, layer + 1)
                for kk in range(2):
                    pe.wait_ge(lo_done, turns * 2 * RING + (2 * g + kk + 1))
                    for c in range(2):
                        for t in range(T):
                            a_hi, a_lo = (v[:, kk * T + t, :] for v in pT_split[layer])
                            w = slice(kk * D + c * N, kk * D + (c + 1) * N)
                            m = split_matmul(PS[:, embed_banks[layer][2 * c + t], :], a_hi, a_lo,
                                             w_hi[:, g % RING, w], w_lo[:, g % RING, w], kk == 0, kk == 1)
                    m.then_inc(used, 1)

            def ple_gate(g, turned, xt, following, final, turns=0):
                def turn(t):
                    pe.wait_ge(x_ready, turned + t + 1)
                    turn_x(x, t, final)

                turn(0)
                pair = OUT_FINAL if final else OUT
                tile_by_tile([(g + j, pair + j // 2, j % 2, j % 2 == 0, j % 2 == 1) for j in range(4)],
                             xt, [lambda: turn(1)] + following, True, turns)

            ple_proj(0, G_PLE0)
            ple_gate(G_PLE0 + 1, T, 2 * T, [lambda: turn_xn(2, 0)], False)


            def proj(n, evac=None):
                c, h = n // 2, n % 2
                if evac:
                    pe.wait_ge(*evac)
                half_granule(G_INC + n, c % 2, h, h == 0, h == 1)

            def turn_heads(src, signal):
                for hd in range(HEADS):
                    for t in range(T):
                        c = (hd % 2) * SEQ + t * P
                        m = pe.transpose(PS[:, 4 + hd // 2, c:c + P], src[:, t, hd * P:(hd + 1) * P], ident[:, :])
                    if hd % 2:
                        m.then_inc(signal, 1)

            def level(n):
                pe.wait_ge(qk_ready, n + 1)
                for hd in range(HEADS):
                    for t in range(T):
                        tok = slice(t * P, (t + 1) * P)
                        c = (hd % 2) * SEQ + t * P
                        m = pe.matmul(PS[:, 4 + hd // 2, c:c + P], kT[:, hd, tok], qT[:, hd, tok],
                                      start=True, stop=True, skip_group_check=True)
                m.then_inc(at_done, 1)

            tile_by_tile([(G_INC + n, n // 2, n % 2, n % 2 == 0, n % 2 == 1) for n in range(4)], 3 * T,
                         [lambda: turn_xn(2, 1)])
            proj(4, (f_evac, 1))
            proj(5)
            pe.wait_ge(f_evac, 2)
            turn_heads(f_nat, fT_psum)
            proj(6)
            proj(7)
            pe.wait_ge(q_evac, 2)
            pe.wait_ge(fT_act, 4)
            turn_heads(q_nat, qT_psum)
            proj(8)
            level(0)
            proj(9)
            level(1)
            proj(10)
            level(2)
            proj(11)
            level(3)
            proj(12, (i_evac, 1))
            level(4)
            proj(13)
            level(5)
            proj(14, (i_evac, 2))
            level(6)
            proj(15)
            level(7)
            pe.wait_ge(qk_ready, 9)
            for hd in range(HEADS):
                m = pe.matmul(PS[:, 4 + hd // 4, (hd % 4) * P:(hd % 4 + 1) * P], kT[:, hd, 0:P], qT[:, hd, P:SEQ],
                              start=True, stop=True, skip_group_check=True)
            m.then_inc(at_done, 1)
            pe.wait_ge(g_evac, 2)
            pe.wait_ge(qk_ready, 10)
            for t in range(T):
                for hd in range(HEADS):
                    o = PS[:, 2 * t + hd // 4, (hd % 4) * P:(hd % 4 + 1) * P]
                    m = pe.matmul(o, attn[:, hd, t, :], iv[:, t, hd * HD:(hd + 1) * HD], start=True, stop=(t == 0),
                                  skip_group_check=True)
                    if t == 1:
                        m = pe.matmul(o, attx[:, hd, :], iv[:, 0, hd * HD:(hd + 1) * HD], start=False, stop=True,
                                      skip_group_check=True)
                m.then_inc(o_done, 1)
            def turn_o(t):
                pe.wait_ge(o_ready, t + 1)
                turn_x(oo, t)

            turn_o(0)
            tile_by_tile([(G_OUTC + n, OUT + n // 2, n % 2, n % 2 == 0, n % 2 == 1) for n in range(4)], 4 * T,
                         [lambda: turn_o(1), lambda: turn_xn(3, 0)], True)

            pe.wait_ge(s_wr, 2)
            for t in range(T):
                if t:
                    turn_xn(3, t)
                pe.wait_ge(xT_ready, 5 * T + t + 1)
                for k in range(KT):
                    tok = slice(t * P, (t + 1) * P)
                    m = split_matmul(PS[:, 0, t * E:(t + 1) * E], xT_hi[:, k, tok], xT_lo[:, k, tok],
                                     wr_hi[:, k, :], wr_lo[:, k, :], k == 0, k == KT - 1)
            m.then_inc(lg_done, 1)
            pe.wait_ge(sel_cnt, 1)
            chosen = rt[:, 0:2 * E].rearrange("p (t e) -> p t e", t=T)
            pe.matmul(PS[:, 1, 0:E], before[:, :], chosen[:, 0, :], start=True, stop=True, skip_group_check=True)
            pe.matmul(PS[:, 1, E:2 * E], before[:, :], chosen[:, 1, :], start=True, stop=False, skip_group_check=True)
            pe.matmul(PS[:, 1, E:2 * E], ones[:, :], chosen[:, 0, :], start=False, stop=True, skip_group_check=True)
            pe.matmul(PS[:, 1, 2 * E:3 * E], ones[:, :], chosen[:, 0, :], start=True, stop=False, skip_group_check=True)
            pe.matmul(PS[:, 1, 2 * E:3 * E], ones[:, :], chosen[:, 1, :], start=False, stop=True,
                      skip_group_check=True).then_inc(cnt_done, 1)

            def gather(half):
                for k in range(HK * half, HK * (half + 1)):
                    for t in range(T):
                        m = pe.matmul(PS[:, 6 + half, (k % 4) * P:(k % 4 + 1) * P], xn[:, t, k * P:(k + 1) * P],
                                      sel[:, t, :], start=(t == 0), stop=(t == T - 1), skip_group_check=True)
                m.then_inc(gat_done, 1)

            def turn_sel():
                for t in range(T):
                    m = pe.transpose(PS[:, 3, t * P:(t + 1) * P], sel[:, t, :], ident[:, :])
                m.then_inc(tsel_psum, 1)

            def scatter(base=0):
                for t in range(T):
                    for c in range(2):
                        o, q = PS[:, (4, base)[t] + c, :], slice(HK * c, HK * (c + 1))
                        pe.matmul(o, selT[:, t, :], ye_hi[:, q, :], start=True, stop=False, skip_group_check=True)
                        m = pe.matmul(o, selT[:, t, :], ye_lo[:, q, :], start=False, stop=True, skip_group_check=True)
                    m.then_inc(sc_done, 1)

            def unit_gu(g, turns, tokens=None):
                for side in range(2):
                    for h in range(2):
                        if tokens is not None and side == 0:
                            pe.wait_ge(xg_ready, tokens + (h - 1))
                        for j in range(HK):
                            if j % 2 == 0:
                                pe.wait_ge(lo_done, turns * 2 * RING + (2 * (g + 2 * side + h) + j // 2 + 1))
                            r = slice(j * N, (j + 1) * N)
                            s = (g + 2 * side + h) % RING
                            m = split_matmul(PS[:, side, :], xT_hi[:, HK * h + j, 0:P], xT_lo[:, HK * h + j, 0:P],
                                             w_hi[:, s, r], w_lo[:, s, r], h == 0 and j == 0, h == 1 and j == HK - 1)
                            if j % 2:
                                m.then_inc(used, 1)

            def unit_turn(n):
                pe.wait_ge(h_ready, n)
                hv = hh.rearrange("p (j q r) -> p j r q", j=2, r=2)
                for j in range(2):
                    for r in range(2):
                        c = (j * 2 + r) * P
                        m = pe.transpose(PS[:, 2, c:c + P], hv[:, j, r, :], ident[:, :])
                m.then_inc(hT_psum, 1)

            def unit_down(g, n, last, turns):
                pe.wait_ge(hT_ready, n)
                for j in range(2):
                    for r in range(2):
                        pe.wait_ge(lo_done, turns * 2 * RING + (2 * (g + j) + r + 1))
                        for c in range(2):
                            a = slice((j * 2 + r) * P, (j * 2 + r + 1) * P)
                            w = slice(r * D + c * N, r * D + (c + 1) * N)
                            s = (g + j) % RING
                            m = split_matmul(PS[:, 4 + c, :], hT_hi[:, a], hT_lo[:, a],
                                             w_hi[:, s, w], w_lo[:, s, w], False, last and j == 1 and r == 1)
                        m.then_inc(used, 1)

            def item(i, last):
                unit_turn(i * EU + (FB + 1))
                if not last:
                    pe.wait_ge(sel_ready, i + 2)
                    gather(0)
                pe.wait_ge(ye_ready, i + 1)
                pe.wait_ge(selT_ready, i + 1)
                scatter()
                if not last:
                    gather(1)
                pe.wait_ge(acc_done, i * T + (T + 1))
                clear((4,))
                pe.wait_ge(acc_done, i * T + 2 * T)
                clear((5,))
                with pe.Fori(0, EU - 1) as u:
                    unit_gu(G_MOE + 4, i * EU + u)
                    unit_down(G_MOE + 8, i * EU + u + (FB + 1), False, i * EU + u)
                    unit_turn(i * EU + u + (FB + 2))
                if last:
                    pe.wait_ge(selT_ready, i + 2)
                    ple_proj(1, G_MOE + ITEM - 2, i * EU)
                    unit_down(G_MOE + ITEM - 1, i * EU + (FB + EU), True, i * EU)
                else:
                    pe.wait_ge(selT_ready, i + 2)
                    turn_sel()
                    unit_gu(G_MOE + ITEM - 2, i * EU, i * 2 + 4)
                    unit_down(G_MOE + ITEM + 2, i * EU + (FB + EU), True, i * EU)

            pe.wait_ge(sel_ready, 1)
            gather(0)
            gather(1)
            turn_sel()
            pe.wait_ge(table_ready, 1)
            last_item = pe.value_load(itab[0:1, 0:1], min_val=E - 1, max_val=ITEMS - 1)
            unit_gu(G_MOE, 0, 2)
            with pe.Fori(0, last_item) as i:
                item(i, False)
            item(last_item, True)
            pe.wait_ge(ye_ready, last_item + 2)
            scatter(1)
            ple_gate(G_MOE + 1, 4 * T, 6 * T, [], True, last_item * EU + EU)

        @block.scalar
        def _(act):
            def hi(g, turns=0):
                for s in range(2):
                    part = slice(s * HW, (s + 1) * HW)
                    if g >= RING:
                        act.wait_ge(used, turns * 2 * RING + (2 * (g - RING) + s + 1))
                    act.wait_ge(raw_full[raw_slot(g)][s], raw_count(g, turns))
                    act.activation(w_hi[:, g % RING, part], raw_part(g, s), ACT.Copy).then_inc(hi_done, 1)

            def product(g, turns=0):
                act.wait_ge(used, turns * 2 * RING + 2 * g)

            def his(a, b):
                for g in range(a, b):
                    hi(g)

            def xT(t, n, v, final=False):
                for b in range(2):
                    act.wait_ge(xT_psum, 2 * T * n + 2 * t + b + 1)
                    for j in range(HK):
                        kt, src = HK * b + j, PS[:, tile_bank(t, final) + b, j * P:(j + 1) * P]
                        m = act.activation(xT_hi[:, kt, t * P:(t + 1) * P], src, ACT.Copy,
                                           scale=1.0 if v is None else vcol[:, v + kt:v + kt + 1])
                    m.then_inc(xT_act, 1)

            def square_y(k, t, src):
                for c in range(2):
                    if c == 1:
                        act.wait_ge(weighed, 2 * T * k + 2 * t + 1)
                    act.activation(junk[:, t * D + c * N:t * D + (c + 1) * N], src(t)[:, c, :], ACT.Square,
                                   accum_out=ss[:, 2 * c + t:2 * c + t + 1]).then_inc(y_squared, 1)

            def square_x(t):
                act.activation(junk[:, t * D:(t + 1) * D], x[:, t, :], ACT.Square,
                               accum_out=ss[:, 4 + t:5 + t]).then_inc(ss_ready, 1)

            def scale_x(t, n):
                act.wait_ge(rstd_ready, T * n + t + 1)
                act.activation(xn[:, t, :], x[:, t, :], ACT.Copy, scale=nr[:, 1, t:t + 1]).then_inc(xn_ready, 1)

            in_psum = lambda t: PS[:, 4 + 2 * t:6 + 2 * t, :]

            def norms(k, y_n, g, x_n, n, v, turned, between=lambda: None):
                for t in range(T):
                    if t == 0:
                        act.wait_ge(y_tile0, y_n)
                    else:
                        between()
                        product(g)
                    square_y(k, t, in_psum)
                    act.wait_ge(x_ready, x_n + t + 1)
                    square_x(t)
                    scale_x(t, n)
                    xT(t, turned, v)

            for t in range(T):
                act.wait_ge(x_full[t], 16)
                square_x(t)
            scale_x(0, 0)
            hi(0)
            act.wait_ge(columns_full, 16)
            xT(0, 0, V_N00)
            scale_x(1, 0)
            his(1, 3)
            hi(3)
            xT(1, 0, V_N00)
            act.wait_ge(router_full, 32)
            act.activation(wr_hi[:, :, :], wr[:, :, :], ACT.Copy).then_inc(s_wr, 1)
            act.wait_ge(exp_ask, 1)
            act.activation(lbc[:, 0:2, :], lbc[:, 2:4, :], ACT.Exp).then_inc(exp_done, 1)
            his(4, 7)
            product(G_AB + 2)
            act.activation(av, PS[:, 0:2, :], ACT.Gelu_apprx_tanh).then_inc(v_gelu, 1)
            his(7, 9)
            product(G_AB + 4)
            act.activation(xb, PS[:, 2:4, :], ACT.Copy).then_inc(xb_ready, 1)
            his(9, 12)
            product(G_AB + 8)
            act.activation(bg, PS[:, 6:8, :], ACT.Copy).then_inc(bg_ready, 1)
            act.wait_ge(cT_psum, 1)
            act.activation(cT[:, :, 2:SEQ + 2], PS[:, 2:4, :].rearrange("p b (k s) -> p (b k) s", k=2),
                           ACT.Copy).then_inc(cT_ready, 1)
            his(12, 14)
            product(G_AB + 10)
            act.activation(uu, PS[:, 0:2, :], ACT.Gelu_apprx_tanh).then_inc(u_ready, 1)
            act.wait_ge(ybT_ready, 1)
            act.activation(xT_hi[:, HK:KT, :], ybT, ACT.Copy).then_inc(yb_act, 1)
            act.wait_ge(yT_psum, 1)
            act.activation(xT_hi[:, 0:HK, :], PS[:, 0:2, :].rearrange("p b (k s) -> p (b k) s", k=2),
                           ACT.Copy).then_inc(ya_act, 1)
            his(14, 18)
            norms(0, 1, G_FFN, 0, 1, V_N02, 1)
            his(18, 20)

            def silu():
                act.activation(sg.rearrange("p (t n) -> p t n", t=T), PS[:, 0:2, 0:256], ACT.Silu).then_inc(silu_done, 1)

            def hT(n):
                act.wait_ge(hT_psum, n)
                act.activation(hT_hi[:, :], PS[:, 2, :], ACT.Copy).then_inc(hT_act, 1)

            hi(20)
            product(G_FFN + 2)
            silu()
            hT(1)
            with act.Fori(0, (FB - 1) // 2) as it:
                for j in range(2):
                    hi(21 + 3 * j, it)
                    hi(22 + 3 * j, it)
                    product(G_FFN + 4 + 3 * j, it)
                    silu()
                    hi(23 + 3 * j, it)
                    hT(2 * it + (j + 2))
            act.wait_ge(y_tile0, 2)
            square_y(1, 0, in_psum)
            product(G_PLE0)
            square_y(1, 1, in_psum)

            def pT(n):
                act.wait_ge(p_full, 16 * n)
                act.activation(pT_split[n - 1][0], pT_in.rearrange("p (k c) -> p k c", c=P), ACT.Copy).then_inc(pT_act, 1)

            def gate(t, c, final=False):
                act.activation(pgate[:, t, c, :], PS[:, tile_bank(t, final) + c, :], ACT.Sigmoid).then_inc(gate_act, 1)

            pT(1)
            xT(0, 2, None)
            his(51, 52)
            xT(1, 2, None)
            his(52, 54)
            act.wait_ge(y_tile0, 3)
            for t in range(T):
                if t:
                    his(54, 56)
                    product(G_INC)
                for c in range(2):
                    gate(t, c)
                act.wait_ge(x_ready, 2 * T + t + 1)
                square_x(t)
                scale_x(t, 2)
                xT(t, 3, V_N10)
            his(56, 59)
            product(G_INC + 2)
            act.activation(f_nat[:, :, 0:N], PS[:, 0:2, :], ACT.Copy).then_inc(f_evac, 1)
            his(59, 61)
            product(G_INC + 4)
            act.activation(f_nat[:, :, N:D], PS[:, 2:4, :], ACT.Copy).then_inc(f_evac, 1)
            his(61, 62)
            product(G_INC + 6)
            act.activation(q_nat[:, :, 0:N], PS[:, 0:2, :], ACT.Copy).then_inc(q_evac, 1)
            for b in range(4):
                act.wait_ge(fT_psum, b + 1)
                act.activation(fT[:, 2 * b:2 * b + 2, :], PS[:, 4 + b, :].rearrange("p (h s) -> p h s", h=2),
                               ACT.Sigmoid).then_inc(fT_act, 1)
            his(62, 64)
            product(G_INC + 8)
            act.activation(q_nat[:, :, N:D], PS[:, 2:4, :], ACT.Copy).then_inc(q_evac, 1)
            for b in range(4):
                act.wait_ge(qT_psum, b + 1)
                act.activation(qT[:, 2 * b:2 * b + 2, :], PS[:, 4 + b, :].rearrange("p (h s) -> p h s", h=2),
                               ACT.Silu).then_inc(qT_act, 1)
            his(64, 66)
            product(G_INC + 10)
            act.activation(iv[:, :, 0:N], PS[:, 0:2, :], ACT.Copy).then_inc(i_evac, 1)
            his(66, 68)
            product(G_INC + 12)
            act.activation(iv[:, :, N:D], PS[:, 2:4, :], ACT.Copy).then_inc(i_evac, 1)
            his(68, 70)
            product(G_INC + 14)
            act.wait_ge(qk_ready, 4)
            act.activation(gg[:, :, 0:N], PS[:, 0:2, :], ACT.Silu).then_inc(g_evac, 1)
            his(70, 72)
            product(G_INC + 16)
            act.activation(gg[:, :, N:D], PS[:, 2:4, :], ACT.Silu).then_inc(g_evac, 1)
            his(72, 74)
            for t in range(T):
                act.wait_ge(o_done, t + 1)
                act.activation(osq[:, t * D:(t + 1) * D], PS[:, 2 * t:2 * t + 2, :].rearrange("p b n -> p (b n)"),
                               ACT.Square).then_inc(o_sq, 1)
                xT(t, 4, None)
            norms(2, 4, G_MOE, 3 * T, 3, V_N12, 5, lambda: his(74, 76))
            his(76, 78)
            act.wait_ge(lg_max, 1)
            act.activation(rt[:, 2 * E:4 * E], rt[:, 4 * E:6 * E], ACT.Exp).then_inc(lg_exp, 1)

            def xg(n):
                for b in range(2):
                    act.wait_ge(gat_done, n * 2 + (b - 1))
                    for j in range(HK):
                        k = HK * b + j
                        m = act.activation(xT_hi[:, k, 0:P], PS[:, 6 + b, j * P:(j + 1) * P], ACT.Copy,
                                           scale=vcol[:, V_N12 + k:V_N12 + k + 1])
                    m.then_inc(xg_act, 1)

            def unit_silu():
                act.activation(sg, PS[:, 0, :], ACT.Silu).then_inc(silu_done, 1)

            xg(1)
            act.wait_ge(table_ready, 1)
            last_item = act.value_load(itab[0:1, 0:1], min_val=E - 1, max_val=ITEMS - 1)

            def output(g, turns):
                product(g, turns)
                act.activation(ye_hi, PS[:, 4:6, :].rearrange("p b (k c) -> p (b k) c", k=HK), ACT.Copy).then_inc(ye_act, 1)

            def item(i, last):
                product(G_MOE + 2, i * EU)
                unit_silu()
                hi(G_MOE + 7, i * EU)
                output(G_MOE + 4, i * EU)
                hT(i * EU + (FB + 1))
                hi(G_MOE + 8, i * EU)
                hi(G_MOE + 9, i * EU)
                act.wait_ge(tsel_psum, i + 1)
                act.wait_ge(sc_done, i * T + T)
                act.activation(selT[:, :, :], PS[:, 3, 0:T * P].rearrange("p (t c) -> p t c", t=T),
                               ACT.Copy).then_inc(selT_ready, 1)

                def unit(u, end):
                    for q in (10, 11, 12):
                        hi(G_MOE + q, i * EU + u)
                    product(G_MOE + 8, i * EU + u)
                    unit_silu()
                    if end:
                        xg(i + 2)
                    hi(G_MOE + 13, i * EU + u)
                    hi(G_MOE + 14, i * EU + u)
                    hT(i * EU + u + (FB + 2))
                    hi(G_MOE + 15, i * EU + u)

                with act.Fori(0, EU - 2) as u:
                    unit(u, False)
                if last:
                    pT(2)
                unit(EU - 2, not last)
                for q in ((4,) if last else (4, 5, 6)):
                    hi(G_MOE + ITEM + q, i * EU)

            hi(G_MOE + 6)
            product(G_MOE + 4)
            with act.Fori(0, last_item) as i:
                item(i, False)
            item(last_item, True)
            output(G_MOE + 1, last_item * EU + EU)
            for t in range(T):
                act.wait_ge(acc_done, last_item * T + (2 * T + t + 1))
                square_y(3, t, lambda t: acc[:, t, :].rearrange("p (c n) -> p c n", c=2))
            for t in range(T):
                xT(t, 6, None, True)
            act.wait_ge(y_tile0, 5)
            for c in range(2):
                gate(0, c, True)
            for c in range(2):
                product(G_MOE + 3 + 2 * c, last_item * EU + EU)
                gate(1, c, True)

        @block.vector
        def _(dve):
            count = [0]

            def step(ins):
                count[0] += 1
                ins.then_inc(dve_step, 1)
                dve.wait_ge(dve_step, count[0])

            def lo(g, turns=0):
                for s in range(2):
                    part = slice(s * HW, (s + 1) * HW)
                    dve.wait_ge(hi_done, turns * 2 * RING + (2 * g + s + 1))
                    dve.tensor_tensor(w_lo[:, g % RING, part], raw_part(g, s), w_hi[:, g % RING, part].bitcast(F32),
                                      ALU.subtract).then_inc(lo_done, 1)

            def los(a, b):
                for g in range(a, b):
                    lo(g)

            def rsqrt(c0, c1):
                v, y, a = (nr[:, k, c0:c1] for k in range(3))
                step(dve.tensor_single_scalar(a.bitcast(I32), v.bitcast(I32), 1, op=ALU.logical_shift_right))
                step(dve.tensor_scalar(y.bitcast(I32), a.bitcast(I32), -1.0, float(0x5F3759DF), ALU.mult, ALU.add))
                for _ in range(3):
                    step(dve.tensor_tensor(a, y, y, ALU.mult))
                    step(dve.scalar_tensor_tensor(out=a, in0=a, scalar=-0.5, in1=v, op0=ALU.mult, op1=ALU.mult))
                    step(dve.scalar_tensor_tensor(out=y, in0=a, scalar=1.5, in1=y, op0=ALU.add, op1=ALU.mult))

            def norm_x(n, t):
                dve.wait_ge(ss_ready, T * n + t + 1)
                step(dve.tensor_scalar(nr[:, 0, t:t + 1], ss[:, 4 + t:5 + t], 1.0 / D, EPS, ALU.mult, ALU.add))
                rsqrt(t, t + 1)
                dve.sem_inc(rstd_ready, 1)

            def weigh_y(k, t, gains, src):
                dve.wait_ge(gain_full, 16 * gains)
                for c in (1, 0):
                    if c == 0:
                        dve.wait_ge(y_squared, 2 * T * k + 2 * t + 1)
                    dve.tensor_tensor(yg[t][:, c, :], src(t)[:, c, :], gain[:, c * N:(c + 1) * N], ALU.mult).then_inc(weighed, 1)
                dve.wait_ge(weighed, 2 * T * k + 2 * t + 2)
                if t == T - 1 and gains < 5:
                    dve.sem_inc(gain_free, 1)

            def stats_y(k, t):
                dve.wait_ge(y_squared, 2 * T * k + 2 * t + 2)
                step(dve.tensor_tensor(nr[:, 2, t:t + 1], ss[:, t:t + 1], ss[:, T + t:T + t + 1], ALU.add))
                step(dve.tensor_scalar(nr[:, 0, t:t + 1], nr[:, 2, t:t + 1], 1.0 / D, EPS, ALU.mult, ALU.add))
                rsqrt(t, t + 1)

            def add_y(t, xr):
                xt = x[:, t, :].rearrange("p (c n) -> p c n", c=2)
                dve.scalar_tensor_tensor(out=xt, in0=yg[t], scalar=nr[:, 1, t:t + 1], in1=xt, op0=ALU.mult,
                                         op1=ALU.add).then_inc(x_ready, 1)
                dve.wait_ge(x_ready, xr + t + 1)

            def xT(t, n, v, final=False):
                for b in range(2):
                    dve.wait_ge(xT_act, 2 * T * n + 2 * t + b + 1)
                    for j in range(HK):
                        kt, src = HK * b + j, PS[:, tile_bank(t, final) + b, j * P:(j + 1) * P]
                        dst, up = xT_lo[:, kt, t * P:(t + 1) * P], xT_hi[:, kt, t * P:(t + 1) * P].bitcast(F32)
                        if v is None:
                            m = dve.tensor_tensor(dst, src, up, ALU.subtract)
                        else:
                            m = dve.scalar_tensor_tensor(out=dst, in0=src, scalar=vcol[:, v + kt:v + kt + 1],
                                                         in1=up, op0=ALU.mult, op1=ALU.subtract)
                m.then_inc(xT_ready, 1)

            in_psum = lambda t: PS[:, 4 + 2 * t:6 + 2 * t, :]

            def norms(k, y_n, g, gains, n, xr, v, turned, between=lambda: None):
                for t in range(T):
                    if t == 0:
                        dve.wait_ge(y_tile0, y_n)
                    else:
                        between()
                        dve.wait_ge(used, 2 * g)
                    weigh_y(k, t, gains, in_psum)
                    stats_y(k, t)
                    add_y(t, xr)
                    norm_x(n, t)
                    xT(t, turned, v)

            dve.memset(cT[:, :, 0:2], 0.0)
            norm_x(0, 0)
            norm_x(0, 1)
            lo(0)
            dve.wait_ge(columns_full, 16)
            xT(0, 0, V_N00)
            los(1, 4)
            xT(1, 0, V_N00)
            l0, l1 = vcol[:, V_LB0:V_LB0 + 8], vcol[:, V_LB1:V_LB1 + 8]
            step(dve.tensor_tensor(lbc[:, 0, :], l0, l1, ALU.max))
            step(dve.tensor_tensor(lbc[:, 2, :], l0, lbc[:, 0, :], ALU.subtract))
            step(dve.tensor_tensor(lbc[:, 3, :], l1, lbc[:, 0, :], ALU.subtract))
            dve.sem_inc(exp_ask, 1)
            dve.wait_ge(s_wr, 1)
            dve.tensor_tensor(wr_lo[:, :, :], wr[:, :, :], wr_hi[:, :, :].bitcast(F32), ALU.subtract).then_inc(s_wr, 1)
            dve.wait_ge(ws_full, 16)
            dve.memset(wsT[64:P, :, 0:64], 0.0).then_inc(s_wsE, 1)
            dve.wait_ge(seg_in, 2)
            ii, ir, cmp = iota_c[:, :].bitcast(I32), rt[:, 0:P].bitcast(I32), rt[:, P:2 * P]
            xr_ = rt[:, 2 * P:3 * P].bitcast(I32)
            step(dve.tensor_tensor(xr_, ii, ir, ALU.bitwise_xor))
            step(dve.tensor_tensor(cmp, ii, ir, ALU.is_gt))
            step(dve.tensor_copy(rt[:, 0:P], xr_))
            step(dve.tensor_tensor(cmp, cmp, rt[:, 0:P], ALU.mult))
            for lv in range(7):
                dve.tensor_scalar(seg[:, lv, :], cmp, float(2 ** lv), None, ALU.is_ge)
            step(dve.tensor_copy(rt[:, 0:P], ii))
            step(dve.tensor_copy(iota_c[:, :], rt[:, 0:P]))
            dve.wait_ge(exp_done, 1)
            step(dve.tensor_tensor(lbc[:, 2, :], lbc[:, 0, :], lbc[:, 1, :], ALU.add))
            step(dve.reciprocal(lbc[:, 3, :], lbc[:, 2, :]))
            step(dve.tensor_tensor(lbc[:, 0, :], lbc[:, 0, :], lbc[:, 3, :], ALU.mult))
            step(dve.tensor_tensor(lbc[:, 1, :], lbc[:, 1, :], lbc[:, 3, :], ALU.mult))
            step(dve.tensor_tensor(lbc[:, 2, :], lbc[:, 0, :], lbc[:, 1, :], ALU.add))
            step(dve.tensor_tensor(lbc[:, 0, :], lbc[:, 2, :], lbc[:, 0, :], ALU.subtract))
            step(dve.tensor_scalar(lbc[:, 1, :], lbc[:, 0, :], -1.0, 1.0, ALU.mult, ALU.add))
            los(4, 8)
            heads = "p t (h d) -> p (t h) d"
            AG = T * AH
            m1, m2 = rt[:, 0:AG], rt[:, AG:2 * AG]
            dve.wait_ge(v_gelu, 1)
            vh, ch, qh = av.rearrange(heads, h=AH), vc.rearrange(heads, h=AH), sq.rearrange(heads, h=AH)
            step(dve.tensor_reduce(m1, vh, AXX, ALU.add))
            step(dve.tensor_scalar(m1, m1, 1.0 / AD, None, ALU.mult))
            step(dve.tensor_tensor(ch, vh, m1.unsqueeze(2).broadcast_to([P, AG, AD]), ALU.subtract))
            lo(8)
            dve.wait_ge(xb_ready, 1)
            dve.wait_ge(used, 2 * (G_AB + 6))
            dve.tensor_tensor(xb, PS[:, 4:6, :], xb, ALU.mult).then_inc(c_ready, 1)
            step(dve.tensor_tensor(qh, ch, ch, ALU.mult))
            step(dve.tensor_reduce(m2, qh, AXX, ALU.add))
            step(dve.tensor_scalar(nr[:, 0, 0:AG], m2, 1.0 / AD, EPS, ALU.mult, ALU.add))
            rsqrt(0, AG)
            lo(9)
            step(dve.tensor_tensor(ch, ch, nr[:, 1, 0:AG].unsqueeze(2).broadcast_to([P, AG, AD]), ALU.mult))
            dve.wait_ge(ln_full, 32)
            step(dve.tensor_tensor(vc, vc, lng.unsqueeze(1).broadcast_to([P, T, AW]), ALU.mult))
            dve.tensor_tensor(vc, vc, lnb.unsqueeze(1).broadcast_to([P, T, AW]), ALU.add).then_inc(vn_ready, 1)
            los(10, 12)
            dve.wait_ge(cT_ready, 1)
            dve.wait_ge(vn_ready, 1)
            for tap in range(3):
                for k in range(HK):
                    w = vcol[:, V_CONV + tap * HK + k:V_CONV + tap * HK + k + 1]
                    src = cT[:, k, tap:tap + SEQ]
                    if tap == 0:
                        m = dve.tensor_scalar(conv[:, k, :], src, w, None, ALU.mult)
                    else:
                        m = dve.scalar_tensor_tensor(out=conv[:, k, :], in0=src, scalar=w, in1=conv[:, k, :],
                                                     op0=ALU.mult, op1=ALU.add)
                step(m)
            dve.wait_ge(bgT_psum, 1)
            step(dve.tensor_tensor(ybT, conv, PS[:, 4:6, :].rearrange("p b (k s) -> p (b k) s", k=2), ALU.mult))
            dve.sem_inc(ybT_ready, 1)
            dve.wait_ge(yb_act, 1)
            dve.tensor_tensor(xT_lo[:, HK:KT, :], ybT, xT_hi[:, HK:KT, :].bitcast(F32), ALU.subtract).then_inc(yb_ready, 1)
            lo(12)
            dve.wait_ge(u_ready, 1)
            dve.wait_ge(gm_done, 1)
            for h in range(AH):
                src = PS[:, 2 + h // 4, (h % 4) * P:(h % 4 + 1) * P].rearrange("p (t d) -> p t d", t=T)
                cols = slice(h * AD, (h + 1) * AD)
                m = dve.scalar_tensor_tensor(out=ya[:, :, cols], in0=src, scalar=vcol[:, V_ABS + h:V_ABS + h + 1],
                                             in1=uu[:, :, cols], op0=ALU.add, op1=ALU.mult)
            m.then_inc(ya_ready, 1)
            lo(13)
            dve.wait_ge(ya_act, 1)
            dve.tensor_tensor(xT_lo[:, 0:HK, :], PS[:, 0:2, :].rearrange("p b (k s) -> p (b k) s", k=2),
                              xT_hi[:, 0:HK, :].bitcast(F32), ALU.subtract).then_inc(yaT_ready, 1)
            los(14, 18)
            norms(0, 1, G_FFN, 1, 1, 0, V_N02, 1)
            los(18, 21)

            def hidden(n):
                dve.wait_ge(silu_done, n)
                dve.tensor_tensor(hh.rearrange("p (t n) -> p t n", t=T), sg.rearrange("p (t n) -> p t n", t=T),
                                  PS[:, 0:2, 256:512], ALU.mult).then_inc(h_ready, 1)

            def hT(n):
                dve.wait_ge(hT_act, n)
                dve.tensor_tensor(hT_lo[:, :], PS[:, 2, :], hT_hi[:, :].bitcast(F32), ALU.subtract).then_inc(hT_ready, 1)

            hidden(1)
            hT(1)
            with dve.Fori(0, (FB - 1) // 2) as it:
                for j in range(2):
                    lo(21 + 3 * j, it)
                    lo(22 + 3 * j, it)
                    hidden(2 * it + (j + 2))
                    lo(23 + 3 * j, it)
                    hT(2 * it + (j + 2))

            def pT(n):
                dve.wait_ge(pT_act, n)
                up, low = pT_split[n - 1]
                dve.tensor_tensor(low, pT_in.rearrange("p (k c) -> p k c", c=P), up.bitcast(F32),
                                  ALU.subtract).then_inc(pT_ready, 1)

            def embed(n, t, xr):
                for c in range(2):
                    g, xc = pgate[:, t, c, :], x[:, t, c * N:(c + 1) * N]
                    dve.wait_ge(gate_act, 2 * T * n + 2 * t + c + 1)
                    step(dve.tensor_tensor(g, g, PS[:, embed_banks[n][2 * c + t], :], ALU.mult))
                    m = dve.tensor_tensor(xc, xc, g, ALU.add)
                m.then_inc(x_ready, 1)
                dve.wait_ge(x_ready, xr + t + 1)

            dve.wait_ge(y_tile0, 2)
            weigh_y(1, 0, 2, in_psum)
            stats_y(1, 0)
            dve.wait_ge(used, 2 * G_PLE0)
            weigh_y(1, 1, 2, in_psum)
            add_y(0, T)
            pT(1)
            stats_y(1, 1)
            add_y(1, T)
            xT(0, 2, None)
            los(51, 52)
            xT(1, 2, None)
            los(52, 54)
            for t in range(T):
                if t:
                    los(54, 56)
                embed(0, t, 2 * T)
                norm_x(2, t)
                xT(t, 3, V_N10)
            los(56, 62)
            for hd in range(HEADS):
                dve.wait_ge(fT_act, hd // 2 + 1)
                m = dve.tensor_scalar(fT[:, hd, :], fT[:, hd, :], lbc[:, 1, hd:hd + 1], lbc[:, 0, hd:hd + 1],
                                      ALU.mult, ALU.add)
            step(m)
            step(dve.tensor_scalar(kT, fT, -1.0, 1.0, ALU.mult, ALU.add))
            los(62, 64)
            dve.wait_ge(qT_act, 4)
            dve.sem_inc(qk_ready, 1)

            def meet(lv):
                at = attn.rearrange("p h t n -> p (h t) n")
                src = PS[:, 4:8, :].rearrange("p b (g n) -> p (b g) n", g=4)
                dve.wait_ge(at_done, lv + 1)
                if lv == 0:
                    step(dve.tensor_tensor(at, src, ident[:, :].unsqueeze(1).broadcast_to([P, 2 * HEADS, P]), ALU.mult))
                else:
                    step(dve.copy_predicated(at, seg[:, lv - 1, :].unsqueeze(1).broadcast_to([P, 2 * HEADS, P]), src))

            flat = "p h s -> p (h s)"
            qf, kf, ff = qT.rearrange(flat), kT.rearrange(flat), fT.rearrange(flat)
            totals = (junk[:, :].bitcast(F32), tot)
            prev = ff
            meet(0)
            step(dve.tensor_tensor(qT, qT, fT, ALU.mult))
            dve.sem_inc(qk_ready, 1)
            lo(64)
            for lv in range(1, 8):
                width, blocks = 2 ** (lv - 1), HEADS * SEQ // 2 ** (lv - 1)
                meet(lv)
                pv = prev.rearrange("p (m e) -> p m e", e=2)
                q4 = qf.rearrange("p (m e w) -> p m e w", e=2, w=width)
                k4 = kf.rearrange("p (m e w) -> p m e w", e=2, w=width)
                shape = [P, blocks // 2, width]
                dve.tensor_tensor(q4[:, :, 1, :], q4[:, :, 1, :], pv[:, :, 0].unsqueeze(2).broadcast_to(shape), ALU.mult)
                step(dve.tensor_tensor(k4[:, :, 0, :], k4[:, :, 0, :], pv[:, :, 1].unsqueeze(2).broadcast_to(shape),
                                       ALU.mult))
                dve.sem_inc(qk_ready, 1)
                lo(64 + lv)
                if lv < 7:
                    prev = totals[lv % 2][:, 0:blocks // 2]
                    step(dve.tensor_tensor(prev, pv[:, :, 0], pv[:, :, 1], ALU.mult))
            dve.wait_ge(at_done, 9)
            step(dve.tensor_copy(attx, PS[:, 4:6, :].rearrange("p b (h n) -> p (b h) n", h=4)))
            dve.sem_inc(qk_ready, 1)
            dve.wait_ge(g_evac, 2)
            dve.wait_ge(gain_full, 48)
            for t in range(T):
                step(dve.tensor_tensor(gg[:, t, :], gg[:, t, :], gain[:, :], ALU.mult))
                if t == T - 1:
                    dve.sem_inc(gain_free, 1)
                dve.wait_ge(o_sq, t + 1)
                heads = slice(t * HEADS, (t + 1) * HEADS)
                ot = oo[:, t, :].rearrange("p (h n) -> p h n", n=HD)
                step(dve.tensor_reduce(rt[:, heads], osq[:, t * D:(t + 1) * D].rearrange("p (g n) -> p g n", n=HD), AXX,
                                       ALU.add))
                step(dve.tensor_scalar(nr[:, 0, heads], rt[:, heads], 1.0 / HD, EPS, ALU.mult, ALU.add))
                rsqrt(t * HEADS, (t + 1) * HEADS)
                step(dve.tensor_tensor(ot, PS[:, 2 * t:2 * t + 2, :].rearrange("p b (h n) -> p (b h) n", n=HD),
                                       nr[:, 1, heads].unsqueeze(2).broadcast_to([P, HEADS, HD]), ALU.mult))
                dve.tensor_tensor(oo[:, t, :], oo[:, t, :], gg[:, t, :], ALU.mult).then_inc(o_ready, 1)
                dve.wait_ge(o_ready, t + 1)
                if t == 0:
                    lo(72)
                xT(t, 4, None)
            lo(73)
            norms(2, 4, G_MOE, 4, 3, 3 * T, V_N12, 5, lambda: los(74, 76))
            chosen, ex, lm, lg = (rt[:, k * T * E:(k + 1) * T * E] for k in range(4))
            mx, rank = rt[:, 64:64 + T], rt[:, 80:80 + T * E]
            later = rt[:, 256:256 + E * E].rearrange("p (a b) -> p a b", a=E)
            pair = rt[:, 128:128 + E * E].rearrange("p (a b) -> p a b", a=E)
            ranks = SC[:, 4 * 1024 + T * P:4 * 1024 + T * P + 2 * T * E * E].rearrange(
                "p (k t a b) -> p k t a b", k=2, t=T, a=E)
            above, same = ranks[:, 0], ranks[:, 1]

            def by_row(v):
                return v.unsqueeze(2).broadcast_to([P, E, E])

            def by_col(v):
                return v.unsqueeze(1).broadcast_to([P, E, E])

            step(dve.tensor_tensor(later, by_col(iota_c[:, 0:E]), by_row(iota_c[:, 0:E]), ALU.is_lt))
            los(76, 78)
            dve.wait_ge(lg_done, 1)
            tE = "p (t e) -> p t e"
            step(dve.tensor_tensor(lg.rearrange(tE, t=T), PS[:, 0, 0:T * E].rearrange(tE, t=T),
                                   br[:, :].unsqueeze(1).broadcast_to([P, T, E]), ALU.add))
            step(dve.tensor_reduce(mx, lg.rearrange(tE, t=T), AXX, ALU.max))
            step(dve.tensor_tensor(lm.rearrange(tE, t=T), lg.rearrange(tE, t=T), mx.unsqueeze(2).broadcast_to([P, T, E]),
                                   ALU.subtract))
            dve.sem_inc(lg_max, 1)
            l_row = lg.rearrange(tE, t=T).unsqueeze(3).broadcast_to([P, T, E, E])
            l_col = lg.rearrange(tE, t=T).unsqueeze(2).broadcast_to([P, T, E, E])
            dve.tensor_tensor(above, l_col, l_row, ALU.is_gt)
            step(dve.tensor_tensor(same, l_col, l_row, ALU.is_equal))
            step(dve.tensor_tensor(same, same, later.unsqueeze(1).broadcast_to([P, T, E, E]), ALU.mult))
            step(dve.tensor_tensor(above, above, same, ALU.add))
            step(dve.tensor_reduce(rank.rearrange(tE, t=T), above, AXX, ALU.add))
            step(dve.tensor_scalar(chosen, rank, 2.0, None, ALU.is_lt))
            dve.sem_inc(sel_cnt, 1)
            gates = rt[:, 320:320 + T * E]
            dve.wait_ge(lg_exp, 1)
            step(dve.tensor_tensor(ex, ex, chosen, ALU.mult))
            step(dve.tensor_reduce(mx, ex.rearrange(tE, t=T), AXX, ALU.add))
            step(dve.reciprocal(mx, mx))
            step(dve.tensor_tensor(gates.rearrange(tE, t=T), ex.rearrange(tE, t=T), mx.unsqueeze(2).broadcast_to([P, T, E]),
                                   ALU.mult))
            slot = rt[:, 96:96 + T * E]
            step(dve.memset(tab[:, 0, :, :], -1.0))
            step(dve.memset(tab[:, 1, :, :], 0.0))
            dve.wait_ge(cnt_done, 1)
            step(dve.scalar_tensor_tensor(out=slot, in0=PS[:, 1, 0:T * E], scalar=1.0, in1=chosen, op0=ALU.add, op1=ALU.mult))
            step(dve.tensor_scalar(slot, slot, -1.0, None, ALU.add))
            step(dve.tensor_copy(tab[:, 0, :, 1:E + 1], slot.rearrange(tE, t=T)))
            dve.tensor_copy(tab[:, 1, :, 1:E + 1], gates.rearrange(tE, t=T))

            def select(col):
                dve.tensor_copy(cur[:, 0, :].unsqueeze(2), tab[:, 0, :, bass.ds(col, 1)]).then_inc(cur_step, 1)

            def compare():
                for t in range(T):
                    m = dve.tensor_scalar(sel[:, t, :], iota_c[:, :], cur[:, 0, t:t + 1], None, ALU.is_equal)
                m.then_inc(sel_ready, 1)

            select(1)
            dve.wait_ge(cur_step, 1)
            compare()
            over, place, one, tmp = (rt[:, 336 + k * E:336 + (k + 1) * E] for k in range(4))
            head = rt[:, 368:368 + 2 + XTRA]
            step(dve.tensor_scalar(over, PS[:, 1, T * E:(T + 1) * E], float(P), None, ALU.is_gt))
            step(dve.tensor_tensor(pair, later, by_col(over), ALU.mult))
            step(dve.tensor_reduce(place, pair, AXX, ALU.add))
            step(dve.tensor_reduce(head[:, 0:1], over, AXX, ALU.add))
            step(dve.tensor_scalar(head[:, 0:1], head[:, 0:1], float(E - 1), None, ALU.add))
            step(dve.memset(head[:, 1:2], float(E - 1)))
            for j in range(XTRA):
                step(dve.scalar_tensor_tensor(out=one, in0=place, scalar=float(j), in1=over, op0=ALU.is_equal, op1=ALU.mult))
                step(dve.tensor_tensor(tmp, one, iota_c[:, 0:E], ALU.mult))
                step(dve.tensor_reduce(head[:, 2 + j:3 + j], tmp, AXX, ALU.add))
                for k, v in ((0, slot), (1, gates)):
                    p3 = pair[:, 0:T, :]
                    step(dve.tensor_tensor(p3, v.rearrange(tE, t=T), one.unsqueeze(1).broadcast_to([P, T, E]), ALU.mult))
                    m = dve.tensor_reduce(tab[:, k, :, E + j + 1:E + j + 2], p3, AXX, ALU.add)
                    step(m)
            step(dve.tensor_scalar(tab[:, 0, :, E + 1:E + 1 + XTRA], tab[:, 0, :, E + 1:E + 1 + XTRA], -float(P), None, ALU.add))
            dve.tensor_copy(itab[0:1, 0:2 + XTRA], head[0:1, :]).then_inc(table_ready, 1)
            dve.wait_ge(table_ready, 1)
            last_item = dve.value_load(itab[0:1, 0:1], min_val=E - 1, max_val=ITEMS - 1)

            def xg(n):
                for b in range(2):
                    dve.wait_ge(xg_act, n * 2 + (b - 1))
                    for j in range(HK):
                        k = HK * b + j
                        m = dve.scalar_tensor_tensor(out=xT_lo[:, k, 0:P], in0=PS[:, 6 + b, j * P:(j + 1) * P],
                                                     scalar=vcol[:, V_N12 + k:V_N12 + k + 1],
                                                     in1=xT_hi[:, k, 0:P].bitcast(F32), op0=ALU.mult, op1=ALU.subtract)
                    m.then_inc(xg_ready, 1)

            def unit_hidden(n):
                dve.wait_ge(silu_done, n)
                dve.tensor_tensor(hh, sg, PS[:, 1, :], ALU.mult).then_inc(h_ready, 1)

            def output(n):
                dve.wait_ge(ye_act, n)
                dve.tensor_tensor(ye_lo, PS[:, 4:6, :].rearrange("p b (k c) -> p (b k) c", k=HK), ye_hi.bitcast(F32),
                                  ALU.subtract).then_inc(ye_ready, 1)

            def add_tile(i, t, base):
                dve.wait_ge(sc_done, i * T + (t + 1))
                b = (4, base)[t]
                dve.scalar_tensor_tensor(out=acc[:, t, :], in0=PS[:, b:b + 2, :].rearrange("p b n -> p (b n)"),
                                         scalar=cur[:, 1, t:t + 1], in1=acc[:, t, :], op0=ALU.mult,
                                         op1=ALU.add).then_inc(acc_done, 1)

            def gates_of(i, steps):
                dve.tensor_copy(cur[:, 1, :].unsqueeze(2), tab[:, 1, :, bass.ds(i, 1)]).then_inc(cur_step, 1)
                dve.wait_ge(cur_step, steps)
                dve.wait_ge(acc_done, i * T + T)

            def add_output(i, steps):
                gates_of(i, steps)
                for t in range(T):
                    add_tile(i, t, 0)

            def item(i, last):
                unit_hidden(i * EU + (FB + 1))
                lo(G_MOE + 7, i * EU)
                output(i + 1)
                hT(i * EU + (FB + 1))
                add_output(i, i * 2 + (2 if last else 3))
                lo(G_MOE + 8, i * EU)
                lo(G_MOE + 9, i * EU)

                def unit(u, end):
                    for q in (10, 11, 12):
                        lo(G_MOE + q, i * EU + u)
                    unit_hidden(i * EU + u + (FB + 2))
                    if end:
                        xg(i + 2)
                    lo(G_MOE + 13, i * EU + u)
                    lo(G_MOE + 14, i * EU + u)
                    hT(i * EU + u + (FB + 2))
                    lo(G_MOE + 15, i * EU + u)

                with dve.Fori(0, EU - 2) as u:
                    unit(u, False)
                if last:
                    pT(2)
                unit(EU - 2, not last)
                for q in ((4,) if last else (4, 5, 6)):
                    lo(G_MOE + ITEM + q, i * EU)

            xg(1)
            lo(G_MOE + 6)
            with dve.Fori(0, last_item) as i:
                dve.wait_ge(tsel_psum, i + 1)
                select(i + 2)
                dve.wait_ge(cur_step, i * 2 + 2)
                compare()
                item(i, False)
            item(last_item, True)
            output(last_item + 2)
            gates_of(last_item + 1, last_item * 2 + 3)
            for t in range(T):
                add_tile(last_item + 1, t, 1)
                dve.wait_ge(acc_done, last_item * T + (2 * T + t + 1))
                weigh_y(3, t, 5, lambda t: acc[:, t, :].rearrange("p (c n) -> p c n", c=2))
                if t == 1:
                    xT(0, 6, None, True)
                stats_y(3, t)
                add_y(t, 4 * T)
            xT(1, 6, None, True)
            for t in range(T):
                embed(1, t, 5 * T)


_INS = ["x", "p", "norm_g", "w_in_ab", "a_ln_g", "a_ln_b", "a_ws", "a_bs", "b_conv", "w_out_ab", "ffn_w_gu",
        "ffn_w_down", "w_in_c", "lb_param", "c_onorm_g", "w_out_c", "w_router", "b_router", "e_w_gu", "e_w_down",
        "ple_w_proj", "ple_w_gate"]
_LAID_OUT = ["x", "pT", "columns", "norm_g", "w_in_ab", "a_ln_g", "a_ln_b", "a_wsT", "w_out_ab", "ffn_w_gu",
             "ffn_w_down", "w_in_c", "c_onorm_g", "w_out_c", "w_router", "b_router", "e_w_gu", "e_w_down",
             "ple_w_proj", "ple_w_gate"]


def granules(w, sides=1, columns=512):
    n, rows, m = w.shape
    w = w.reshape(n, 2, 4, P, sides, m // sides // columns, columns)
    w = w.transpose(0, 5, 1, 3, 2, 4, 6)
    return w.reshape(n, 2 * m // sides // columns, P, 4 * sides * columns)


def expert_granules(w):
    n, rows, m = w.shape
    w = w.reshape(n, 2, 4, P, 2, m // 1024, 512)
    w = w.transpose(0, 5, 4, 1, 3, 2, 6)
    return w.reshape(n, 4 * (m // 1024), P, GW)


def kernel(**inputs):
    import numpy as _np
    import concourse.bacc as _bacc
    from concourse import mybir as _mybir
    from concourse.bass_utils import run_bass_kernel_spmd as _run

    data = {name: _np.asarray(inputs[name]) for name in _INS}
    for name in ("w_in_ab", "w_out_ab", "w_in_c", "w_out_c", "ple_w_gate"):
        data[name] = granules(data[name]).reshape(-1, P, GW)
    data["ffn_w_gu"] = granules(data["ffn_w_gu"], 2, 256).reshape(-1, P, GW)
    data["e_w_gu"] = expert_granules(data["e_w_gu"][0])
    data["columns"] = _np.concatenate([data["norm_g"][:, ::2].reshape(-1, P), data["lb_param"].reshape(-1, P),
                                       data["a_bs"].reshape(-1, P), data["b_conv"].reshape(-1, P)]).T
    data["a_wsT"] = data["a_ws"][0].transpose(2, 0, 1)
    data["pT"] = data["p"][:, 0].reshape(2, -1, P, 2).transpose(0, 2, 3, 1).reshape(2, P, -1)
    data["w_router"] = data["w_router"][0].reshape(-1, P, data["w_router"].shape[2]).transpose(1, 0, 2)

    nc = _bacc.Bacc("TRN2", target_bir_lowering=False, num_devices=1)
    arrays, args = {}, []
    for name in _LAID_OUT:
        a = _np.ascontiguousarray(data[name])
        arrays[f"in_{name}"] = a
        args.append(nc.dram_tensor(f"in_{name}", a.shape, _mybir.dt.from_np(a.dtype), kind="ExternalInput").ap())
    out = nc.dram_tensor("out_0", inputs["x"].shape, _mybir.dt.float32, kind="ExternalOutput").ap()
    trunk(nc, *args, out)
    r = _run(nc, [arrays], core_ids=[0])
    return r.results[0]["out_0"]
```
